# Optimizing a Trainium2 kernel written in Bass

```python
import math
import jax
import jax.numpy as jnp
from jax import lax
import numpy as np

D_MODEL = 1024
BATCH = 1
SEQ = 256
DEPTH = 2
DEC_BATCH = 1
DEC_SEQ = 64
PAST_LEN = 512

CHUNK = 64
N_EVEN = (DEPTH + 1) // 2
N_ODD = DEPTH // 2
EPS = 1e-6

A_HEADS = 8
A_HEAD_DIM = 64
A_W = A_HEADS * A_HEAD_DIM
IDX_HEADS = 4
IDX_DIM = 64
TOPK_MAX = 256
Q_BLOCK = 64
N_BUCKETS = 32
MAX_DISTANCE = 128

B_HEADS = 4
B_KEY_DIM = 64
B_VAL_DIM = 128
B_KW = B_HEADS * B_KEY_DIM
B_VW = B_HEADS * B_VAL_DIM
B_GATE_RANK = 16
B_GATE_TAU = 16.0

C_HEADS = 8
C_HEAD_DIM = 128
C_W = C_HEADS * C_HEAD_DIM
CONV_WIDTH = 4
CONV_CH = 3 * C_W

D_FF = 2816

EVEN_SIZES = (A_W, A_W, A_W, IDX_HEADS * IDX_DIM, IDX_DIM, IDX_HEADS, B_KW, B_KW, B_VW, B_VW, B_GATE_RANK)
EVEN_IN = 3 * A_W + IDX_HEADS * IDX_DIM + IDX_DIM + IDX_HEADS + 2 * B_KW + 2 * B_VW + B_GATE_RANK
ODD_SIZES = (CONV_CH, C_W, C_HEADS, C_HEADS)
ODD_IN = CONV_CH + C_W + 2 * C_HEADS

kernel_name = 'streaming_dsa_gla_gdn_macaron_step'

def _rmsnorm(x, g):
    xf = x.astype(jnp.float32)
    y = xf * lax.rsqrt(jnp.mean(xf * xf, axis=-1, keepdims=True) + EPS)
    return (y * g.astype(jnp.float32)).astype(x.dtype)

def _l2norm(x):
    xf = x.astype(jnp.float32)
    return xf * lax.rsqrt(jnp.sum(xf * xf, axis=-1, keepdims=True) + EPS)

def _swiglu(h, wg, wu, wd):
    return (jax.nn.silu(h @ wg) * (h @ wu)) @ wd

def _split(x, sizes):
    parts, start = [], 0
    for s in sizes:
        parts.append(x[..., start:start + s])
        start += s
    return parts

def _t5_bucket(rel):
    half = N_BUCKETS // 2
    max_exact = half // 2
    n = jnp.abs(rel)
    nf = jnp.maximum(n, 1).astype(jnp.float32)
    large = max_exact + (jnp.log(nf / max_exact) / math.log(MAX_DISTANCE / max_exact) * (half - max_exact)).astype(jnp.int32)
    large = jnp.minimum(large, half - 1)
    return jnp.where(rel > 0, half, 0) + jnp.where(n < max_exact, n, large)

def _dsa_attention(q, k, v, q_idx, w_idx, k_idx, q_pos, k_pos, rel_bias, topk, qblock):
    bsz, lq, nh, hd = q.shape
    nblk = lq // qblock
    k_chunk = k_pos // CHUNK
    gather = jax.vmap(lambda arr, idx: arr[idx])

    def blk(args):
        qb, qib, wb, pb = args
        s = jax.nn.relu(jnp.einsum('bqhd,bkd->bqhk', qib, k_idx))
        score = jnp.einsum('bqh,bqhk->bqk', wb, s).astype(jnp.float32)
        adm = k_chunk[None, :] <= (pb // CHUNK)[:, None]
        score = jnp.where(adm[None], score, -jnp.inf)
        _, sel = lax.top_k(score, topk)
        k_sel = gather(k, sel)
        v_sel = gather(v, sel)
        sel_pos = k_pos[sel]
        logits = jnp.einsum('bqhd,bqkhd->bhqk', qb, k_sel).astype(jnp.float32) * (hd ** -0.5)
        bias = rel_bias[_t5_bucket(sel_pos - pb[None, :, None])].astype(jnp.float32)
        logits = logits + jnp.transpose(bias, (0, 3, 1, 2))
        ok = (sel_pos // CHUNK) <= (pb // CHUNK)[None, :, None]
        logits = jnp.where(ok[:, None], logits, -jnp.inf)
        p = jax.nn.softmax(logits, axis=-1).astype(v.dtype)
        return jnp.einsum('bhqk,bqkhd->bqhd', p, v_sel)

    def to_blocks(t):
        return jnp.swapaxes(t.reshape((bsz, nblk, qblock) + t.shape[2:]), 0, 1)

    out = lax.map(blk, (to_blocks(q), to_blocks(q_idx), to_blocks(w_idx), q_pos.reshape(nblk, qblock)))
    return jnp.swapaxes(out, 0, 1).reshape(bsz, lq, nh, hd)

def _gla_chunked(q, k, v, g, s0, chunk):
    bsz, L, nh, dk = q.shape
    dv = v.shape[-1]
    n = L // chunk

    def to_chunks(t):
        return jnp.transpose(t.astype(jnp.float32).reshape(bsz, n, chunk, nh, t.shape[-1]), (1, 0, 3, 2, 4))

    causal = jnp.tril(jnp.ones((chunk, chunk), dtype=bool))
    mid = chunk // 2

    def step(S, inp):
        qc, kc, vc, gc = inp
        b = jnp.cumsum(gc, axis=-2)
        b_mid = b[..., mid:mid + 1, :]
        b_last = b[..., -1:, :]
        o_inter = jnp.einsum('bhcd,bhde->bhce', qc * jnp.exp(b), S)
        a = jnp.einsum('bhtd,bhsd->bhts', qc * jnp.exp(b - b_mid), kc * jnp.exp(b_mid - b))
        a = jnp.where(causal, a, 0.0)
        o = o_inter + jnp.einsum('bhts,bhse->bhte', a, vc)
        S_new = jnp.swapaxes(jnp.exp(b_last), -1, -2) * S + jnp.einsum('bhcd,bhce->bhde', kc * jnp.exp(b_last - b), vc)
        return S_new, o

    S, o = lax.scan(step, s0.astype(jnp.float32), (to_chunks(q), to_chunks(k), to_chunks(v), to_chunks(g)))
    o = jnp.transpose(o, (1, 0, 3, 2, 4)).reshape(bsz, L, nh, dv)
    return o, S.astype(s0.dtype)

def _gated_delta_chunked(q, k, v, g, beta, s0, chunk):
    bsz, L, nh, dk = q.shape
    dv = v.shape[-1]
    n = L // chunk

    def to_chunks(t):
        t = t.astype(jnp.float32).reshape((bsz, n, chunk, nh) + t.shape[3:])
        return jnp.moveaxis(t, (1, 3), (0, 2))

    incl = jnp.tril(jnp.ones((chunk, chunk), dtype=bool))
    strict = jnp.tril(jnp.ones((chunk, chunk), dtype=bool), k=-1)
    eye = jnp.eye(chunk, dtype=jnp.float32)

    def step(S, inp):
        qc, kc, vc, gc, bc = inp
        gcum = jnp.cumsum(gc, axis=-1)
        decay = jnp.exp(jnp.where(incl, gcum[..., :, None] - gcum[..., None, :], -jnp.inf))
        kb = kc * bc[..., None]
        lower = jnp.where(strict, jnp.einsum('bhtd,bhsd->bhts', kb, kc) * decay, 0.0)
        rhs = jnp.concatenate([vc * bc[..., None], kb * jnp.exp(gcum)[..., None]], axis=-1)
        sol = lax.linalg.triangular_solve(eye + lower, rhs, left_side=True, lower=True, unit_diagonal=True)
        u, w = sol[..., :dv], sol[..., dv:]
        v_new = u - jnp.einsum('bhcd,bhde->bhce', w, S)
        attn = jnp.where(incl, jnp.einsum('bhtd,bhsd->bhts', qc, kc) * decay, 0.0)
        o = jnp.einsum('bhcd,bhde->bhce', qc * jnp.exp(gcum)[..., None], S) + jnp.einsum('bhts,bhse->bhte', attn, v_new)
        g_last = gcum[..., -1:]
        S_new = jnp.exp(g_last)[..., None] * S + jnp.einsum('bhcd,bhce->bhde', kc * jnp.exp(g_last - gcum)[..., None], v_new)
        return S_new, o

    S, o = lax.scan(step, s0.astype(jnp.float32), (to_chunks(q), to_chunks(k), to_chunks(v), to_chunks(g), to_chunks(beta)))
    o = jnp.moveaxis(o, (0, 2), (1, 3)).reshape(bsz, L, nh, dv)
    return o, S.astype(s0.dtype)

def _mix_even(h, past_k, past_v, past_ki, s0, w_in, q_norm, k_norm, rel_bias, gate_w2, gate_b2, gla_norm, w_out):
    bsz, L, _ = h.shape
    q, k, v, qi, ki, wi, qb, kb, vb, rb, ab = _split(h @ w_in, EVEN_SIZES)
    q = _rmsnorm(q.reshape(bsz, L, A_HEADS, A_HEAD_DIM), q_norm)
    k = _rmsnorm(k.reshape(bsz, L, A_HEADS, A_HEAD_DIM), k_norm)
    v = v.reshape(bsz, L, A_HEADS, A_HEAD_DIM)
    qi = qi.reshape(bsz, L, IDX_HEADS, IDX_DIM)
    if past_k is None:
        past_len = 0
        k_all, v_all, ki_all = k, v, ki
    else:
        past_len = past_k.shape[1]
        k_all = jnp.concatenate([past_k.astype(k.dtype), k], axis=1)
        v_all = jnp.concatenate([past_v.astype(v.dtype), v], axis=1)
        ki_all = jnp.concatenate([past_ki.astype(ki.dtype), ki], axis=1)
    n_keys = past_len + L
    q_pos = past_len + jnp.arange(L, dtype=jnp.int32)
    k_pos = jnp.arange(n_keys, dtype=jnp.int32)
    o_a = _dsa_attention(q, k_all, v_all, qi, wi, ki_all, q_pos, k_pos, rel_bias,
                         min(TOPK_MAX, n_keys // 4), min(Q_BLOCK, L))
    log_alpha = jax.nn.log_sigmoid((ab @ gate_w2 + gate_b2).astype(jnp.float32)) / B_GATE_TAU
    o_b, s_new = _gla_chunked(qb.reshape(bsz, L, B_HEADS, B_KEY_DIM) * (B_KEY_DIM ** -0.5),
                              kb.reshape(bsz, L, B_HEADS, B_KEY_DIM),
                              vb.reshape(bsz, L, B_HEADS, B_VAL_DIM),
                              log_alpha.reshape(bsz, L, B_HEADS, B_KEY_DIM), s0, min(CHUNK, L))
    o_b = _rmsnorm(o_b.astype(h.dtype), gla_norm).reshape(bsz, L, B_VW) * jax.nn.silu(rb)
    out = jnp.concatenate([o_a.reshape(bsz, L, A_W), o_b], axis=-1) @ w_out
    return out, k, v, ki, s_new

def _mix_odd(h, conv_prev, s0, w_in, conv_w, a_log, dt_bias, norm_g, w_out):
    bsz, L, _ = h.shape
    qkv, z, a, b = _split(h @ w_in, ODD_SIZES)
    xpad = jnp.concatenate([conv_prev.astype(qkv.dtype), qkv], axis=1)
    conv = xpad[:, 0:L] * conv_w[0]
    for j in range(1, CONV_WIDTH):
        conv = conv + xpad[:, j:j + L] * conv_w[j]
    q, k, v = _split(jax.nn.silu(conv), (C_W, C_W, C_W))
    q = _l2norm(q.reshape(bsz, L, C_HEADS, C_HEAD_DIM)) * (C_HEAD_DIM ** -0.5)
    k = _l2norm(k.reshape(bsz, L, C_HEADS, C_HEAD_DIM))
    v = v.reshape(bsz, L, C_HEADS, C_HEAD_DIM)
    beta = jax.nn.sigmoid(b.astype(jnp.float32))
    g = -jnp.exp(a_log.astype(jnp.float32)) * jax.nn.softplus(a.astype(jnp.float32) + dt_bias.astype(jnp.float32))
    o, s_new = _gated_delta_chunked(q, k, v, g, beta, s0, min(CHUNK, L))
    o = _rmsnorm(o.astype(h.dtype), norm_g) * jax.nn.silu(z.reshape(bsz, L, C_HEADS, C_HEAD_DIM))
    out = o.reshape(bsz, L, C_W) @ w_out
    return out, xpad[:, -(CONV_WIDTH - 1):], s_new

def _trunk(x, past, prm):
    bsz = x.shape[0]
    ks, vs, kis, glas, deltas, convs = [], [], [], [], [], []
    for i in range(DEPTH):
        h = _rmsnorm(x, prm['ffn_norm'][i, 0])
        x = x + 0.5 * _swiglu(h, prm['ffn_w_gate'][i, 0], prm['ffn_w_up'][i, 0], prm['ffn_w_down'][i, 0])
        h = _rmsnorm(x, prm['mix_norm'][i])
        j = i // 2
        if i % 2 == 0:
            if past is None:
                pk = pv = pki = None
                s0 = jnp.zeros((bsz, B_HEADS, B_KEY_DIM, B_VAL_DIM), x.dtype)
            else:
                pk, pv, pki, s0 = past['k'][j], past['v'][j], past['ki'][j], past['gla'][j]
            mixed, k_new, v_new, ki_new, s_new = _mix_even(
                h, pk, pv, pki, s0, prm['ev_w_in'][j], prm['ev_q_norm'][j], prm['ev_k_norm'][j],
                prm['rel_bias'], prm['ev_gate_w2'][j], prm['ev_gate_b2'][j], prm['ev_gla_norm'][j], prm['ev_w_out'][j])
            ks.append(k_new)
            vs.append(v_new)
            kis.append(ki_new)
            glas.append(s_new)
        else:
            if past is None:
                cprev = jnp.zeros((bsz, CONV_WIDTH - 1, CONV_CH), x.dtype)
                s0 = jnp.zeros((bsz, C_HEADS, C_HEAD_DIM, C_HEAD_DIM), x.dtype)
            else:
                cprev, s0 = past['conv'][j], past['delta'][j]
            mixed, c_new, s_new = _mix_odd(
                h, cprev, s0, prm['od_w_in'][j], prm['od_conv_w'][j], prm['od_a_log'][j],
                prm['od_dt_bias'][j], prm['od_norm'][j], prm['od_w_out'][j])
            convs.append(c_new)
            deltas.append(s_new)
        x = x + mixed
        h = _rmsnorm(x, prm['ffn_norm'][i, 1])
        x = x + 0.5 * _swiglu(h, prm['ffn_w_gate'][i, 1], prm['ffn_w_up'][i, 1], prm['ffn_w_down'][i, 1])
    return x, jnp.stack(ks), jnp.stack(vs), jnp.stack(kis), jnp.stack(glas), jnp.stack(deltas), jnp.stack(convs)

def setup_inputs(seed: int = 0) -> dict:
    key = jax.random.key(seed)
    keys = iter(jax.random.split(key, 40))

    def nrm(shape, scale):
        return scale * jax.random.normal(next(keys), shape, jnp.float32)

    d = {}
    d['x_prompt'] = nrm((BATCH, SEQ, D_MODEL), 1.0)
    d['x_sample'] = nrm((DEC_BATCH, DEC_SEQ, D_MODEL), 1.0)
    d['cache_attn_k'] = nrm((N_EVEN, DEC_BATCH, PAST_LEN, A_HEADS, A_HEAD_DIM), 1.0)
    d['cache_attn_v'] = nrm((N_EVEN, DEC_BATCH, PAST_LEN, A_HEADS, A_HEAD_DIM), 1.0)
    d['cache_idx_k'] = nrm((N_EVEN, DEC_BATCH, PAST_LEN, IDX_DIM), 1.0)
    d['state_gla'] = nrm((N_EVEN, DEC_BATCH, B_HEADS, B_KEY_DIM, B_VAL_DIM), 0.1)
    d['state_delta'] = nrm((N_ODD, DEC_BATCH, C_HEADS, C_HEAD_DIM, C_HEAD_DIM), 0.1)
    d['state_conv'] = nrm((N_ODD, DEC_BATCH, CONV_WIDTH - 1, CONV_CH), 1.0)
    d['ffn_norm'] = 1.0 + nrm((DEPTH, 2, D_MODEL), 0.02)
    d['ffn_w_gate'] = nrm((DEPTH, 2, D_MODEL, D_FF), D_MODEL ** -0.5)
    d['ffn_w_up'] = nrm((DEPTH, 2, D_MODEL, D_FF), D_MODEL ** -0.5)
    d['ffn_w_down'] = nrm((DEPTH, 2, D_FF, D_MODEL), D_FF ** -0.5)
    d['mix_norm'] = 1.0 + nrm((DEPTH, D_MODEL), 0.02)
    d['ev_w_in'] = nrm((N_EVEN, D_MODEL, EVEN_IN), D_MODEL ** -0.5)
    d['ev_q_norm'] = 1.0 + nrm((N_EVEN, A_HEAD_DIM), 0.02)
    d['ev_k_norm'] = 1.0 + nrm((N_EVEN, A_HEAD_DIM), 0.02)
    d['rel_bias'] = nrm((N_BUCKETS, A_HEADS), 0.5)
    d['ev_gate_w2'] = nrm((N_EVEN, B_GATE_RANK, B_KW), B_GATE_RANK ** -0.5)
    d['ev_gate_b2'] = nrm((N_EVEN, B_KW), 0.1)
    d['ev_gla_norm'] = 1.0 + nrm((N_EVEN, B_VAL_DIM), 0.02)
    d['ev_w_out'] = nrm((N_EVEN, A_W + B_VW, D_MODEL), (A_W + B_VW) ** -0.5)
    d['od_w_in'] = nrm((N_ODD, D_MODEL, ODD_IN), D_MODEL ** -0.5)
    d['od_conv_w'] = nrm((N_ODD, CONV_WIDTH, CONV_CH), CONV_WIDTH ** -0.5)
    d['od_a_log'] = jnp.log(jax.random.uniform(next(keys), (N_ODD, C_HEADS), jnp.float32, 1.0, 16.0))
    dt = jnp.exp(jax.random.uniform(next(keys), (N_ODD, C_HEADS), jnp.float32, math.log(1e-3), math.log(1e-1)))
    d['od_dt_bias'] = dt + jnp.log(-jnp.expm1(-dt))
    d['od_norm'] = 1.0 + nrm((N_ODD, C_HEAD_DIM), 0.02)
    d['od_w_out'] = nrm((N_ODD, C_W, D_MODEL), C_W ** -0.5)
    return d

def reference(x_prompt, x_sample, cache_attn_k, cache_attn_v, cache_idx_k, state_gla, state_delta, state_conv,
              ffn_norm, ffn_w_gate, ffn_w_up, ffn_w_down, mix_norm, ev_w_in, ev_q_norm, ev_k_norm, rel_bias,
              ev_gate_w2, ev_gate_b2, ev_gla_norm, ev_w_out, od_w_in, od_conv_w, od_a_log, od_dt_bias, od_norm,
              od_w_out):
    prm = {'ffn_norm': ffn_norm, 'ffn_w_gate': ffn_w_gate, 'ffn_w_up': ffn_w_up, 'ffn_w_down': ffn_w_down,
           'mix_norm': mix_norm, 'ev_w_in': ev_w_in, 'ev_q_norm': ev_q_norm, 'ev_k_norm': ev_k_norm,
           'rel_bias': rel_bias, 'ev_gate_w2': ev_gate_w2, 'ev_gate_b2': ev_gate_b2, 'ev_gla_norm': ev_gla_norm,
           'ev_w_out': ev_w_out, 'od_w_in': od_w_in, 'od_conv_w': od_conv_w, 'od_a_log': od_a_log,
           'od_dt_bias': od_dt_bias, 'od_norm': od_norm, 'od_w_out': od_w_out}
    past = {'k': cache_attn_k, 'v': cache_attn_v, 'ki': cache_idx_k, 'gla': state_gla,
            'delta': state_delta, 'conv': state_conv}
    y_prompt, p_attn_k, p_attn_v, p_idx_k, p_gla, p_delta, p_conv = _trunk(x_prompt, None, prm)
    y_sample, s_attn_k, s_attn_v, s_idx_k, s_gla, s_delta, s_conv = _trunk(x_sample, past, prm)
    return (y_prompt, y_sample, p_attn_k, p_attn_v, p_idx_k, p_gla, p_delta, p_conv,
            s_attn_k, s_attn_v, s_idx_k, s_gla, s_delta, s_conv)


_drawn_inputs = setup_inputs


def setup_inputs(seed=0):
    import zlib

    import numpy as np

    out = dict(_drawn_inputs(seed))
    spreads = {}
    factors = {'state_gla': 3.247,
     'ev_q_norm': 8.0,
     'ev_k_norm': 3.008,
     'ev_gla_norm': 4.534,
     'od_norm': 6.215}
    for name, (base, spread) in spreads.items():
        noise = np.random.default_rng([zlib.crc32(name.encode()), seed]).standard_normal(out[name].shape)
        drawn = base * np.exp(spread * noise) if base else spread * noise
        out[name] = jnp.asarray(drawn.astype(out[name].dtype))
    for name, factor in factors.items():
        out[name] = (out[name] * factor).astype(out[name].dtype)
    return out
```

```python
from contextlib import ExitStack

import concourse.bass as bass
from concourse import mybir

ALU = mybir.AluOpType
ACT = mybir.ActivationFunctionType
F32 = mybir.dt.float32
AX = mybir.AxisListType.X

P = 128
D = 1024
KT = D // P
TP, TS = 256, 64
T = TP + TS
RB_N = 29300
CH = 64
NCH = T // CH
PAST = 512
FF = 2816
FT = FF // P
EPS = 1e-6
BIG = 1e30
TAKEN = -3.0e38
PADDED = -2.0e38
A_H, A_D, A_PAIRS = 8, 64, 4
IDX_H, IDX_D, IDX_PAIRS = 4, 64, 2
TOP_P = min(256, TP // 4)
NK_S = PAST + TS
TOP_S = min(256, NK_S // 4)
B_PAIRS, B_K, B_V, B_RANK, B_TAU = 2, 64, 128, 16, 16.0
C_H, C_D, C_PAIRS = 8, 128, 4
N_BUCKETS, MAX_DIST = 32, 128
REL0 = NK_S - 1
REL_N = 640

EV = {}
_at = 0
for _name, _size in (("q", 512), ("k", 512), ("v", 512), ("qi", 256), ("ki", 64), ("wi", 4),
                     ("qb", 256), ("kb", 256), ("vb", 512), ("rb", 512), ("ab", 16)):
    EV[_name] = _at
    _at += _size
EV_LOADS = [[(EV["qi"], 128), (EV["qi"] + 128, 128)], [(EV["ki"], 68), (EV["ab"], 16)]]
for _name, _tiles in (("q", 4), ("k", 4), ("qb", 2), ("kb", 2), ("vb", 4), ("v", 4), ("rb", 4)):
    for _t in range(0, _tiles, 2):
        EV_LOADS.append([(EV[_name] + 128 * _t, 128), (EV[_name] + 128 * _t + 128, 128)])
T_QI, T_KI, T_AB, T_Q, T_K, T_QB, T_KB, T_VB, T_V, T_RB = 0, 2, 3, 4, 8, 12, 14, 16, 20, 24
N_EV = 2 * len(EV_LOADS)

OD_TILES = list(range(8, 16)) + list(range(0, 8)) + list(range(16, 32))
N_OD = len(OD_TILES)

GU_FFN = [0, 22 + 14, 22 + 14 + 22, 22 + 14 + 22 + 22 + 16]
GU_EV = 22
GU_OD = 80
DN_FFN = [0, 12, 20, 32]
DN_EV, DN_OD = 8, 28
N_GU = 118
N_DN = 40


def bucket_runs():
    def bucket(rel):
        n, half = abs(rel), N_BUCKETS // 2
        exact = half // 2
        if n >= exact:
            j = max(j for j in range(half - exact + 1) if n ** exact >= exact ** exact * (MAX_DIST // exact) ** j)
            n = min(half - 1, exact + j)
        return n + (half if rel > 0 else 0)
    runs = []
    for rel in range(-REL0, REL_N - REL0):
        b = bucket(rel)
        if runs and runs[-1][0] == b:
            runs[-1][2] = rel
        else:
            runs.append([b, rel, rel])
    return runs


def build(nc, I, O):
    with ExitStack() as ctx:
        def sb(name, shape):
            return ctx.enter_context(nc.sbuf_tensor(name, shape, F32))

        def sem(name):
            return ctx.enter_context(nc.semaphore(name))

        PS = ctx.enter_context(nc.psum_tensor("PS", [P, 8 * 512], F32))
        xT = sb("xT", [P, KT, T])
        hT = sb("hT", [P, KT, T])
        gu = sb("gu", [P, 2, 2048])
        dn = sb("dn", [P, 2, FT * 128])
        RA = sb("RA", [P, 7040])
        RB = sb("RB", [P, RB_N])
        ident = sb("ident", [P, P])
        ones = sb("ones", [P, P])
        cols = sb("cols", [P, 226])
        rs = sb("rs", [P, 1280])
        oT = hT[:, :, :]

        def bank(b, n=512, at=0):
            return PS[:, b * 512 + at:b * 512 + at + n]

        def banks(b, m, n):
            return PS[:, b * 512:(b + m) * 512].rearrange("p (a c) -> p a c", a=m)[:, :, 0:n]

        def view(t, at, *dims):
            n = 1
            for d in dims:
                n *= d
            flat = t[:, at:at + n]
            if len(dims) == 1:
                return flat
            names = "abcd"[:len(dims)]
            return flat.rearrange(f"p ({' '.join(names)}) -> p {' '.join(names)}",
                                  **{n_: d for n_, d in zip(names, dims)})

        act = view(RA, 0, FT, T)
        squares = view(RA, 0, KT, T)
        xnat = view(RA, 0, 3, D)
        qbd = view(RA, 0, NCH, A_PAIRS, P)
        qibd = view(RA, 2560, NCH, IDX_PAIRS, P)
        pT = view(RA, 3840, 5, 512)
        workX = view(RA, 3840, 256)
        workY = view(RA, 3840 + 256, 576)
        sqE = view(RA, 3840 + 1280, 4, T)
        gx = view(RA, 3840, 2, T)
        gx2 = view(RA, 3840 + 640, 2, T)
        e_mid_n = view(RA, 3840 + 1280, 2, T)
        e_b = view(RA, 3840 + 1920, 2, T)
        dwi = view(RA, 6400, 10, CH)
        n = 0
        pr = view(RB, n, N_EV, T); n += N_EV * T
        vcache = view(RB, n, 4, 512); n += 2048
        kcT = view(RB, n, A_PAIRS, 512); n += 2048
        ipn = view(RB, n, 4, 64); n += 256
        kiT = view(RB, n, TP + NK_S); n += TP + NK_S
        biasT = view(RB, n, A_PAIRS, NK_S); n += A_PAIRS * NK_S
        Sg = view(RB, n, 7, B_PAIRS, P); n += 7 * B_PAIRS * P
        pen1 = view(RB, n, 128); n += 128
        pen2 = view(RB, n, 192); n += 192
        pen3 = view(RB, n, 256); n += 256
        penS = view(RB, n, NK_S); n += NK_S
        l_at = n
        n += A_PAIRS * NK_S
        vtok = view(RB, n, 3, 512); n += 1536
        ktok = view(RB, 0, 3, 512)
        bd_at = n
        qe_bd = view(RB, n, B_PAIRS, NCH, P); n += 1280
        km_bd = view(RB, n, B_PAIRS, NCH, P); n += 1280
        kl_bd = view(RB, n, B_PAIRS, NCH, P); n += 1280
        qm = view(RB, n, B_PAIRS, T); n += 640
        kwtok = view(RB, n, 3, 68); n += 204
        wcol = view(RB, n, NCH, IDX_PAIRS); n += 10
        mx = view(RB, n, NCH, 3, 4); n += 60
        es = view(RB, n, B_PAIRS, NCH); n += 10
        rbT = view(RB, n, 32); n += 32
        w2 = view(RB, n, 256); n += 256
        top8 = view(RB, n, 8); n += 8
        halves = view(RB, n, P); n += P
        causal = view(RB, n, CH); n += CH
        istk = view(RB, n, CH); n += CH
        assert n <= RB_N, n
        kcn = view(RB, bd_at, 4, 512)
        biasrow = view(RB, l_at, REL_N)
        rX3 = view(RB, l_at, 2, 256)
        rX2 = view(RB, l_at + 512, 2, 192)
        rYS = view(RB, l_at + 896, 2, NK_S)
        rY1 = view(RB, l_at + 2048, 2, 128)
        gB = view(RB, l_at, B_PAIRS, T)
        gdm = view(RB, l_at + 640, B_PAIRS, T)
        gdl = view(RB, l_at + 1280, B_PAIRS, T)
        vp = pr[:, T_V:T_V + 4, :].rearrange("p a b -> p (a b)").rearrange("p (u e) -> p u e", e=P)
        n = 0
        cv = view(RB, n, 3, C_PAIRS, NCH, P); n += 24 * T
        qp = view(RB, n, 4, 326); n += 4 * 326
        zT = view(RB, n, 8, T); n += 8 * T
        Sd = view(RB, n, 2, C_H, P); n += 2048
        cst = view(RB, n, 24, 6); n += 144
        uT = view(RB, n, NCH, C_PAIRS, P); n += 2560
        At = view(RB, n, NCH, C_PAIRS, P); n += 2560
        Kl = view(RB, n, NCH, C_PAIRS, P); n += 2560
        lm_at = n
        Lm = view(RB, n, NCH, C_PAIRS, P); n += 2560
        Vb = Lm
        csr = view(RB, n, 24 * P)
        Dm = view(RB, n, NCH, C_PAIRS, P); n += 2560
        lev = view(RB, n, 6, P); n += 768
        maskI = view(RB, n, P); n += P
        maskS = view(RB, n, P); n += P
        wab = view(RB, n, 8, 16); n += 128
        rows8 = view(RB, n, 4, T); n += 4 * T
        gl = view(RB, n, C_H, NCH); n += C_H * NCH
        es8 = view(RB, n, C_H, NCH); n += C_H * NCH
        colG = view(RB, n, 2, NCH, C_PAIRS); n += 40
        egc = view(RB, n, NCH, C_PAIRS); n += 20
        ncol = view(RB, n, NCH, C_PAIRS); n += 20
        bhalf = view(RB, n, NCH, C_PAIRS); n += 20
        klc = view(RB, n, NCH, C_PAIRS); n += 20
        assert n <= RB_N, n
        tT = view(RA, 0, NCH, C_PAIRS, P)
        yT = view(RA, 2560, NCH, C_PAIRS, P)
        vnew = view(RA, 5120, C_PAIRS, 2, P)
        Rr = view(RA, 6144, C_PAIRS, P)
        sqO = view(RA, 0, 8, T)
        orr = view(RA, 2560, 8, T)
        zth = view(RB, lm_at, 8, T)
        cring = view(RA, 0, 4, 323)
        sq4 = view(RA, 2560, 4 * T)
        th2 = view(RA, 3840, 2, 323)
        vbx = pr[:, T_VB:T_VB + 4, :].rearrange("p a b -> p (a b)").rearrange("p (a c e) -> p a c e", a=2, e=P)
        ytok = view(RA, 0, 3, D)
        tanh_g = view(rs, 0, 2, T)
        gated = view(rs, 640, 2, T)

        def group(g):
            return cv[:, 1 - g // 2, 2 * (g % 2):2 * (g % 2) + 2, :, :].rearrange("p a c e -> p (a c e)")

        def growv(i):
            return rows8[:, i, :]

        def logit(b):
            return view(RB, l_at + (1024 if b in (1, 3) else 0), A_PAIRS, CH * (b + 1) if b < 4 else NK_S)

        def pt_slot(b):
            return (0, 2, 0, 2, 0)[b]

        C_FFN, C_MIX, C_GLA, C_OD, C_B2, C_QN, C_KN = 0, 32, 48, 49, 50, 52, 53
        C_CONV, C_ST = 54, 150

        gu_loaded = [sem("gu_loaded0"), sem("gu_loaded1")]
        dn_loaded = [sem("dn_loaded0"), sem("dn_loaded1")]
        gu_half, gu_done = sem("gu_half"), sem("gu_done")
        dn_half, dn_done = sem("dn_half"), sem("dn_done")
        x_upd = sem("x_upd")
        tanh_done, act_mid, act_done = sem("tanh_done"), sem("act_mid"), sem("act_done")
        sq_done, norm_sum, norm_recip, norm_rstd, h_ready = (sem(s) for s in (
            "sq_done", "norm_sum", "norm_recip", "norm_rstd", "h_ready"))
        consts = sem("consts")
        params_in, x_in, caches_in, small_in, out_sem = (sem(s) for s in (
            "params_in", "x_in", "caches_in", "small_in", "out_sem"))
        pool_step, dve_step, act_step = sem("pool_step"), sem("dve_step"), sem("act_step")
        pro_pe, pro_evac = sem("pro_pe"), sem("pro_evac")

        scratch = nc.dram_tensor("bias_rows", (A_H, CH, REL_N), F32, kind="Internal").ap()

        def gu_source(n):
            slot = gu[:, n % 2, :]
            for f in range(4):
                if GU_FFN[f] <= n < GU_FFN[f] + FT:
                    g = n - GU_FFN[f]
                    return [(slot[:, j * 1024:(j + 1) * 1024].rearrange("p (k c) -> p k c", k=KT),
                             ffn_w(I[name], f)[:, :, g * P:(g + 1) * P])
                            for j, name in enumerate(("ffn_w_gate", "ffn_w_up"))]
            if GU_EV <= n < GU_EV + len(EV_LOADS):
                tiles = EV_LOADS[n - GU_EV]
                w = I["ev_w_in"][0].rearrange("(k p) c -> p k c", p=P)
                if tiles[1][0] == tiles[0][0] + P:
                    dst = slot.rearrange("p (k c) -> p k c", k=KT)
                    src = w[:, :, tiles[0][0]:tiles[0][0] + 256]
                    return [(dst[:, 4 * j:4 * j + 4, :], src[:, 4 * j:4 * j + 4, :]) for j in range(2)]
                return [(slot.rearrange("p (k c) -> p k c", k=KT)[:, :, 128 * j:128 * j + w_],
                         w[:, :, c0:c0 + w_]) for j, (c0, w_) in enumerate(tiles)]
            t = OD_TILES[2 * (n - GU_OD)]
            dst = slot.rearrange("p (k c) -> p k c", k=KT)
            src = I["od_w_in"][0].rearrange("(k p) c -> p k c", p=P)[:, :, t * P:t * P + 256]
            return [(dst[:, 4 * j:4 * j + 4, :], src[:, 4 * j:4 * j + 4, :]) for j in range(2)]

        def ffn_w(w, f):
            return w[f // 2, f % 2].rearrange("(k p) c -> p k c", p=P)

        def dn_source(n):
            for f in range(4):
                if DN_FFN[f] <= n < DN_FFN[f] + KT:
                    m = n - DN_FFN[f]
                    return (dn[:, n % 2, :].rearrange("p (k c) -> p k c", k=FT),
                            ffn_w(I["ffn_w_down"], f)[:, :, m * P:(m + 1) * P])
            w, m = (I["ev_w_out"], n - DN_EV) if n < DN_EV + 4 else (I["od_w_out"], n - DN_OD)
            return (dn[:, n % 2, 0:2048].rearrange("p (k c) -> p k c", k=KT),
                    w[0].rearrange("(k p) c -> p k c", p=P)[:, :, m * 256:(m + 1) * 256])

        X_FFN = [0, 16, 24, 40]
        X_EV, X_OD = 8, 32
        NORM_FFN = [0, 2, 3, 5]
        NORM_EV, NORM_OD = 1, 4

        names = ("ev_evac kct_pe kct_evac kw_pe kw_evac idx_prep rawX rawX_used combX combX_used rawY rawY_used combY "
                 "combY_used dwi_ready qsq ksq qsum ksum qk_recip qk_rstd q_ready k_ready gate_pe gate_used g_neg "
                 "g_ln g_args g_exps bds_ready zero_q zero_bd ktr ktok_evac vtr vtok_evac ga_pe abd_ready vp_pe vp_evac "
                 "kl_pe kl_evac su_pe sg_ready go_pe go_evac gsq gsum grecip grstd sil_t ob_ready qk_pe l_done nmx "
                 "exps_done p_ready pt_pe pt_evac pv_pe pv_evac bias_out bias_in zero_qi")
        s = {k: sem("ev_" + k) for k in names.split()}
        names = ("evac ab_in ab_pe conv th silu zero_v masks g1 g2 g_rows col_pe cols_ready row_pe "
                 "row_used dexp sq sum recip rstd kq_ready kk_pe kk_used kt_evac vt_pe "
                 "vt_evac t1 u1_pe u1_evac bm y_pe y_evac t_pe u_pe t_upd u_upd cs_pe cs_evac rg_pe eg qe ks_pe r_ready "
                 "vn_pe vn_evac o_pe o_evac s_pe s_upd osq osum orecip orstd zt og states ds_in gexp")
        o = {k: sem("od_" + k) for k in names.split()}

        block = ctx.enter_context(nc.Block())

        @block.sync
        def _(sp):
            def load_gu(n):
                if n >= 2:
                    sp.wait_ge(gu_done, n - 1)
                for dst, src in gu_source(n):
                    sp.dma_start(dst, src).then_inc(gu_loaded[n % 2], 16)

            def load_dn(n):
                if n >= 2:
                    sp.wait_ge(dn_done, n - 1)
                dst, src = dn_source(n)
                sp.dma_start(dst, src).then_inc(dn_loaded[n % 2], 16)

            def ffn(f, following):
                base, wg, wu = GU_FFN[f], ffn_w(I["ffn_w_gate"], f), ffn_w(I["ffn_w_up"], f)
                with sp.Fori(1, FT // 2) as i:
                    for slot in range(2):
                        sp.wait_ge(gu_done, base - 1 + slot + 2 * i)
                        for j, w in enumerate((wg, wu)):
                            dst = gu[:, slot, j * 1024:(j + 1) * 1024].rearrange("p (k c) -> p k c", k=KT)
                            sp.dma_start(dst, w[:, :, bass.ds(256 * i + P * slot, P)]).then_inc(gu_loaded[slot], 16)
                load_dn(DN_FFN[f])
                load_dn(DN_FFN[f] + 1)
                if following is not None:
                    load_gu(following)
                    load_gu(following + 1)
                wd = ffn_w(I["ffn_w_down"], f)
                with sp.Fori(1, KT // 2) as i:
                    for slot in range(2):
                        sp.wait_ge(dn_done, DN_FFN[f] - 1 + slot + 2 * i)
                        sp.dma_start(dn[:, slot, :].rearrange("p (k c) -> p k c", k=FT),
                                     wd[:, :, bass.ds(256 * i + P * slot, P)]).then_inc(dn_loaded[slot], 16)

            sp.dma_start(xnat[:, 0:2, :], I["x_prompt"][0].rearrange("(i p) d -> p i d", p=P)).then_inc(x_in, 16)
            sp.dma_start(xnat[0:TS, 2, :], I["x_sample"][0]).then_inc(x_in, 16)
            load_gu(0)
            load_gu(1)
            sp.dma_start(kcn, I["cache_attn_k"][0, 0].rearrange("(t p) h d -> p t (h d)", p=P)).then_inc(caches_in, 16)
            sp.dma_start(vcache, I["cache_attn_v"][0, 0].rearrange("(t p) h d -> p t (h d)", p=P)).then_inc(caches_in, 16)
            sp.dma_start(ipn, I["cache_idx_k"][0, 0].rearrange("(t p) d -> p t d", p=P)).then_inc(caches_in, 16)
            sp.dma_start(Sg[:, 5, :, :],
                         I["state_gla"][0, 0].rearrange("(a b) d e -> a (b d) e", b=2).rearrange("a q e -> q a e")).then_inc(caches_in, 16)
            sp.dma_start(w2[0:B_RANK, :], I["ev_gate_w2"][0]).then_inc(caches_in, 16)
            ffn(0, GU_EV)
            for l in range(2, len(EV_LOADS)):
                load_gu(GU_EV + l)
            load_dn(DN_EV)
            load_dn(DN_EV + 1)
            load_gu(GU_FFN[1])
            load_gu(GU_FFN[1] + 1)
            load_dn(DN_EV + 2)
            load_dn(DN_EV + 3)
            ffn(1, GU_FFN[2])
            sp.wait_ge(x_upd, X_FFN[1] + 2)
            sp.wait_ge(out_sem, 16 * 8)
            sp.dma_start(wab, I["od_w_in"][0].rearrange("(k p) c -> p k c", p=P)[:, :, 4 * D:4 * D + 16])\
              .then_inc(o["ab_in"], 16)
            sp.dma_start(Sd[:, 1, :, :], I["state_delta"][0, 0].rearrange("h d e -> d h e")).then_inc(o["ds_in"], 16)
            ffn(2, GU_OD)
            for l in range(2, 16):
                load_gu(GU_OD + l)
            load_dn(DN_OD)
            load_dn(DN_OD + 1)
            load_gu(GU_FFN[3])
            load_gu(GU_FFN[3] + 1)
            load_dn(DN_OD + 2)
            load_dn(DN_OD + 3)
            ffn(3, None)

        @block.tensor
        def _(pe):
            mm, tr = pe.matmul, pe.transpose

            def prologue():
                pe.wait_ge(consts, 1)
                pe.wait_ge(x_in, 32)
                for i in range(3):
                    rows = P if i < 2 else TS
                    for half in range(2):
                        for k in range(4):
                            ins = tr(bank(2 * i + half)[:, k * P:k * P + rows],
                                     xnat[0:rows, i, (4 * half + k) * P:(4 * half + k + 1) * P], ident[0:rows, 0:rows])
                        ins.then_inc(pro_pe, 1)
                pe.wait_ge(params_in, 16 * 11)
                tr(bank(6)[:, 0:54], rs[0:54, 0:P], ident[0:54, 0:54])
                tr(bank(6)[:, 54:150], rs[0:96, P:2 * P], ident[0:96, 0:96])
                tr(bank(6)[:, 150:222], rs[0:72, 2 * P:3 * P], ident[0:72, 0:72]).then_inc(pro_pe, 1)

            def norm(r):
                for k in range(KT):
                    if k % 2 == 0:
                        pe.wait_ge(sq_done, 4 * r + k // 2 + 1)
                    if r == 0 and k == 0:
                        pe.wait_ge(pro_evac, 7)
                    ins = mm(bank(6, T), ones[:, :], squares[:, k, :], start=(k == 0), stop=(k == KT - 1))
                ins.then_inc(norm_sum, 1)

            def ffn(f):
                base = GU_FFN[f]
                pe.wait_ge(h_ready, KT * (NORM_FFN[f] + 1))
                if f:
                    pe.wait_ge(x_upd, X_FFN[f] + 2)
                with pe.Fori(0, FT // 2) as i:
                    for slot in range(2):
                        pe.wait_ge(gu_loaded[slot], 32 * (base // 2) + 32 + 32 * i)
                        pe.wait_ge(act_done, FT * f + 1 + slot + 2 * i)
                        for j, done in ((0, gu_half), (1, gu_done)):
                            for k in range(KT):
                                ins = mm(bank(2 * slot + j, T), gu[:, slot, j * 1024 + k * P:j * 1024 + (k + 1) * P],
                                         hT[:, k, :], start=(k == 0), stop=(k == KT - 1))
                            ins.then_inc(done, 1)
                pe.wait_ge(act_done, 2 + FT * (f + 1))
                with pe.Fori(0, KT // 2) as i:
                    for slot in range(2):
                        pe.wait_ge(dn_loaded[slot], 16 * (DN_FFN[f] // 2) + 16 + 16 * i)
                        pe.wait_ge(x_upd, X_FFN[f] + 1 + slot + 2 * i)
                        for k in range(FT):
                            ins = mm(bank(4 + slot, T), dn[:, slot, k * P:(k + 1) * P], act[:, k, :],
                                     start=(k == 0), stop=(k == FT - 1))
                        ins.then_inc(dn_done, 1)

            def project_out(base_dn, base_x):
                for m in range(KT):
                    n = base_dn + m // 2
                    if m % 2 == 0:
                        pe.wait_ge(dn_loaded[n % 2], 16 * (n // 2 + 1))
                    pe.wait_ge(x_upd, base_x + 1 + m)
                    for k in range(KT):
                        ins = mm(bank(4 + m % 2, T), dn[:, n % 2, k * 256 + (m % 2) * P:k * 256 + (m % 2) * P + P],
                                 oT[:, k, :], start=(k == 0), stop=(k == KT - 1))
                    ins.then_inc((dn_half, dn_done)[m % 2], 1)

            def project_in(n, t, widths, evac):
                pe.wait_ge(gu_loaded[n % 2], 32 * (n // 2 + 1))
                for j in range(2):
                    if t + j >= 4:
                        pe.wait_ge(evac, t + j - 3)
                    for k in range(KT):
                        ins = mm(bank((t + j) % 4, T)[0:widths[j], :],
                                 gu[:, n % 2, k * 256 + j * P:k * 256 + j * P + widths[j]], hT[:, k, :],
                                 start=(k == 0), stop=(k == KT - 1))
                    ins.then_inc((gu_half, gu_done)[j], 1)

            def even():
                pe.wait_ge(x_upd, X_EV + 2)
                pe.wait_ge(caches_in, 16 * 5)
                for p in range(A_PAIRS):
                    for kt in range(4):
                        ins = tr(bank(p)[:, kt * P:(kt + 1) * P], kcn[:, kt, p * P:(p + 1) * P], ident[:, :])
                    ins.then_inc(s["kct_pe"], 1)
                for kt in range(4):
                    ins = tr(bank(7)[0:IDX_D, kt * P:(kt + 1) * P], ipn[:, kt, :], ident[:, :])
                ins.then_inc(s["kct_pe"], 1)
                norm(NORM_EV)
                pe.wait_ge(h_ready, KT * (NORM_EV + 1))
                pe.wait_ge(s["kct_evac"], 5)
                for l, tiles in enumerate(EV_LOADS):
                    project_in(GU_EV + l, 2 * l, [w for _, w in tiles], s["ev_evac"])
                    if l == 2:
                        key_token_rows()
                    if l == 4:
                        raw_scores_x()
                    if l == 5:
                        combine_x()
                    if l == 6:
                        raw_scores_y()
                    if l == 7:
                        combine_y()
                    if l == 8:
                        head_sums(s["qsq"], s["combY_used"], 1, s["qsum"])
                    if l == 9:
                        head_sums(s["ksq"], s["qk_recip"], 1, s["ksum"])
                    if l == 10:
                        gate()
                token_rows()
                gla()
                attention()
                pe.wait_ge(s["ob_ready"], 4)
                pe.wait_ge(s["pv_evac"], 5)
                project_out(DN_EV, X_EV)

            def key_token_rows():
                pe.wait_ge(s["ev_evac"], T_KI + 1)
                for i in range(3):
                    rows = P if i < 2 else TS
                    ins = tr(bank(7)[0:rows, i * 68:(i + 1) * 68], pr[0:68, T_KI, i * P:i * P + rows], ident[0:68, 0:68])
                ins.then_inc(s["kw_pe"], 1)

            def raw_scores_x():
                pe.wait_ge(s["idx_prep"], 1)
                for b, bk in ((3, 4), (2, 5)):
                    for p in range(IDX_PAIRS):
                        ins = mm(bank(bk)[:, p * 256:p * 256 + CH * (b + 1)], qibd[:, b, p, :], kiT[:, 0:CH * (b + 1)],
                                 start=True, stop=True)
                ins.then_inc(s["rawX"], 1)

            def weigh(b, out, rrow, done=None):
                for p in range(IDX_PAIRS):
                    ins = mm(out, dwi[:, 2 * b + p, :], rrow(p), start=(p == 0), stop=(p == 1))
                if done is not None:
                    ins.then_inc(done, 1)

            def combine_x():
                pe.wait_ge(s["rawX_used"], 1)
                pe.wait_ge(s["dwi_ready"], 1)
                weigh(3, bank(7)[CH:P, 0:256], lambda p: rX3[:, p, :])
                weigh(2, bank(7)[0:CH, 0:192], lambda p: rX2[:, p, :], s["combX"])

            def raw_scores_y():
                for p in range(IDX_PAIRS):
                    mm(bank(4)[:, p * 128:(p + 1) * 128], qibd[:, 1, p, :], kiT[:, 0:128], start=True, stop=True)
                    mm(bank(5 + p), qibd[:, 4, p, :], kiT[:, TP:TP + 512], start=True, stop=True)
                    ins = mm(bank(4)[:, 256 + 64 * p:320 + 64 * p], qibd[:, 4, p, :], kiT[:, TP + 512:TP + NK_S],
                             start=True, stop=True)
                ins.then_inc(s["rawY"], 1)

            def combine_y():
                pe.wait_ge(s["rawY_used"], 1)
                pe.wait_ge(s["combX_used"], 1)
                weigh(4, bank(7)[CH:P, :], lambda p: rYS[:, p, 0:512])
                weigh(4, bank(4)[CH:P, 0:64], lambda p: rYS[:, p, 512:NK_S])
                weigh(1, bank(4)[0:CH, 128:256], lambda p: rY1[:, p, :], s["combY"])

            def head_sums(squared, free, n_free, done):
                pe.wait_ge(free, n_free)
                for p in range(4):
                    pe.wait_ge(squared, p + 1)
                    ins = mm(bank(4 + p, T), halves[:, :], sqE[:, p, :], start=True, stop=True)
                ins.then_inc(done, 1)

            def gate():
                pe.wait_ge(s["qk_recip"], 2)
                for j in range(2):
                    ins = mm(bank(4 + j, T), w2[0:B_RANK, j * P:(j + 1) * P], pr[0:B_RANK, T_AB, :], start=True, stop=True)
                ins.then_inc(s["gate_pe"], 1)

            def token_rows():
                pe.wait_ge(s["ev_evac"], N_EV)
                pe.wait_ge(s["k_ready"], 4)
                pe.wait_ge(s["gate_used"], 1)
                for name, first, src, done in (("v", 0, T_V, s["vtr"]), ("k", 4, T_K, s["ktr"])):
                    for i in range(3):
                        rows = P if i < 2 else TS
                        for p in range(4):
                            ins = tr(bank(first + i)[0:rows, p * P:(p + 1) * P], pr[:, src + p, i * P:i * P + rows],
                                     ident[:, :])
                        ins.then_inc(done, 1)

            def gla():
                pe.wait_ge(s["q_ready"], 8)
                pe.wait_ge(s["vtok_evac"], 3)
                for u in range(10):
                    p, c = divmod(u, NCH)
                    ins = tr(PS[:, u * P:(u + 1) * P], vbx[:, p, c, :],
                             ident[:, :])
                ins.then_inc(s["vp_pe"], 1)
                pe.wait_ge(s["bds_ready"], 1)
                pe.wait_ge(s["ktok_evac"], 3)
                for u in range(10):
                    ins = tr(PS[:, 1536 + u * P:1536 + (u + 1) * P], kl_bd[:, u // NCH, u % NCH, :], ident[:, :])
                ins.then_inc(s["kl_pe"], 1)
                for u in range(10):
                    p, c = divmod(u, NCH)
                    ins = mm(PS[:, 3072 + u * CH:3072 + (u + 1) * CH], km_bd[:, p, c, :], qm[:, p, c * CH:(c + 1) * CH],
                             start=True, stop=True)
                ins.then_inc(s["ga_pe"], 1)
                pe.wait_ge(s["vp_evac"], 1)
                pe.wait_ge(s["kl_evac"], 1)
                for u in range(10):
                    ins = mm(PS[:, u * P:(u + 1) * P], kl_bd[:, u // NCH, u % NCH, :], vp[:, u, :], start=True, stop=True)
                ins.then_inc(s["su_pe"], 1)
                pe.wait_ge(s["abd_ready"], 1)
                pe.wait_ge(s["sg_ready"], 1)
                for u in range(10):
                    p, c = divmod(u, NCH)
                    mm(PS[:, 1536 + u * P:1536 + (u + 1) * P], vp[:, u, :], km_bd[:, p, c, :], start=True, stop=False)
                    ins = mm(PS[:, 1536 + u * P:1536 + (u + 1) * P], Sg[:, c if c < 4 else 5, p, :], qe_bd[:, p, c, :],
                             start=False, stop=True)
                ins.then_inc(s["go_pe"], 1)
                pe.wait_ge(s["gsq"], 1)
                for h in range(4):
                    ins = mm(bank(h, T), ones[:, :], sqE[:, h, :], start=True, stop=True)
                ins.then_inc(s["gsum"], 1)

            def attention():
                QK0 = [0, 2, 0, 2, 0]
                PTB = [[4], [5], [4, 5], [4, 5], [5, 6, 7, 0, 1]]
                PVB = [6, 7, 6, 7, 2]

                def scores(b):
                    if b == 0:
                        pe.wait_ge(s["grecip"], 1)
                        pe.wait_ge(s["go_evac"], 2)
                    if b >= 2 and b < 4:
                        pe.wait_ge(s["l_done"], b - 1)
                    if b == 4:
                        pe.wait_ge(s["l_done"], 4)
                        pe.wait_ge(s["pt_evac"], 4)
                    for p in range(A_PAIRS):
                        if b < 4:
                            nk = CH * (b + 1)
                            ins = mm(PS[:, QK0[b] * 512 + p * 256:QK0[b] * 512 + p * 256 + nk], qbd[:, b, p, :],
                                     pr[:, T_K + p, 0:nk], start=True, stop=True)
                        else:
                            mm(bank(p), qbd[:, b, p, :], kcT[:, p, :], start=True, stop=True)
                            ins = mm(bank(4)[:, p * 64:(p + 1) * 64], qbd[:, b, p, :], pr[:, T_K + p, TP:T],
                                     start=True, stop=True)
                    ins.then_inc(s["qk_pe"], 1)

                def turn(b):
                    pe.wait_ge(s["p_ready"], b + 1)
                    if b in (2, 3):
                        pe.wait_ge(s["pt_evac"], b)
                    if b == 4:
                        pe.wait_ge(s["pv_evac"], 4)
                    nk = CH * (b + 1) if b < 4 else NK_S
                    for kt, bk in enumerate(PTB[b]):
                        w = min(P, nk - kt * P)
                        for p in range(A_PAIRS):
                            ins = tr(bank(bk)[0:w, p * P:(p + 1) * P], logit(b)[:, p, kt * P:kt * P + w], ident[:, :])
                    ins.then_inc(s["pt_pe"], 1)

                def values(b):
                    pe.wait_ge(s["pt_evac"], b + 1)
                    if b in (2, 3):
                        pe.wait_ge(s["pv_evac"], b - 1)
                    nk = CH * (b + 1) if b < 4 else NK_S
                    kts = range((nk + P - 1) // P)
                    for p in range(A_PAIRS):
                        for kt in kts:
                            w = min(P, nk - kt * P)
                            if b < 4:
                                v = vtok[0:w, kt, p * P:(p + 1) * P]
                            else:
                                v = vcache[:, kt, p * P:(p + 1) * P] if kt < 4 else vtok[0:w, 2, p * P:(p + 1) * P]
                            ins = mm(bank(PVB[b])[:, p * P:(p + 1) * P], v, pT[0:w, pt_slot(b) + kt, p * P:(p + 1) * P],
                                     start=(kt == 0), stop=(kt == kts[-1]))
                    ins.then_inc(s["pv_pe"], 1)

                scores(0)
                scores(1)
                turn(0)
                scores(2)
                values(0)
                turn(1)
                scores(3)
                values(1)
                turn(2)
                values(2)
                turn(3)
                values(3)
                scores(4)
                turn(4)
                values(4)

            def odd():
                pe.wait_ge(h_ready, KT * (NORM_OD + 1))
                pe.wait_ge(o["ab_in"], 16)
                for j in range(2):
                    for k in range(KT):
                        ins = mm(bank(4 + j, T)[0:C_H, :], wab[:, k, 8 * j:8 * j + 8], hT[:, k, :],
                                 start=(k == 0), stop=(k == KT - 1))
                ins.then_inc(o["ab_pe"], 1)
                for l in range(16):
                    project_in(GU_OD + l, 2 * l, [P, P], o["evac"])
                    if l == 1:
                        gate_columns()
                    if l == 2:
                        gate_rows(0)
                    if l == 3:
                        gate_rows(1)
                    if l in (5, 6, 8, 9):
                        key_sums((5, 6, 8, 9).index(l))
                    if l == 12:
                        key_products()
                    if l == 14:
                        first_inverse()
                for level in range(5):
                    double_inverse(level)
                state_rows()
                recurrence()
                out_sums()
                pe.wait_ge(o["og"], 1)
                project_out(DN_OD, X_OD)

            def gate_columns():
                pe.wait_ge(o["g_rows"], 1)
                for w in range(2):
                    for c in range(NCH):
                        at = (w * NCH + c) * 8
                        ins = tr(bank(6)[0:CH, at:at + 8], growv(2 + w)[0:C_H, c * CH:(c + 1) * CH], ident[0:C_H, 0:C_H])
                ins.then_inc(o["col_pe"], 1)

            def gate_rows(half):
                if half == 0:
                    pe.wait_ge(o["cols_ready"], 1)
                else:
                    pe.wait_ge(o["row_used"], 1)
                for h in range(4):
                    ins = mm(bank(4 + h, T), ident[0:C_H, 4 * half + h:4 * half + h + 1].to_broadcast([C_H, P]),
                             growv(2)[0:C_H, :], start=True, stop=True)
                ins.then_inc(o["row_pe"], 1)

            def key_sums(g):
                if g == 0:
                    pe.wait_ge(o["row_used"], 2)
                else:
                    pe.wait_ge(o["recip"], g)
                pe.wait_ge(o["sq"], g + 1)
                for h in range(4):
                    ins = mm(bank(4 + h, T), ones[:, :], sq4[:, h * T:(h + 1) * T], start=True, stop=True)
                ins.then_inc(o["sum"], 1)

            def kview(p, c):
                return cv[:, 1, p, c, :]

            def qview(p, c):
                return cv[:, 0, p, c, :]

            def key_products():
                pe.wait_ge(o["kq_ready"], 4)
                for c in range(NCH):
                    if c:
                        pe.wait_ge(o["kk_used"], 2 * c)
                        pe.wait_ge(o["kt_evac"], c)
                    for p in range(C_PAIRS):
                        mm(bank(4)[:, p * P:(p + 1) * P], kview(p, c), kview(p, c), start=True, stop=True)
                        mm(bank(5)[:, p * P:(p + 1) * P], kview(p, c), qview(p, c), start=True, stop=True)
                        ins = tr(bank(6)[:, p * P:(p + 1) * P], kview(p, c), ident[:, :])
                    ins.then_inc(o["kk_pe"], 1)

            def first_inverse():
                for c in range(NCH):
                    pe.wait_ge(o["t1"], c + 1)
                    if c == 0:
                        pe.wait_ge(o["kt_evac"], NCH)
                    else:
                        pe.wait_ge(o["u1_evac"], c)
                    for p in range(C_PAIRS):
                        ins = tr(bank(7)[:, p * P:(p + 1) * P], tT[:, c, p, :], ident[:, :])
                    ins.then_inc(o["u1_pe"], 1)

            def double_inverse(level):
                def y(c):
                    m = level * NCH + c
                    pe.wait_ge(o["bm"], m + 1)
                    if m >= 2:
                        pe.wait_ge(o["y_evac"], m - 1)
                    if level:
                        pe.wait_ge(o["u_upd"], m - NCH + 1)
                    for p in range(C_PAIRS):
                        ins = mm(bank(4 + m % 2)[:, p * P:(p + 1) * P], Dm[:, c, p, :], uT[:, c, p, :], start=True, stop=True)
                    ins.then_inc(o["y_pe"], 1)

                def tu(c):
                    m = level * NCH + c
                    pe.wait_ge(o["y_evac"], m + 1)
                    if level:
                        pe.wait_ge(o["t_upd"], m - NCH + 1)
                    if level < 4:
                        if m:
                            pe.wait_ge(o["t_upd"], m)
                        for p in range(C_PAIRS):
                            ins = mm(bank(6)[:, p * P:(p + 1) * P], yT[:, c, p, :], tT[:, c, p, :], start=True, stop=True)
                        ins.then_inc(o["t_pe"], 1)
                    if m:
                        pe.wait_ge(o["u_upd"], m)
                    for p in range(C_PAIRS):
                        ins = mm(bank(7)[:, p * P:(p + 1) * P], tT[:, c, p, :], yT[:, c, p, :], start=True, stop=True)
                    ins.then_inc(o["u_pe"], 1)

                if level == 0:
                    pe.wait_ge(o["u1_evac"], NCH)
                y(0)
                y(1)
                for c in range(NCH):
                    tu(c)
                    if c + 2 < NCH:
                        y(c + 2)

            def state_rows():
                pe.wait_ge(o["evac"], N_OD)
                pe.wait_ge(o["silu"], 24)
                for c in range(NCH):
                    if c >= 2:
                        pe.wait_ge(o["vt_evac"], c - 1)
                    for p in range(C_PAIRS):
                        ins = tr(bank(c % 2)[:, p * P:(p + 1) * P],
                                 cv[:, 2, p, c, :], ident[:, :])
                    ins.then_inc(o["vt_pe"], 1)
                pe.wait_ge(o["vt_evac"], NCH)
                pe.wait_ge(o["u_upd"], 5 * NCH)
                for t in range(24):
                    ins = tr(PS[0:6, t * P:(t + 1) * P], cst[:, t, :], ident[:, :])
                ins.then_inc(o["cs_pe"], 1)
                pe.wait_ge(o["cs_evac"], 1)
                for h in range(C_H):
                    ins = mm(bank(h, T), ident[0:C_H, h:h + 1].to_broadcast([C_H, P]), growv(2)[0:C_H, :],
                             start=True, stop=True)
                ins.then_inc(o["rg_pe"], 1)

            def recurrence():
                pe.wait_ge(o["qe"], C_PAIRS)
                pe.wait_ge(o["zero_v"], 1)
                pe.wait_ge(o["states"], 1)
                pe.wait_ge(o["ds_in"], 16)
                for n_, c in enumerate((0, 4, 1, 2, 3)):
                    S = Sd[:, 1 if c == 4 else 0, :, :]
                    if n_:
                        pe.wait_ge(o["r_ready"], n_)
                    if n_ > 1:
                        pe.wait_ge(o["s_upd"], n_ if n_ > 2 else 1)
                    for p in range(C_PAIRS):
                        for par in range(2):
                            ins = mm(bank(0)[par * CH:(par + 1) * CH, p * P:(p + 1) * P],
                                     cv[:, 1, p, c, par * CH:(par + 1) * CH], S[:, 2 * p + par, :],
                                     start=True, stop=True)
                    ins.then_inc(o["ks_pe"], 1)
                    pe.wait_ge(o["r_ready"], n_ + 1)
                    if n_:
                        pe.wait_ge(o["vn_evac"], n_)
                    for p in range(C_PAIRS):
                        ins = mm(bank(1)[:, p * P:(p + 1) * P], uT[:, c, p, :], Rr[:, p, :], start=True, stop=True)
                    ins.then_inc(o["vn_pe"], 1)
                    pe.wait_ge(o["vn_evac"], n_ + 1)
                    if n_:
                        pe.wait_ge(o["o_evac"], n_)
                    for p in range(C_PAIRS):
                        for par in range(2):
                            out = bank(2)[:, p * P + par * CH:p * P + (par + 1) * CH]
                            mm(out, S[:, 2 * p + par, :], cv[:, 0, p, c, par * CH:(par + 1) * CH],
                               start=True, stop=False)
                            ins = mm(out, vnew[:, p, par, :], At[:, c, p, par * CH:(par + 1) * CH],
                                     start=False, stop=True)
                    ins.then_inc(o["o_pe"], 1)
                    if n_:
                        pe.wait_ge(o["s_upd"], n_)
                    for p in range(C_PAIRS):
                        ins = mm(bank(3 + p // 2)[:, (p % 2) * 256:(p % 2) * 256 + 256], Kl[:, c, p, :],
                                 vnew[:, p, :, :], start=True, stop=True)
                    ins.then_inc(o["s_pe"], 1)

            def out_sums():
                pe.wait_ge(o["osq"], 1)
                pe.wait_ge(o["s_upd"], NCH)
                pe.wait_ge(o["o_evac"], NCH)
                for h in range(C_H):
                    ins = mm(bank(h, T), ones[:, :], sqO[:, h, :], start=True, stop=True)
                ins.then_inc(o["osum"], 1)

            def epilogue():
                pe.wait_ge(x_upd, X_FFN[3] + 2 + KT)
                for i in range(3):
                    rows = P if i < 2 else TS
                    for half in range(2):
                        for k in range(4):
                            ins = tr(bank(2 * i + half)[0:rows, k * P:(k + 1) * P],
                                     xT[:, 4 * half + k, i * P:i * P + rows], ident[:, :])
                        ins.then_inc(pro_pe, 1)

            prologue()
            norm(NORM_FFN[0])
            ffn(0)
            even()
            norm(NORM_FFN[1])
            ffn(1)
            norm(NORM_FFN[2])
            ffn(2)
            norm(NORM_OD)
            odd()
            norm(NORM_FFN[3])
            ffn(3)
            epilogue()

        @block.scalar
        def _(sc):
            act_ = sc.activation
            steps = [0]

            def link(ins):
                steps[0] += 1
                ins.then_inc(act_step, 1)
                sc.wait_ge(act_step, steps[0])

            def copy(out, in_, scale=1.0):
                return act_(out, in_, ACT.Copy, scale=scale)

            def prologue():
                rows = [(0, 32, 0, I["ffn_norm"].rearrange("a b (k p) -> (a b k) p", p=P)),
                        (32, 48, 0, I["mix_norm"].rearrange("a (k p) -> (a k) p", p=P)),
                        (48, 49, 0, I["ev_gla_norm"]), (49, 50, 0, I["od_norm"]),
                        (50, 52, 0, I["ev_gate_b2"].rearrange("a (k p) -> (a k) p", p=P)),
                        (0, 96, P, I["od_conv_w"][0].rearrange("j (k p) -> (j k) p", p=P)),
                        (0, 72, 2 * P, I["state_conv"][0, 0].rearrange("j (k p) -> (j k) p", p=P))]
                for r0, r1, at, src in rows:
                    sc.dma_start(rs[r0:r1, at:at + P], src).then_inc(params_in, 16)
                for row, name in ((C_QN, "ev_q_norm"), (C_KN, "ev_k_norm")):
                    for par in range(2):
                        sc.dma_start(rs[row:row + 1, par * A_D:(par + 1) * A_D], I[name]).then_inc(params_in, 16)
                sc.dma_start(rbT[0:A_H, :], I["rel_bias"].rearrange("b h -> h b"),
                             allow_slow_non_contiguous=True).then_inc(small_in, 16)
                sc.dma_start(cols[0:C_H, 222:223], I["od_a_log"].rearrange("a h -> h a")).then_inc(small_in, 16)
                sc.dma_start(cols[0:C_H, 223:224], I["od_dt_bias"].rearrange("a h -> h a")).then_inc(small_in, 16)
                for i in range(3):
                    n_ = P if i < 2 else TS
                    for half in range(2):
                        sc.wait_ge(pro_pe, 2 * i + half + 1)
                        copy(xT[:, 4 * half:4 * half + 4, i * P:i * P + n_],
                             bank(2 * i + half).rearrange("p (k c) -> p k c", k=4)[:, :, 0:n_]).then_inc(pro_evac, 1)
                sc.wait_ge(pro_pe, 7)
                copy(cols[:, 0:222], bank(6, 222)).then_inc(pro_evac, 1)

            def norm(r, x_base):
                if r == 0:
                    sc.wait_ge(pro_evac, 7)
                sc.wait_ge(x_upd, x_base + 2)
                for j in range(4):
                    act_(squares[:, 2 * j:2 * j + 2, :], xT[:, 2 * j:2 * j + 2, :], ACT.Square).then_inc(sq_done, 1)
                sc.wait_ge(norm_recip, r + 1)
                act_(rs[:, 0:T], rs[:, 0:T], ACT.Sqrt).then_inc(norm_rstd, 1)

            def ffn(f):
                base = GU_FFN[f]
                with sc.Fori(0, FT // 2) as i:
                    for slot in range(2):
                        sc.wait_ge(gu_half, base + 1 + slot + 2 * i)
                        act_(tanh_g[:, slot, :], bank(2 * slot, T), ACT.Tanh, scale=0.5).then_inc(tanh_done, 1)

            def even():
                for p in range(A_PAIRS):
                    sc.wait_ge(s["kct_pe"], p + 1)
                    copy(kcT[:, p, :], bank(p)).then_inc(s["kct_evac"], 1)
                sc.wait_ge(s["kct_pe"], 5)
                copy(kiT[0:IDX_D, TP:TP + PAST], bank(7)[0:IDX_D, :])
                copy(kiT[IDX_D:P, TP:TP + PAST], bank(7)[0:IDX_D, :]).then_inc(s["kct_evac"], 1)
                norm(NORM_EV, X_EV)
                for l, tiles in enumerate(EV_LOADS):
                    for j, done in ((0, gu_half), (1, gu_done)):
                        t, w = 2 * l + j, tiles[j][1]
                        sc.wait_ge(done, GU_EV + l + 1)
                        if T_VB <= t < T_VB + 4:
                            dst = vbx[:, (t - T_VB) // 2, :, (t % 2) * CH:(t % 2 + 1) * CH]
                            copy(dst, bank(t % 4, T).rearrange("p (c t) -> p c t", t=CH)).then_inc(s["ev_evac"], 1)
                        else:
                            copy(pr[0:w, t, :], bank(t % 4, T)[0:w, :]).then_inc(s["ev_evac"], 1)
                    if l == 4:
                        sc.wait_ge(s["rawX"], 1)
                        act_(rX3, bank(4).rearrange("p (a c) -> p a c", a=2), ACT.Relu)
                        act_(rX2, bank(5).rearrange("p (a c) -> p a c", a=2)[:, :, 0:192], ACT.Relu)\
                            .then_inc(s["rawX_used"], 1)
                    if l == 5:
                        for p in range(4):
                            sc.wait_ge(s["ev_evac"], T_Q + p + 1)
                            act_(sqE[:, p, :], pr[:, T_Q + p, :], ACT.Square).then_inc(s["qsq"], 1)
                    if l == 6:
                        sc.wait_ge(s["rawY"], 1)
                        for p in range(IDX_PAIRS):
                            act_(rYS[:, p, 0:512], bank(5 + p), ACT.Relu)
                            act_(rYS[:, p, 512:NK_S], bank(4)[:, 256 + 64 * p:320 + 64 * p], ACT.Relu)
                        act_(rY1, bank(4, 256).rearrange("p (a c) -> p a c", a=2), ACT.Relu).then_inc(s["rawY_used"], 1)
                    if l == 9:
                        sc.wait_ge(s["qsum"], 1)
                        for p in range(4):
                            act_(sqE[:, p, :], pr[:, T_K + p, :], ACT.Square).then_inc(s["ksq"], 1)
                        sc.wait_ge(s["qk_recip"], 1)
                        act_(rs[:, 0:4 * T], rs[:, 0:4 * T], ACT.Sqrt).then_inc(s["qk_rstd"], 1)
                    if l == 11:
                        sc.wait_ge(s["qk_recip"], 2)
                        act_(rs[:, 0:4 * T], rs[:, 0:4 * T], ACT.Sqrt).then_inc(s["qk_rstd"], 1)
                sc.wait_ge(s["g_neg"], 1)
                link(act_(gx2, gx2, ACT.Exp))
                act_(gx2, gx2, ACT.Ln, bias=1.0).then_inc(s["g_ln"], 1)
                for name, dst, first in (("v", vtok, 0), ("k", ktok, 4)):
                    for i in range(3):
                        n_ = P if i < 2 else TS
                        sc.wait_ge(s[name + "tr"], i + 1)
                        copy(dst[0:n_, i, :], bank(first + i)[0:n_, :]).then_inc(s[name + "tok_evac"], 1)
                sc.wait_ge(s["g_args"], 1)
                k_ = 1.0 / B_TAU
                act_(e_b, gB, ACT.Exp, scale=k_)
                act_(es, gB.rearrange("p a (c t) -> p a c t", t=CH)[:, :, :, CH - 1], ACT.Exp, scale=k_)
                act_(e_mid_n, gdm, ACT.Exp, scale=-k_)
                act_(gdm, gdm, ACT.Exp, scale=k_)
                act_(gdl, gdl, ACT.Exp, scale=k_).then_inc(s["g_exps"], 1)
                sc.wait_ge(s["vp_pe"], 1)
                copy(vp, PS[:, 0:1280].rearrange("p (u e) -> p u e", e=P)).then_inc(s["vp_evac"], 1)
                sc.wait_ge(s["kl_pe"], 1)
                copy(kl_bd, PS[:, 1536:2816].rearrange("p (a c e) -> p a c e", a=2, e=P)).then_inc(s["kl_evac"], 1)
                sc.wait_ge(s["go_pe"], 1)
                for p in range(B_PAIRS):
                    copy(oT[:, 4 + 2 * p:6 + 2 * p, :].rearrange("p a (c t) -> p c a t", t=CH),
                         PS[:, 1536 + 640 * p:2176 + 640 * p].rearrange("p (c a t) -> p c a t", a=2, t=CH))\
                        .then_inc(s["go_evac"], 1)
                sc.wait_ge(s["go_evac"], 2)
                act_(sqE, oT[:, 4:8, :], ACT.Square).then_inc(s["gsq"], 1)
                act_(kl_bd.rearrange("p a c e -> p (a c e)"), pr[:, T_RB:T_RB + 4, :].rearrange("p a b -> p (a b)"),
                     ACT.Tanh, scale=0.5).then_inc(s["sil_t"], 1)
                sc.wait_ge(s["grecip"], 1)
                act_(rs[:, 0:4 * T], rs[:, 0:4 * T], ACT.Sqrt).then_inc(s["grstd"], 1)

                def exps(b):
                    sc.wait_ge(s["nmx"], b + 1)
                    for p in range(A_PAIRS):
                        ins = act_(logit(b)[:, p, :], logit(b)[:, p, :], ACT.Exp, bias=mx[:, b, 1, p:p + 1],
                                   accum_out=mx[:, b, 2, p:p + 1])
                    ins.then_inc(s["exps_done"], 1)

                def turned(b):
                    sc.wait_ge(s["pt_pe"], b + 1)
                    if b >= 2:
                        sc.wait_ge(s["pv_pe"], b - 1 if b < 4 else 4)
                    nk = CH * (b + 1) if b < 4 else NK_S
                    for kt, bk in enumerate([[4], [5], [4, 5], [4, 5], [5, 6, 7, 0, 1]][b]):
                        w = min(P, nk - kt * P)
                        ins = copy(pT[0:w, pt_slot(b) + kt, :], bank(bk)[0:w, :])
                    ins.then_inc(s["pt_evac"], 1)

                exps(0)
                exps(1)
                sc.wait_ge(s["ob_ready"], 4)
                turned(0)
                exps(2)
                turned(1)
                exps(3)
                turned(2)
                turned(3)
                exps(4)
                turned(4)

            def odd():
                def tile_out(t):
                    done = (gu_half, gu_done)[t % 2]
                    sc.wait_ge(done, GU_OD + t // 2 + 1)
                    if t < 24:
                        if t >= 4:
                            sc.wait_ge(o["conv"], t - 3)
                        copy(qp[:, t % 4, 3:259], bank(t % 4, TP))
                        copy(qp[:, t % 4, 262:326], bank(t % 4)[:, TP:T]).then_inc(o["evac"], 1)
                    else:
                        copy(zT[:, t - 24, :], bank(t % 4, T)).then_inc(o["evac"], 1)

                def silu_tanh(t):
                    sc.wait_ge(o["conv"], t + 1)
                    if t >= 2:
                        sc.wait_ge(o["silu"], t - 1)
                    act_(th2[:, t % 2, :], cring[:, t % 4, :], ACT.Tanh, scale=0.5).then_inc(o["th"], 1)

                def square(g):
                    sc.wait_ge(o["silu"], 4 * g + 4)
                    if g:
                        sc.wait_ge(o["sum"], g)
                    act_(sq4, group(g), ACT.Square).then_inc(o["sq"], 1)

                def root(g):
                    sc.wait_ge(o["recip"], g + 1)
                    act_(rs[:, 0:4 * T], rs[:, 0:4 * T], ACT.Sqrt).then_inc(o["rstd"], 1)

                sc.wait_ge(small_in, 48)
                act_(cols[0:C_H, 224:225], cols[0:C_H, 222:223], ACT.Exp)
                sc.wait_ge(o["g1"], 1)
                act_(growv(3)[0:C_H, :], growv(3)[0:C_H, :], ACT.Exp)
                link(act_(growv(1)[0:C_H, :], growv(1)[0:C_H, :], ACT.Exp))
                act_(growv(1)[0:C_H, :], growv(1)[0:C_H, :], ACT.Ln, bias=1.0).then_inc(o["g2"], 1)
                for t in range(N_OD):
                    tile_out(t)
                    if t and t <= 24:
                        silu_tanh(t - 1)
                    if t == 3:
                        sc.wait_ge(o["cols_ready"], 1)
                        act_(egc, colG[:, 0, :, :], ACT.Exp).then_inc(o["gexp"], 1)
                    if t == 9:
                        sc.wait_ge(o["row_used"], 2)
                        act_(es8, gl, ACT.Exp)
                        act_(klc, klc, ACT.Exp)
                        act_(Dm, Dm, ACT.Exp, scale=-1.0)
                        act_(At, At, ACT.Exp).then_inc(o["dexp"], 1)
                    if t == 11:
                        square(0)
                    if t == 13:
                        root(0)
                        square(1)
                    if t == 15:
                        root(1)
                    if t == 17:
                        square(2)
                    if t == 19:
                        root(2)
                        square(3)
                    if t == 21:
                        root(3)
                    if t == 25:
                        for c in range(NCH):
                            sc.wait_ge(o["kk_pe"], c + 1)
                            for p in range(C_PAIRS):
                                ins = copy(Kl[:, c, p, :], bank(6)[:, p * P:(p + 1) * P], klc[:, c, p:p + 1])
                            ins.then_inc(o["kt_evac"], 1)
                    if t == 29:
                        for c in range(NCH):
                            sc.wait_ge(o["u1_pe"], c + 1)
                            copy(uT[:, c, :, :], bank(7).rearrange("p (a c) -> p a c", a=4)).then_inc(o["u1_evac"], 1)
                for level in range(5):
                    for c in range(NCH):
                        m = level * NCH + c
                        sc.wait_ge(o["y_pe"], m + 1)
                        if level:
                            sc.wait_ge(o["u_pe"], m - NCH + 1)
                        copy(yT[:, c, :, :], bank(4 + m % 2).rearrange("p (a c) -> p a c", a=4)).then_inc(o["y_evac"], 1)
                sc.wait_ge(o["bm"], 25)
                for c in range(NCH):
                    sc.wait_ge(o["vt_pe"], c + 1)
                    for p in range(C_PAIRS):
                        ins = copy(Vb[:, c, p, :], bank(c % 2)[:, p * P:(p + 1) * P], bhalf[:, c, p:p + 1])
                    ins.then_inc(o["vt_evac"], 1)
                sc.wait_ge(o["cs_pe"], 1)
                copy(csr[0:6, :], PS[0:6, 0:3072]).then_inc(o["cs_evac"], 1)
                sc.wait_ge(o["rg_pe"], 1)
                act_(oT, banks(0, 8, T), ACT.Exp).then_inc(o["eg"], 1)
                for n_, c in enumerate((0, 4, 1, 2, 3)):
                    sc.wait_ge(o["vn_pe"], n_ + 1)
                    if n_:
                        sc.wait_ge(o["s_pe"], n_)
                    for par in range(2):
                        h = slice(par * CH, (par + 1) * CH)
                        ins = copy(vnew[h, :, par, :], bank(1)[h, :].rearrange("p (a e) -> p a e", a=4))
                    ins.then_inc(o["vn_evac"], 1)
                    sc.wait_ge(o["o_pe"], n_ + 1)
                    copy(oT[:, :, c * CH:(c + 1) * CH], bank(2).rearrange("p (h t) -> p h t", t=CH))\
                        .then_inc(o["o_evac"], 1)
                sc.wait_ge(o["o_evac"], NCH)
                act_(sqO, oT, ACT.Square).then_inc(o["osq"], 1)
                act_(zth, zT, ACT.Tanh, scale=0.5).then_inc(o["zt"], 1)
                sc.wait_ge(o["orecip"], 1)
                act_(orr, orr, ACT.Sqrt).then_inc(o["orstd"], 1)

            def epilogue():
                for i in range(3):
                    n_ = P if i < 2 else TS
                    for half in range(2):
                        sc.wait_ge(pro_pe, 7 + 2 * i + half + 1)
                        copy(ytok[0:n_, i, half * 512:(half + 1) * 512], bank(2 * i + half)[0:n_, :])\
                            .then_inc(pro_evac, 1)

            prologue()
            norm(0, 0)
            ffn(0)
            even()
            norm(2, X_FFN[1])
            ffn(1)
            norm(3, X_FFN[2])
            ffn(2)
            norm(4, X_OD)
            odd()
            norm(5, X_FFN[3])
            ffn(3)
            epilogue()

        @block.vector
        def _(ve):
            tt, ts, stt, cp = ve.tensor_tensor, ve.tensor_scalar, ve.scalar_tensor_tensor, ve.tensor_copy
            steps = [0]

            def link(ins):
                steps[0] += 1
                ins.then_inc(dve_step, 1)
                ve.wait_ge(dve_step, steps[0])

            def norm(r, gain):
                ve.wait_ge(norm_sum, r + 1)
                link(ts(rs[:, 0:T], bank(6, T), 1.0 / D, EPS, ALU.mult, ALU.add))
                ve.reciprocal(rs[:, 0:T], rs[:, 0:T]).then_inc(norm_recip, 1)
                ve.wait_ge(norm_rstd, r + 1)
                for k in range(KT):
                    stt(hT[:, k, :], xT[:, k, :], cols[:, gain + k:gain + k + 1], rs[:, 0:T], ALU.mult, ALU.mult)\
                        .then_inc(h_ready, 1)

            def ffn(f):
                with ve.Fori(0, FT // 2) as i:
                    for slot in range(2):
                        ve.wait_ge(tanh_done, FT * f + 1 + slot + 2 * i)
                        stt(gated[:, slot, :], tanh_g[:, slot, :], 1.0, bank(2 * slot, T), ALU.add, ALU.mult)\
                            .then_inc(act_mid, 1)
                        ve.wait_ge(act_mid, FT * f + 1 + slot + 2 * i)
                        ve.wait_ge(gu_done, GU_FFN[f] + 1 + slot + 2 * i)
                        tt(RA[:, bass.ds(2 * T * i + T * slot, T)], gated[:, slot, :], bank(2 * slot + 1, T), ALU.mult)\
                            .then_inc(act_done, 1)
                xf = xT[:, :, :].rearrange("p k t -> p (k t)")
                with ve.Fori(0, KT // 2) as i:
                    for slot in range(2):
                        ve.wait_ge(dn_done, DN_FFN[f] + 1 + slot + 2 * i)
                        xm = xf[:, bass.ds(2 * T * i + T * slot, T)]
                        stt(xm, bank(4 + slot, T), 0.25, xm, ALU.mult, ALU.add).then_inc(x_upd, 1)

            def residual(base_dn):
                for m in range(KT):
                    ve.wait_ge((dn_half, dn_done)[m % 2], half_count(base_dn, m))
                    tt(xT[:, m, :], bank(4 + m % 2, T), xT[:, m, :], ALU.add).then_inc(x_upd, 1)

            def half_count(base_dn, m):
                if m % 2:
                    return base_dn + m // 2 + 1
                return (4 if base_dn == DN_OD else 0) + m // 2 + 1

            def even():
                norm(1, C_MIX)
                ve.wait_ge(s["ev_evac"], 3)
                ve.wait_ge(s["zero_qi"], 1)
                for h in (slice(0, IDX_D), slice(IDX_D, P)):
                    cp(kiT[h, 0:TP], pr[0:IDX_D, T_KI, 0:TP])
                    cp(kiT[h, TP + PAST:TP + NK_S], pr[0:IDX_D, T_KI, TP:T])
                for par in range(2):
                    h = slice(par * IDX_D, (par + 1) * IDX_D)
                    for p in range(IDX_PAIRS):
                        ins = cp(qibd[h, :, p, par * CH:(par + 1) * CH],
                                 pr[h, T_QI + p, :].rearrange("p (c t) -> p c t", t=CH))
                ins.then_inc(s["idx_prep"], 1)
                ve.wait_ge(s["kw_pe"], 1)
                cp(kwtok[:, 0:2, :], bank(7, 136).rearrange("p (a c) -> p a c", a=2))
                ins = cp(kwtok[0:TS, 2, :], bank(7)[0:TS, 136:204])
                ins.then_inc(s["kw_evac"], 1)
                ve.wait_ge(s["kw_evac"], 1)
                for par in range(2):
                    h = slice(par * CH, (par + 1) * CH)
                    for bp in range(2):
                        cp(wcol[h, bp:4:2, :], kwtok[bp * CH:(bp + 1) * CH, 0:2, IDX_D + par:IDX_D + IDX_H:2])
                    ins = cp(wcol[h, 4, :], kwtok[0:CH, 2, IDX_D + par:IDX_D + IDX_H:2])
                link(ins)
                tt(dwi, istk.unsqueeze(1).to_broadcast([P, 10, CH]),
                   wcol.rearrange("p c a -> p (c a)").unsqueeze(2).to_broadcast([P, 10, CH]), ALU.mult)\
                    .then_inc(s["dwi_ready"], 1)

                def take8(work, rounds):
                    for _ in range(rounds):
                        link(ve.max(top8, work))
                        link(ve.match_replace(work, top8, work, TAKEN))

                def penalty(pen, work):
                    ts(pen[0:CH, :], work, TAKEN, -BIG, ALU.not_equal, ALU.mult)
                    return ts(pen[CH:P, :], work, TAKEN, -BIG, ALU.not_equal, ALU.mult)

                ve.memset(workX[0:CH, 192:256], PADDED)
                ve.memset(workY[0:CH, 128:NK_S], PADDED)
                ve.wait_ge(s["combX"], 1)
                cp(workX[CH:P, :], bank(7)[CH:P, 0:256])
                cp(workX[0:CH, 0:192], bank(7)[0:CH, 0:192]).then_inc(s["combX_used"], 1)
                ve.wait_ge(s["combX_used"], 1)
                take8(workX, TOP_P // 8)
                penalty(pen3, workX[CH:P, :])
                penalty(pen2, workX[0:CH, 0:192])
                ve.wait_ge(s["combY"], 1)
                cp(workY[CH:P, 0:512], bank(7)[CH:P, :])
                cp(workY[CH:P, 512:NK_S], bank(4)[CH:P, 0:64])
                cp(workY[0:CH, 0:128], bank(4)[0:CH, 128:256]).then_inc(s["combY_used"], 1)
                ve.wait_ge(s["combY_used"], 1)
                take8(workY, TOP_P // 8)
                penalty(pen1, workY[0:CH, 0:128])

                def head_rstd(summed, n_):
                    ve.wait_ge(summed, 1)
                    link(ts(view(rs, 0, 4, T), banks(4, 4, T), 1.0 / A_D, EPS, ALU.mult, ALU.add))
                    ve.reciprocal(rs[:, 0:4 * T], rs[:, 0:4 * T]).then_inc(s["qk_recip"], 1)

                left = TOP_S // 8 - TOP_P // 8
                head_rstd(s["qsum"], 1)
                take8(workY, left // 2)
                ve.wait_ge(s["qk_rstd"], 1)
                ve.wait_ge(s["zero_q"], 1)
                for p in range(A_PAIRS):
                    for par in range(2):
                        h = slice(par * A_D, (par + 1) * A_D)
                        ins = stt(qbd[h, :, p, par * CH:(par + 1) * CH],
                                  pr[h, T_Q + p, :].rearrange("p (c t) -> p c t", t=CH), cols[h, C_QN:C_QN + 1],
                                  rs[h, p * T:(p + 1) * T].rearrange("p (c t) -> p c t", t=CH), ALU.mult, ALU.mult)
                        ins.then_inc(s["q_ready"], 1)
                ve.wait_ge(s["q_ready"], 8)
                head_rstd(s["ksum"], 2)
                take8(workY, left - left // 2)
                link(penalty(penS, workY[CH:P, :]))
                ve.wait_ge(s["qk_rstd"], 2)
                for p in range(A_PAIRS):
                    stt(pr[:, T_K + p, :], pr[:, T_K + p, :], cols[:, C_KN:C_KN + 1], rs[:, p * T:(p + 1) * T],
                        ALU.mult, ALU.mult).then_inc(s["k_ready"], 1)
                ve.wait_ge(s["gate_pe"], 1)
                for j in range(2):
                    ins = ts(gx[:, j, :], bank(4 + j, T), cols[:, C_B2 + j:C_B2 + j + 1], None, ALU.add)
                ins.then_inc(s["gate_used"], 1)
                ve.wait_ge(s["gate_used"], 1)
                stt(gx2, gx, -1.0, gx, ALU.mult, ALU.min).then_inc(s["g_neg"], 1)
                ve.wait_ge(s["g_ln"], 1)
                link(stt(gx, gx, 0.0, gx2, ALU.min, ALU.subtract))
                for p in range(B_PAIRS):
                    for c in range(NCH):
                        w = slice(c * CH, (c + 1) * CH)
                        ins = ve.tensor_tensor_scan(gB[:, p, w], ones[:, 0:CH], gx[:, p, w], 0.0, ALU.mult, ALU.add)
                link(ins)
                g4 = gB.rearrange("p a (c t) -> p (a c) t", t=CH)
                tt(gdm.rearrange("p a (c t) -> p (a c) t", t=CH), g4, g4[:, :, CH // 2:CH // 2 + 1].to_broadcast([P, 10, CH]),
                   ALU.subtract)
                tt(gdl.rearrange("p a (c t) -> p (a c) t", t=CH), g4[:, :, CH - 1:CH].to_broadcast([P, 10, CH]), g4,
                   ALU.subtract).then_inc(s["g_args"], 1)
                ve.wait_ge(s["g_exps"], 1)
                ve.wait_ge(s["zero_bd"], 1)
                for par in range(2):
                    h = slice(par * B_K, (par + 1) * B_K)
                    w = slice(par * CH, (par + 1) * CH)
                    for p in range(B_PAIRS):
                        def ch(x):
                            return x.rearrange("p (c t) -> p c t", t=CH)
                        stt(qe_bd[h, p, :, w], ch(pr[h, T_QB + p, :]), B_K ** -0.5, ch(e_b[h, p, :]), ALU.mult, ALU.mult)
                        tt(km_bd[h, p, :, w], ch(pr[h, T_KB + p, :]), ch(e_mid_n[h, p, :]), ALU.mult)
                        tt(kl_bd[h, p, :, w], ch(pr[h, T_KB + p, :]), ch(gdl[h, p, :]), ALU.mult)
                stt(qm, pr[:, T_QB:T_QB + 2, :], B_K ** -0.5, gdm, ALU.mult, ALU.mult).then_inc(s["bds_ready"], 1)
                ve.wait_ge(s["ga_pe"], 1)
                kmu = km_bd.rearrange("p a c e -> p (a c) e")
                for par in range(2):
                    h = slice(par * B_K, (par + 1) * B_K)
                    ins = tt(kmu[h, :, par * CH:(par + 1) * CH], PS[h, 3072:3712].rearrange("p (u t) -> p u t", t=CH),
                             causal[h, :].unsqueeze(1).to_broadcast([CH, 10, CH]), ALU.mult)
                ins.then_inc(s["abd_ready"], 1)
                ve.wait_ge(s["su_pe"], 1)
                ve.wait_ge(caches_in, 16 * 5)
                link(ve.memset(Sg[:, 0, :, :], 0.0))
                for c in (4, 0, 1, 2, 3):
                    src, dst = (5, 6) if c == 4 else (c, c + 1)
                    for p in range(B_PAIRS):
                        u = p * NCH + c
                        ins = stt(Sg[:, dst, p, :], Sg[:, src, p, :], es[:, p, c:c + 1], PS[:, u * P:(u + 1) * P],
                                  ALU.mult, ALU.add)
                    if c < 3 or c == 4:
                        link(ins)
                ins.then_inc(s["sg_ready"], 1)
                ve.wait_ge(s["gsum"], 1)
                link(ts(view(rs, 0, 4, T), banks(0, 4, T), 1.0 / B_V, EPS, ALU.mult, ALU.add))
                ve.reciprocal(rs[:, 0:4 * T], rs[:, 0:4 * T]).then_inc(s["grecip"], 1)
                ve.wait_ge(s["grstd"], 1)
                th = kl_bd.rearrange("p a c e -> p (a c e)")
                ve.wait_ge(s["sil_t"], 1)
                stt(th, th, 1.0, pr[:, T_RB:T_RB + 4, :].rearrange("p a b -> p (a b)"), ALU.add, ALU.mult)
                link(stt(oT[:, 4:8, :], oT[:, 4:8, :], cols[:, C_GLA:C_GLA + 1], view(rs, 0, 4, T), ALU.mult, ALU.mult))
                for h in range(4):
                    stt(oT[:, 4 + h, :], oT[:, 4 + h, :], 0.5, th[:, h * T:(h + 1) * T], ALU.mult, ALU.mult)\
                        .then_inc(s["ob_ready"], 1)

                def logits(b):
                    ve.wait_ge(s["qk_pe"], b + 1)
                    if b in (2, 3):
                        ve.wait_ge(s["pt_pe"], b - 1)
                    if b == 4:
                        ve.wait_ge(s["pt_pe"], 4)
                    L = logit(b)
                    k0 = PAST - CH * b
                    if b < 4:
                        nk = CH * (b + 1)
                        src = PS[:, (0, 2, 0, 2)[b] * 512:(0, 2, 0, 2)[b] * 512 + 1024]\
                            .rearrange("p (a c) -> p a c", a=4)[:, :, 0:nk]
                        ins = stt(L, src, A_D ** -0.5, biasT[:, :, k0:NK_S], ALU.mult, ALU.add)
                    else:
                        nk = NK_S
                        stt(L[:, :, 0:512], PS[:, 0:2048].rearrange("p (a c) -> p a c", a=4), A_D ** -0.5,
                            biasT[:, :, 0:512], ALU.mult, ALU.add)
                        ins = stt(L[:, :, 512:NK_S], bank(4, 256).rearrange("p (a c) -> p a c", a=4), A_D ** -0.5,
                                  biasT[:, :, 512:NK_S], ALU.mult, ALU.add)
                    ins.then_inc(s["l_done"], 1)
                    ve.wait_ge(s["l_done"], b + 1)
                    if b:
                        pen = (None, pen1, pen2, pen3, penS)[b]
                        link(tt(L, L, pen.unsqueeze(1).to_broadcast([P, A_PAIRS, nk]), ALU.add))
                    link(ve.tensor_reduce(mx[:, b, 0, :], L, AX, ALU.max))
                    ts(mx[:, b, 1, :], mx[:, b, 0, :], -1.0, None, ALU.mult).then_inc(s["nmx"], 1)

                def probs(b):
                    nk = CH * (b + 1) if b < 4 else NK_S
                    ve.wait_ge(s["exps_done"], b + 1)
                    link(ve.reciprocal(mx[:, b, 0, :], mx[:, b, 2, :]))
                    tt(logit(b), logit(b), mx[:, b, 0, :].unsqueeze(2).to_broadcast([P, A_PAIRS, nk]), ALU.mult)\
                        .then_inc(s["p_ready"], 1)

                def heads_out(b):
                    ve.wait_ge(s["pv_pe"], b + 1)
                    for par in range(2):
                        h = slice(par * A_D, (par + 1) * A_D)
                        ins = cp(oT[h, 0:4, b * CH:(b + 1) * CH],
                                 bank((6, 7, 6, 7, 2)[b])[h, :].rearrange("p (a c) -> p a c", a=4)
                                 [:, :, par * CH:(par + 1) * CH])
                    ins.then_inc(s["pv_evac"], 1)

                ve.wait_ge(s["bias_in"], 32)
                logits(0)
                logits(1)
                probs(0)
                logits(2)
                probs(1)
                heads_out(0)
                logits(3)
                probs(2)
                heads_out(1)
                probs(3)
                heads_out(2)
                heads_out(3)
                logits(4)
                probs(4)
                heads_out(4)
                residual(DN_EV)

            def odd():
                g = [growv(i)[0:C_H, :] for i in range(4)]
                link(ve.memset(qp[:, :, 0:3], 0.0))
                ve.wait_ge(small_in, 48)
                ve.wait_ge(o["ab_pe"], 1)
                ts(g[3], bank(5, T)[0:C_H, :], -80.0, -1.0, ALU.max, ALU.mult)
                link(ts(g[0], bank(4, T)[0:C_H, :], cols[0:C_H, 223:224], None, ALU.add))
                stt(g[1], g[0], -1.0, g[0], ALU.mult, ALU.min).then_inc(o["g1"], 1)
                ve.wait_ge(o["g2"], 1)
                link(ts(g[3], g[3], 1.0, None, ALU.add))
                ve.reciprocal(g[3], g[3])
                link(stt(g[0], g[0], 0.0, g[1], ALU.max, ALU.add))
                link(ts(g[0], g[0], cols[0:C_H, 224:225], -1.0, ALU.mult, ALU.mult))
                for c in range(NCH):
                    w = slice(c * CH, (c + 1) * CH)
                    ins = ve.tensor_tensor_scan(g[2][:, w], ones[0:C_H, 0:CH], g[0][:, w], 0.0, ALU.mult, ALU.add)
                ins.then_inc(o["g_rows"], 1)

                def conv(t):
                    tile_ = OD_TILES[t]
                    buf = qp[:, t % 4, :]
                    ve.wait_ge(o["evac"], t + 1)
                    cp(cst[:, tile_, 0:3], buf[:, 256:259])
                    cp(cst[:, tile_, 3:6], buf[:, 323:326])
                    link(cp(buf[:, 259:262], cols[:, C_ST + tile_:C_ST + 72:24]))
                    c_ = cring[:, t % 4, :]
                    link(ts(c_, buf[:, 0:323], cols[:, C_CONV + tile_:C_CONV + tile_ + 1], None, ALU.mult))
                    for j in range(1, 4):
                        at = C_CONV + 24 * j + tile_
                        ins = stt(c_, buf[:, j:j + 323], cols[:, at:at + 1], c_, ALU.mult, ALU.add)
                        if j < 3:
                            link(ins)
                    ins.then_inc(o["conv"], 1)

                def silu(t):
                    ve.wait_ge(o["th"], t + 1)
                    part, h = OD_TILES[t] // 8, OD_TILES[t] % 8
                    dst = cv[:, part, h // 2, :, (h % 2) * CH:(h % 2 + 1) * CH]
                    for c0, c1, at in ((0, 4, 0), (4, 5, TP + 3)):
                        ins = stt(dst[:, c0:c1, :], th2[:, t % 2, at:at + CH * (c1 - c0)].rearrange("p (c t) -> p c t", t=CH),
                                  1.0, cring[:, t % 4, at:at + CH * (c1 - c0)].rearrange("p (c t) -> p c t", t=CH),
                                  ALU.add, ALU.mult)
                    ins.then_inc(o["silu"], 1)

                def columns():
                    ve.wait_ge(o["col_pe"], 1)
                    for par in range(2):
                        ins = cp(colG[par * CH:(par + 1) * CH, :, :, :].rearrange("p w c a -> p (w c) a"),
                                 bank(6, 80)[0:CH, :].rearrange("p (u h) -> p u h", h=8)[:, :, par:8:2])
                    ins.then_inc(o["cols_ready"], 1)
                    ve.wait_ge(o["cols_ready"], 1)
                    ts(bhalf, colG[:, 1, :, :], 0.5, None, ALU.mult)

                def differences(half):
                    ve.wait_ge(o["row_pe"], half + 1)
                    if half == 0:
                        ve.wait_ge(o["masks"], 1)
                    cp(gl[:, 4 * half:4 * half + 4, :],
                       banks(4, 4, T).rearrange("p h (c t) -> p h c t", t=CH)[:, :, :, CH - 1])
                    for pp in range(2):
                        p = 2 * half + pp
                        for c in range(NCH):
                            row = banks(4 + 2 * pp, 2, T)[:, :, c * CH:(c + 1) * CH]
                            for dst, mask in ((At, maskI), (Dm, maskS)):
                                ins = stt(dst[:, c, p, :].rearrange("p (a t) -> p a t", a=2), row, colG[:, 0, c, p:p + 1],
                                          mask.rearrange("p (a t) -> p a t", a=2), ALU.subtract, ALU.add)
                    if half == 1:
                        link(ins)
                        for par in range(2):
                            h = slice(par * CH, (par + 1) * CH)
                            ins = tt(klc[h, :, :], gl[h, par:8:2, :].rearrange("p a c -> p c a"), colG[h, 0, :, :],
                                     ALU.subtract)
                    ins.then_inc(o["row_used"], 1)

                def head_rstd(g_):
                    ve.wait_ge(o["sum"], g_ + 1)
                    link(ts(view(rs, 0, 4, T), banks(4, 4, T), 0.25, EPS, ALU.mult, ALU.add))
                    ve.reciprocal(rs[:, 0:4 * T], rs[:, 0:4 * T]).then_inc(o["recip"], 1)

                def unit_heads(g_):
                    ve.wait_ge(o["rstd"], g_ + 1)
                    scale = 0.5 if g_ < 2 else 0.5 * C_D ** -0.5
                    c_ = group(g_)
                    stt(c_, c_, scale, rs[:, 0:4 * T], ALU.mult, ALU.mult).then_inc(o["kq_ready"], 1)
                    ve.wait_ge(o["kq_ready"], g_ + 1)

                for t in range(24):
                    conv(t)
                    if t:
                        silu(t - 1)
                    if t == 2:
                        columns()
                    if t == 4:
                        differences(0)
                    if t == 6:
                        differences(1)
                    if t == 12:
                        head_rstd(0)
                    if t == 14:
                        unit_heads(0)
                        head_rstd(1)
                    if t == 16:
                        unit_heads(1)
                    if t == 18:
                        head_rstd(2)
                    if t == 20:
                        unit_heads(2)
                        head_rstd(3)
                    if t == 22:
                        unit_heads(3)
                silu(23)
                ve.wait_ge(o["gexp"], 1)
                stt(ncol, egc, -1.0, colG[:, 1, :, :], ALU.mult, ALU.mult)
                ve.wait_ge(o["dexp"], 1)
                for c in range(NCH):
                    ve.wait_ge(o["kk_pe"], c + 1)
                    for p in range(C_PAIRS):
                        ins = stt(Lm[:, c, p, :], bank(4)[:, p * P:(p + 1) * P], colG[:, 1, c, p:p + 1], Dm[:, c, p, :],
                                  ALU.mult, ALU.mult)
                    ins.then_inc(o["kk_used"], 1)
                    tt(At[:, c, :, :], bank(5).rearrange("p (a c) -> p a c", a=4), At[:, c, :, :], ALU.mult)\
                        .then_inc(o["kk_used"], 1)
                for c in range(NCH):
                    ve.wait_ge(o["kk_used"], 2 * NCH)
                    link(tt(tT[:, c, :, :], Lm[:, c, :, :], lev[:, 0:1, :].to_broadcast([P, C_PAIRS, P]), ALU.mult))
                    tt(tT[:, c, :, :], ident[:, :].unsqueeze(1).to_broadcast([P, C_PAIRS, P]), tT[:, c, :, :],
                       ALU.subtract).then_inc(o["t1"], 1)
                for level in range(5):
                    for c in range(NCH):
                        m = level * NCH + c
                        ve.wait_ge(o["u_pe"], m + 1)
                        if level == 0:
                            ve.wait_ge(o["t1"], NCH)
                            ve.wait_ge(o["u1_evac"], NCH)
                        if level < 4:
                            ve.wait_ge(o["t_pe"], m + 1)
                            tt(tT[:, c, :, :], tT[:, c, :, :], bank(6).rearrange("p (a c) -> p a c", a=4), ALU.subtract)\
                                .then_inc(o["t_upd"], 1)
                        tt(uT[:, c, :, :], uT[:, c, :, :], bank(7).rearrange("p (a c) -> p a c", a=4), ALU.subtract)\
                            .then_inc(o["u_upd"], 1)
                ve.wait_ge(o["eg"], 1)
                for p in range(C_PAIRS):
                    c_ = cv[:, 0, p, :, :].rearrange("p c (a t) -> p c a t", a=2)
                    tt(c_, c_, oT[:, 2 * p:2 * p + 2, :].rearrange("p a (c t) -> p c a t", t=CH), ALU.mult)\
                        .then_inc(o["qe"], 1)
                ve.wait_ge(o["states"], 1)
                for n_, c in enumerate((0, 4, 1, 2, 3)):
                    ve.wait_ge(o["ks_pe"], n_ + 1)
                    ve.wait_ge(o["vt_evac"], NCH)
                    if n_:
                        ve.wait_ge(o["vn_pe"], n_)
                    for p in range(C_PAIRS):
                        ins = stt(Rr[:, p, :], bank(0)[:, p * P:(p + 1) * P], ncol[:, c, p:p + 1], Vb[:, c, p, :],
                                  ALU.mult, ALU.add)
                    ins.then_inc(o["r_ready"], 1)
                    ve.wait_ge(o["s_pe"], n_ + 1)
                    S = Sd[:, 1 if c == 4 else 0, :, :]
                    if n_ > 1:
                        ve.wait_ge(o["s_upd"], n_)
                    for h in range(C_H):
                        ins = stt(S[:, h, :], S[:, h, :], es8[:, h, c:c + 1],
                                  bank(3 + h // 4)[:, (h % 4) * P:(h % 4 + 1) * P], ALU.mult, ALU.add)
                    ins.then_inc(o["s_upd"], 1)
                ve.wait_ge(o["osum"], 1)
                link(ts(orr, banks(0, 8, T), 1.0 / C_D, EPS, ALU.mult, ALU.add))
                ve.reciprocal(orr, orr).then_inc(o["orecip"], 1)
                ve.wait_ge(o["zt"], 1)
                stt(zth, zth, 1.0, zT, ALU.add, ALU.mult)
                ve.wait_ge(o["orstd"], 1)
                link(stt(oT, oT, cols[:, C_OD:C_OD + 1], orr, ALU.mult, ALU.mult))
                stt(oT, oT, 0.5, zth, ALU.mult, ALU.mult).then_inc(o["og"], 1)
                residual(DN_OD)

            ve.sem_inc(x_upd, 2)
            ve.sem_inc(act_done, 2)
            norm(0, C_FFN)
            ffn(0)
            even()
            norm(2, C_FFN + 8)
            ffn(1)
            norm(3, C_FFN + 16)
            ffn(2)
            norm(4, C_MIX + 8)
            odd()
            norm(5, C_FFN + 24)
            ffn(3)

        @block.gpsimd
        def _(po):
            steps = [0]

            def link(ins):
                steps[0] += 1
                ins.then_inc(pool_step, 1)
                po.wait_ge(pool_step, steps[0])

            def store(dst, src):
                po.dma_start(dst, src).then_inc(out_sem, 16)

            sel = po.affine_select
            po.memset(ones[:, :], 1.0)
            link(po.memset(ident[:, :], 0.0))
            sel(out=ident[:, :], in_=ident[:, :], compare_op=ALU.not_equal, fill=1.0, base=0, pattern=[[-1, P]],
                channel_multiplier=1).then_inc(consts, 1)
            po.memset(halves, 0.0)
            po.memset(istk, 0.0)
            link(po.memset(causal, 1.0))
            po.memset(halves[0:64, 0:64], 1.0)
            po.memset(halves[64:P, 64:P], 1.0)
            for par in range(2):
                h = slice(par * CH, (par + 1) * CH)
                sel(out=causal[h, :], in_=causal[h, :], compare_op=ALU.is_ge, fill=0.0, base=0, pattern=[[1, CH]],
                    channel_multiplier=-1)
                ins = sel(out=istk[h, :], in_=istk[h, :], compare_op=ALU.not_equal, fill=1.0, base=0,
                          pattern=[[-1, CH]], channel_multiplier=1)
            link(ins)
            po.wait_ge(small_in, 48)
            for b, lo, hi in bucket_runs():
                ins = po.tensor_copy(biasrow[0:A_H, lo + REL0:hi + REL0 + 1],
                                     rbT[0:A_H, b:b + 1].to_broadcast([A_H, hi - lo + 1]))
            link(ins)
            po.dma_start(scratch, biasrow[0:A_H, :].unsqueeze(1).to_broadcast([A_H, CH, REL_N])).then_inc(s["bias_out"], 16)
            po.wait_ge(s["bias_out"], 16)
            for par in range(2):
                src = bass.AP(scratch.tensor, par * CH * REL_N + CH - 1,
                              [[REL_N - 1, CH], [2 * CH * REL_N, A_PAIRS], [1, NK_S]])
                po.dma_start(biasT[par * CH:(par + 1) * CH, :, :], src).then_inc(s["bias_in"], 16)
            po.wait_ge(x_upd, X_EV + 2)
            po.wait_ge(h_ready, KT * (NORM_EV + 1))
            po.memset(view(RA, 2560, 1280), 0.0).then_inc(s["zero_qi"], 1)
            po.memset(view(RA, 0, 2560), 0.0).then_inc(s["zero_q"], 1)
            po.wait_ge(s["kct_pe"], 4)
            po.memset(view(RB, bd_at, 3840), 0.0).then_inc(s["zero_bd"], 1)
            po.wait_ge(s["kw_evac"], 1)
            store(O["p_idx_k"][0, 0].rearrange("(i p) d -> p i d", p=P), kwtok[:, 0:2, 0:IDX_D])
            store(O["s_idx_k"][0, 0], kwtok[0:TS, 2, 0:IDX_D])
            for name, tok in (("v", vtok), ("k", ktok)):
                po.wait_ge(s[name + "tok_evac"], 3)
                store(O[f"p_attn_{name}"][0, 0].rearrange("(i p) h d -> p i (h d)", p=P), tok[:, 0:2, :])
                store(O[f"s_attn_{name}"][0, 0].rearrange("p h d -> p (h d)"), tok[0:TS, 2, :])
            po.wait_ge(s["sg_ready"], 1)
            for name, i in (("p_gla", 4), ("s_gla", 6)):
                store(O[name][0, 0].rearrange("(a b) d e -> a (b d) e", b=2).rearrange("a q e -> q a e"), Sg[:, i, :, :])
            po.wait_ge(x_upd, X_FFN[1] + 2)
            po.wait_ge(out_sem, 16 * 8)
            po.memset(lev, 0.0)
            po.memset(maskI, -BIG)
            po.memset(maskS, BIG)
            po.memset(Sd[:, 0, :, :], 0.0)
            link(po.memset(klc, 0.0))
            for par in range(2):
                h = slice(par * CH, (par + 1) * CH)
                po.memset(maskI[h, par * CH:(par + 1) * CH], 0.0)
                link(po.memset(maskS[h, par * CH:(par + 1) * CH], 0.0))
                link(sel(out=maskI[h, par * CH:(par + 1) * CH], in_=maskI[h, par * CH:(par + 1) * CH], compare_op=ALU.is_ge,
                    fill=-BIG, base=0, pattern=[[1, CH]], channel_multiplier=-1))
                link(sel(out=maskS[h, par * CH:(par + 1) * CH], in_=maskS[h, par * CH:(par + 1) * CH], compare_op=ALU.is_gt,
                    fill=BIG, base=0, pattern=[[-1, CH]], channel_multiplier=1))
            for i in range(6):
                m = 1 << i
                part = lev[:, i, :].rearrange("p (n r) -> p n r", r=2 * m)[:, :, 0:m]
                link(po.memset(part, 1.0))
                link(sel(out=part, in_=part, compare_op=ALU.is_ge, fill=0.0, base=-m, pattern=[[-2 * m, P // (2 * m)], [0, m]],
                         channel_multiplier=1))
                ins = sel(out=part, in_=part, compare_op=ALU.is_ge, fill=0.0, base=2 * m - 1,
                          pattern=[[2 * m, P // (2 * m)], [0, m]], channel_multiplier=-1)
                if i < 5:
                    link(ins)
            ins.then_inc(o["masks"], 1)
            po.wait_ge(x_upd, X_OD + 2)
            po.memset(vnew.rearrange("p a b e -> p (a b e)"), 0.0).then_inc(o["zero_v"], 1)
            po.sem_inc(o["states"], 1)
            for level in range(5):
                for c in range(NCH):
                    m = level * NCH + c
                    if level == 0:
                        po.wait_ge(o["kk_used"], 2 * NCH)
                    else:
                        po.wait_ge(o["y_pe"], m - NCH + 1)
                    po.tensor_tensor(Dm[:, c, :, :], Lm[:, c, :, :],
                                     lev[:, level + 1:level + 2, :].to_broadcast([P, C_PAIRS, P]), ALU.mult)\
                        .then_inc(o["bm"], 1)
            po.wait_ge(o["cs_evac"], 1)
            store(O["p_conv"][0, 0], csr[0:3, :])
            store(O["s_conv"][0, 0], csr[3:6, :])
            po.wait_ge(o["s_upd"], NCH)
            store(O["p_delta"][0, 0].rearrange("h d e -> d h e"), Sd[:, 0, :, :])
            store(O["s_delta"][0, 0].rearrange("h d e -> d h e"), Sd[:, 1, :, :])
            po.wait_ge(pro_evac, 13)
            store(O["y_prompt"][0].rearrange("(i p) d -> p i d", p=P), ytok[:, 0:2, :])
            store(O["y_sample"][0], ytok[0:TS, 2, :])
            po.wait_ge(out_sem, 16 * 14)


INPUTS = ["x_prompt", "x_sample", "cache_attn_k", "cache_attn_v", "cache_idx_k", "state_gla", "state_delta",
          "state_conv", "ffn_norm", "ffn_w_gate", "ffn_w_up", "ffn_w_down", "mix_norm", "ev_w_in", "ev_q_norm",
          "ev_k_norm", "rel_bias", "ev_gate_w2", "ev_gate_b2", "ev_gla_norm", "ev_w_out", "od_w_in", "od_conv_w",
          "od_a_log", "od_dt_bias", "od_norm", "od_w_out"]
OUTPUTS = [("y_prompt", (1, TP, D)), ("y_sample", (1, TS, D)),
           ("p_attn_k", (1, 1, TP, 8, 64)), ("p_attn_v", (1, 1, TP, 8, 64)), ("p_idx_k", (1, 1, TP, 64)),
           ("p_gla", (1, 1, 4, 64, 128)), ("p_delta", (1, 1, 8, 128, 128)), ("p_conv", (1, 1, 3, 3072)),
           ("s_attn_k", (1, 1, TS, 8, 64)), ("s_attn_v", (1, 1, TS, 8, 64)), ("s_idx_k", (1, 1, TS, 64)),
           ("s_gla", (1, 1, 4, 64, 128)), ("s_delta", (1, 1, 8, 128, 128)), ("s_conv", (1, 1, 3, 3072))]


def kernel(**inputs):
    import numpy as np
    import concourse.bacc as bacc
    from concourse.bass_utils import run_bass_kernel_spmd

    nc = bacc.Bacc("TRN2", target_bir_lowering=False, num_devices=1)
    arrays = {f"in_{name}": np.ascontiguousarray(inputs[name]) for name in INPUTS}
    ins = {name: nc.dram_tensor(f"in_{name}", arrays[f"in_{name}"].shape, F32, kind="ExternalInput").ap()
           for name in INPUTS}
    outs = {name: nc.dram_tensor(f"out_{name}", shape, F32, kind="ExternalOutput").ap() for name, shape in OUTPUTS}
    build(nc, ins, outs)
    r = run_bass_kernel_spmd(nc, [arrays], core_ids=[0])
    return tuple(r.results[0][f"out_{name}"] for name, _ in OUTPUTS)
```

```python
from contextlib import ExitStack

import concourse.bass as bass
from concourse import mybir

ALU = mybir.AluOpType
ACT = mybir.ActivationFunctionType
F32 = mybir.dt.float32
F32R = mybir.dt.float32r
AX = mybir.AxisListType.X

P = 128
D = 1024
KT = D // P
TP, TS = 256, 64
T = TP + TS
ARENA_N = 52968
RB_N = 29300
CH = 64
NCH = T // CH
PAST = 512
FF = 2816
FT = FF // P
EPS = 1e-6
SPLIT_N = (KT + FT) * T + 2 * 2 * FT * P
BIG = 1e30
TAKEN = -3.0e38
PADDED = -2.0e38
A_H, A_D, A_PAIRS = 8, 64, 4
IDX_H, IDX_D, IDX_PAIRS = 4, 64, 2
TOP_P = min(256, TP // 4)
NK_S = PAST + TS
TOP_S = min(256, NK_S // 4)
B_PAIRS, B_K, B_V, B_RANK, B_TAU = 2, 64, 128, 16, 16.0
C_H, C_D, C_PAIRS = 8, 128, 4
N_BUCKETS, MAX_DIST = 32, 128
REL0 = NK_S - 1
REL_N = 640

EV = {}
_at = 0
for _name, _size in (("q", 512), ("k", 512), ("v", 512), ("qi", 256), ("ki", 64), ("wi", 4),
                     ("qb", 256), ("kb", 256), ("vb", 512), ("rb", 512), ("ab", 16)):
    EV[_name] = _at
    _at += _size
EV_LOADS = [[(EV["qi"], 128), (EV["qi"] + 128, 128)], [(EV["ki"], 68), (EV["ab"], 16)]]
for _name, _tiles in (("q", 4), ("k", 4), ("qb", 2), ("kb", 2), ("vb", 4), ("v", 4), ("rb", 4)):
    for _t in range(0, _tiles, 2):
        EV_LOADS.append([(EV[_name] + 128 * _t, 128), (EV[_name] + 128 * _t + 128, 128)])
T_QI, T_KI, T_AB, T_Q, T_K, T_QB, T_KB, T_VB, T_V, T_RB = 0, 2, 3, 4, 8, 12, 14, 16, 20, 24
N_EV = 2 * len(EV_LOADS)

OD_TILES = list(range(8, 16)) + list(range(0, 8)) + list(range(16, 32))
N_OD = len(OD_TILES)

GU_FFN = [0, 22 + 14, 22 + 14 + 22, 22 + 14 + 22 + 22 + 16]
GU_EV = 22
GU_OD = 80
DN_FFN = [0, 12, 20, 32]
DN_EV, DN_OD = 8, 28
N_GU = 118
N_DN = 40


def bucket_runs():
    def bucket(rel):
        n, half = abs(rel), N_BUCKETS // 2
        exact = half // 2
        if n >= exact:
            j = max(j for j in range(half - exact + 1) if n ** exact >= exact ** exact * (MAX_DIST // exact) ** j)
            n = min(half - 1, exact + j)
        return n + (half if rel > 0 else 0)
    runs = []
    for rel in range(-REL0, REL_N - REL0):
        b = bucket(rel)
        if runs and runs[-1][0] == b:
            runs[-1][2] = rel
        else:
            runs.append([b, rel, rel])
    return runs


def build(nc, I, O):
    with ExitStack() as ctx:
        def sb(name, shape):
            return ctx.enter_context(nc.sbuf_tensor(name, shape, F32))

        def sem(name):
            return ctx.enter_context(nc.semaphore(name))

        PS = ctx.enter_context(nc.psum_tensor("PS", [P, 8 * 512], F32))
        arena = sb("arena", [P, ARENA_N])
        arena_at = nc.sbuf_base - 4 * ARENA_N
        placed = [0]

        def place(name, *dims):
            at = placed[0]
            n_ = 1
            for d in dims:
                n_ *= d
            placed[0] = at + (n_ + 7) // 8 * 8
            assert placed[0] <= ARENA_N
            return nc.alloc_sbuf_tensor_at(name, [P, *dims], F32, offset=arena_at + 4 * at), at

        def rounded(name, at, *dims):
            return nc.alloc_sbuf_tensor_at(name, [P, *dims], F32R, offset=arena_at + 4 * at)

        xT, _ = place("xT", KT, T)
        hT, hT_at = place("hT", KT, T)
        gu, _ = place("gu", 2, 2048)
        dn, _ = place("dn", 2, FT * 128)
        RA, RA_at = place("RA", 7040)
        RB, RB_at = place("RB", RB_N)
        ident, _ = place("ident", P)
        ones, _ = place("ones", P)
        cols, _ = place("cols", 226)
        rs, _ = place("rs", 1280)
        oT = hT[:, :, :]
        h_hi = rounded("h_hi", hT_at, KT, T)
        act_hi = rounded("act_hi", RA_at, FT * T)
        h_lo = rounded("h_lo", RB_at, KT, T)
        act_lo = rounded("act_lo", RB_at + KT * T, FT * T)
        w_parts = rounded("w_parts", RB_at + (KT + FT) * T, 2, 2, FT * P)

        def bank(b, n=512, at=0):
            return PS[:, b * 512 + at:b * 512 + at + n]

        def banks(b, m, n):
            return PS[:, b * 512:(b + m) * 512].rearrange("p (a c) -> p a c", a=m)[:, :, 0:n]

        def view(t, at, *dims):
            n = 1
            for d in dims:
                n *= d
            flat = t[:, at:at + n]
            if len(dims) == 1:
                return flat
            names = "abcd"[:len(dims)]
            return flat.rearrange(f"p ({' '.join(names)}) -> p {' '.join(names)}",
                                  **{n_: d for n_, d in zip(names, dims)})

        act = view(RA, 0, FT, T)
        squares = view(RA, 0, KT, T)
        xnat = view(RA, 0, 3, D)
        qbd = view(RA, 0, NCH, A_PAIRS, P)
        qibd = view(RA, 2560, NCH, IDX_PAIRS, P)
        pT = view(RA, 3840, 5, 512)
        workX = view(RA, 3840, 256)
        workY = view(RA, 3840 + 256, 576)
        sqE = view(RA, 3840 + 1280, 4, T)
        gx = view(RA, 3840, 2, T)
        gx2 = view(RA, 3840 + 640, 2, T)
        e_mid_n = view(RA, 3840 + 1280, 2, T)
        e_b = view(RA, 3840 + 1920, 2, T)
        dwi = view(RA, 6400, 10, CH)
        n = SPLIT_N
        rstd = view(RB, n, T); n += T
        total = view(RB, n, T); n += T
        square = view(RB, n, T); n += T
        high_at = n
        vcache = view(RB, n, 4, 512); n += 2048
        kcn = view(RB, n, 4, 512); n += 2048
        ipn = view(RB, n, 4, 64); n += 256
        biasT = view(RB, n, A_PAIRS, NK_S)
        biasrow = view(RB, n, REL_N); n += A_PAIRS * NK_S
        Sg5 = view(RB, n, B_PAIRS, P); n += B_PAIRS * P
        rbT = view(RB, n, 32); n += 32
        w2 = view(RB, n, 256); n += 256
        halves = view(RB, n, P); n += P
        causal = view(RB, n, CH); n += CH
        istk = view(RB, n, CH); n += CH
        assert n <= RB_N, n
        n = 0
        pr = view(RB, n, N_EV, T); n += N_EV * T
        kcT = view(RB, n, A_PAIRS, 512); n += 2048
        kiT = view(RB, n, TP + NK_S); n += TP + NK_S
        l_at = n
        n += A_PAIRS * NK_S
        bd_at = n
        qe_bd = view(RB, n, B_PAIRS, NCH, P); n += 1280
        km_bd = view(RB, n, B_PAIRS, NCH, P); n += 1280
        kl_bd = view(RB, n, B_PAIRS, NCH, P); n += 1280
        Sgs = view(RB, n, 6, B_PAIRS, P); n += 6 * B_PAIRS * P
        kwtok = view(RB, n, 3, 68); n += 204
        wcol = view(RB, n, NCH, IDX_PAIRS); n += 10
        mx = view(RB, n, NCH, 3, 4); n += 60
        es = view(RB, n, B_PAIRS, NCH); n += 10
        top8 = view(RB, n, 8); n += 8
        qm = view(RB, n, B_PAIRS, T); n += 640
        pen3 = view(RB, n, 256); n += 256
        pen1 = view(RB, n, 128); n += 128
        assert n <= SPLIT_N, n
        vtok = view(RB, high_at + 2048, 3, 512)
        penS = view(RB, high_at + 2048 + 1536, NK_S)
        pen2 = view(RB, high_at + 2048 + 1536 + NK_S, 192)
        ktok = view(RB, 0, 3, 512)
        rX3 = view(RB, l_at, 2, 256)
        rX2 = view(RB, l_at + 512, 2, 192)
        rYS = view(RB, l_at + 896, 2, NK_S)
        rY1 = view(RB, l_at + 2048, 2, 128)
        gB = view(RB, l_at, B_PAIRS, T)
        gdm = view(RB, l_at + 640, B_PAIRS, T)
        gdl = view(RB, l_at + 1280, B_PAIRS, T)
        vp = pr[:, T_V:T_V + 4, :].rearrange("p a b -> p (a b)").rearrange("p (u e) -> p u e", e=P)
        n = high_at
        Sd = view(RB, n, 2, C_H, P); n += 2048
        cst = view(RB, n, 24, 6); n += 144
        csr = view(RB, n, 24 * P)
        Dm = view(RB, n, NCH, C_PAIRS, P); n += 2560
        lev = view(RB, n, 6, P); n += 768
        maskI = view(RB, n, P); n += P
        maskS = view(RB, n, P); n += P
        wab = view(RB, n, 8, 16); n += 128
        rows8 = view(RB, n, 4, T); n += 4 * T
        gl = view(RB, n, C_H, NCH); n += C_H * NCH
        es8 = view(RB, n, C_H, NCH); n += C_H * NCH
        colG = view(RB, n, 2, NCH, C_PAIRS); n += 40
        egc = view(RB, n, NCH, C_PAIRS); n += 20
        ncol = view(RB, n, NCH, C_PAIRS); n += 20
        bhalf = view(RB, n, NCH, C_PAIRS); n += 20
        klc = view(RB, n, NCH, C_PAIRS); n += 20
        assert n <= RB_N, n
        n = 0
        cv = view(RB, n, 3, C_PAIRS, NCH, P); n += 24 * T
        qp = view(RB, n, 4, 326); n += 4 * 326
        zT = view(RB, n, 8, T); n += 8 * T
        uT = view(RB, n, NCH, C_PAIRS, P); n += 2560
        At = view(RB, n, NCH, C_PAIRS, P); n += 2560
        Kl = view(RB, n, NCH, C_PAIRS, P); n += 2560
        lm_at = n
        Lm = view(RB, n, NCH, C_PAIRS, P); n += 2560
        Vb = Lm
        assert n <= high_at, n
        tT = view(RA, 0, NCH, C_PAIRS, P)
        yT = view(RA, 2560, NCH, C_PAIRS, P)
        vnew = view(RA, 5120, C_PAIRS, 2, P)
        Rr = view(RA, 6144, C_PAIRS, P)
        sqO = view(RA, 0, 8, T)
        orr = view(RA, 2560, 8, T)
        zth = view(RB, lm_at, 8, T)
        cring = view(RA, 0, 4, 323)
        sq4 = view(RA, 2560, 4 * T)
        th2 = view(RA, 3840, 2, 323)
        vbx = pr[:, T_VB:T_VB + 4, :].rearrange("p a b -> p (a b)").rearrange("p (a c e) -> p a c e", a=2, e=P)
        ytok = view(RA, 0, 3, D)
        tanh_g = view(rs, 0, 2, T)
        gated = view(rs, 640, 2, T)

        def group(g):
            return cv[:, 1 - g // 2, 2 * (g % 2):2 * (g % 2) + 2, :, :].rearrange("p a c e -> p (a c e)")

        def Sg(i):
            return Sg5 if i == 5 else Sgs[:, i if i < 5 else 5, :, :]

        def growv(i):
            return rows8[:, i, :]

        def logit(b):
            return view(RB, l_at + (1024 if b in (1, 3) else 0), A_PAIRS, CH * (b + 1) if b < 4 else NK_S)

        def pt_slot(b):
            return (0, 2, 0, 2, 0)[b]

        C_FFN, C_MIX, C_GLA, C_OD, C_B2, C_QN, C_KN = 0, 32, 48, 49, 50, 52, 53
        C_CONV, C_ST = 54, 150

        gu_loaded = [sem("gu_loaded0"), sem("gu_loaded1")]
        dn_loaded = [sem("dn_loaded0"), sem("dn_loaded1")]
        gu_half, gu_done = sem("gu_half"), sem("gu_done")
        dn_half, dn_done = sem("dn_half"), sem("dn_done")
        x_upd = sem("x_upd")
        scaled, tanh_done, act_mid, act_done, act_split = (sem(s) for s in (
            "scaled", "tanh_done", "act_mid", "act_done", "act_split"))
        hi_done, lo_done, h_hi_done = sem("hi_done"), sem("lo_done"), sem("h_hi_done")
        sq_done, total_ready, norm_sum, norm_recip, norm_rstd, h_ready = (sem(s) for s in (
            "sq_done", "total_ready", "norm_sum", "norm_recip", "norm_rstd", "h_ready"))
        consts = sem("consts")
        params_in, x_in, caches_in, small_in, out_sem = (sem(s) for s in (
            "params_in", "x_in", "caches_in", "small_in", "out_sem"))
        pool_step, dve_step, act_step = sem("pool_step"), sem("dve_step"), sem("act_step")
        pro_pe, pro_evac = sem("pro_pe"), sem("pro_evac")

        scratch = nc.dram_tensor("bias_rows", (A_H, CH, REL_N), F32, kind="Internal").ap()

        def gu_source(n):
            slot = gu[:, n % 2, :]
            for f in range(4):
                if GU_FFN[f] <= n < GU_FFN[f] + FT:
                    g = n - GU_FFN[f]
                    return [(slot[:, j * 1024:(j + 1) * 1024].rearrange("p (k c) -> p k c", k=KT),
                             ffn_w(I[name], f)[:, :, g * P:(g + 1) * P])
                            for j, name in enumerate(("ffn_w_gate", "ffn_w_up"))]
            if GU_EV <= n < GU_EV + len(EV_LOADS):
                tiles = EV_LOADS[n - GU_EV]
                w = I["ev_w_in"][0].rearrange("(k p) c -> p k c", p=P)
                if tiles[1][0] == tiles[0][0] + P:
                    dst = slot.rearrange("p (k c) -> p k c", k=KT)
                    src = w[:, :, tiles[0][0]:tiles[0][0] + 256]
                    return [(dst[:, 4 * j:4 * j + 4, :], src[:, 4 * j:4 * j + 4, :]) for j in range(2)]
                return [(slot.rearrange("p (k c) -> p k c", k=KT)[:, :, 128 * j:128 * j + w_],
                         w[:, :, c0:c0 + w_]) for j, (c0, w_) in enumerate(tiles)]
            t = OD_TILES[2 * (n - GU_OD)]
            dst = slot.rearrange("p (k c) -> p k c", k=KT)
            src = I["od_w_in"][0].rearrange("(k p) c -> p k c", p=P)[:, :, t * P:t * P + 256]
            return [(dst[:, 4 * j:4 * j + 4, :], src[:, 4 * j:4 * j + 4, :]) for j in range(2)]

        def ffn_w(w, f):
            return w[f // 2, f % 2].rearrange("(k p) c -> p k c", p=P)

        def dn_source(n):
            for f in range(4):
                if DN_FFN[f] <= n < DN_FFN[f] + KT:
                    m = n - DN_FFN[f]
                    return (dn[:, n % 2, :].rearrange("p (k c) -> p k c", k=FT),
                            ffn_w(I["ffn_w_down"], f)[:, :, m * P:(m + 1) * P])
            w, m = (I["ev_w_out"], n - DN_EV) if n < DN_EV + 4 else (I["od_w_out"], n - DN_OD)
            return (dn[:, n % 2, 0:2048].rearrange("p (k c) -> p k c", k=KT),
                    w[0].rearrange("(k p) c -> p k c", p=P)[:, :, m * 256:(m + 1) * 256])

        def halves_before(f, c):
            return 2 * ((FT + KT) * f + c)

        def gu_free(n):
            for f in range(4):
                if GU_FFN[f] <= n < GU_FFN[f] + FT:
                    return lo_done, halves_before(f, n - GU_FFN[f] + 1)
            return gu_done, n + 1

        def dn_free(n):
            for f in range(4):
                if DN_FFN[f] <= n < DN_FFN[f] + KT:
                    return lo_done, halves_before(f, FT + n - DN_FFN[f] + 1)
            return dn_done, n + 1

        X_FFN = [0, 16, 24, 40]
        X_EV, X_OD = 8, 32
        NORM_FFN = [0, 2, 3, 5]
        NORM_EV, NORM_OD = 1, 4

        names = ("ev_evac kct_pe kct_evac kw_pe kw_evac idx_prep rawX rawX_used combX combX_used rawY rawY_used combY "
                 "combY_used dwi_ready qsq ksq qsum ksum qk_recip qk_rstd q_ready k_ready gate_pe gate_used g_neg "
                 "g_ln g_args g_exps bds_ready zero_q zero_bd ktr ktok_evac vtr vtok_evac ga_pe abd_ready vp_pe vp_evac "
                 "kl_pe kl_evac su_pe sg_ready go_pe go_evac gsq gsum grecip grstd sil_t ob_ready qk_pe l_done nmx "
                 "exps_done p_ready pt_pe pt_evac pv_pe pv_evac bias_out bias_in zero_qi")
        s = {k: sem("ev_" + k) for k in names.split()}
        names = ("evac ab_in ab_pe conv th silu zero_v masks g1 g2 g_rows col_pe cols_ready row_pe "
                 "row_used dexp sq sum recip rstd kq_ready kk_pe kk_used kt_evac vt_pe "
                 "vt_evac t1 u1_pe u1_evac bm y_pe y_evac t_pe u_pe t_upd u_upd cs_pe cs_evac rg_pe eg qe ks_pe r_ready "
                 "vn_pe vn_evac o_pe o_evac s_pe s_upd osq osum orecip orstd zt og states ds_in gexp")
        o = {k: sem("od_" + k) for k in names.split()}

        block = ctx.enter_context(nc.Block())

        @block.sync
        def _(sp):
            def load_gu(n):
                if n >= 2:
                    sp.wait_ge(*gu_free(n - 2))
                for dst, src in gu_source(n):
                    sp.dma_start(dst, src).then_inc(gu_loaded[n % 2], 16)

            def load_dn(n):
                if n >= 2:
                    sp.wait_ge(*dn_free(n - 2))
                dst, src = dn_source(n)
                sp.dma_start(dst, src).then_inc(dn_loaded[n % 2], 16)

            def ffn(f, following):
                wg, wu = ffn_w(I["ffn_w_gate"], f), ffn_w(I["ffn_w_up"], f)
                with sp.Fori(1, FT // 2) as i:
                    for slot in range(2):
                        sp.wait_ge(lo_done, halves_before(f, slot - 1) + 4 * i)
                        for j, w in enumerate((wg, wu)):
                            dst = gu[:, slot, j * 1024:(j + 1) * 1024].rearrange("p (k c) -> p k c", k=KT)
                            sp.dma_start(dst, w[:, :, bass.ds(256 * i + P * slot, P)]).then_inc(gu_loaded[slot], 16)
                load_dn(DN_FFN[f])
                load_dn(DN_FFN[f] + 1)
                if following is not None:
                    load_gu(following)
                    load_gu(following + 1)
                wd = ffn_w(I["ffn_w_down"], f)
                with sp.Fori(1, KT // 2) as i:
                    for slot in range(2):
                        sp.wait_ge(lo_done, halves_before(f, FT + slot - 1) + 4 * i)
                        sp.dma_start(dn[:, slot, :].rearrange("p (k c) -> p k c", k=FT),
                                     wd[:, :, bass.ds(256 * i + P * slot, P)]).then_inc(dn_loaded[slot], 16)

            sp.dma_start(xnat[:, 0:2, :], I["x_prompt"][0].rearrange("(i p) d -> p i d", p=P)).then_inc(x_in, 16)
            sp.dma_start(xnat[0:TS, 2, :], I["x_sample"][0]).then_inc(x_in, 16)
            load_gu(0)
            load_gu(1)
            sp.dma_start(kcn, I["cache_attn_k"][0, 0].rearrange("(t p) h d -> p t (h d)", p=P)).then_inc(caches_in, 16)
            sp.dma_start(vcache, I["cache_attn_v"][0, 0].rearrange("(t p) h d -> p t (h d)", p=P)).then_inc(caches_in, 16)
            sp.dma_start(ipn, I["cache_idx_k"][0, 0].rearrange("(t p) d -> p t d", p=P)).then_inc(caches_in, 16)
            sp.dma_start(Sg5,
                         I["state_gla"][0, 0].rearrange("(a b) d e -> a (b d) e", b=2).rearrange("a q e -> q a e")).then_inc(caches_in, 16)
            sp.dma_start(w2[0:B_RANK, :], I["ev_gate_w2"][0]).then_inc(caches_in, 16)
            ffn(0, GU_EV)
            for l in range(2, len(EV_LOADS)):
                load_gu(GU_EV + l)
            load_dn(DN_EV)
            load_dn(DN_EV + 1)
            load_gu(GU_FFN[1])
            load_gu(GU_FFN[1] + 1)
            load_dn(DN_EV + 2)
            load_dn(DN_EV + 3)
            ffn(1, GU_FFN[2])
            sp.wait_ge(x_upd, X_FFN[1] + 2)
            sp.wait_ge(out_sem, 16 * 8)
            sp.dma_start(wab, I["od_w_in"][0].rearrange("(k p) c -> p k c", p=P)[:, :, 4 * D:4 * D + 16])\
              .then_inc(o["ab_in"], 16)
            sp.dma_start(Sd[:, 1, :, :], I["state_delta"][0, 0].rearrange("h d e -> d h e")).then_inc(o["ds_in"], 16)
            ffn(2, GU_OD)
            for l in range(2, 16):
                load_gu(GU_OD + l)
            load_dn(DN_OD)
            load_dn(DN_OD + 1)
            load_gu(GU_FFN[3])
            load_gu(GU_FFN[3] + 1)
            load_dn(DN_OD + 2)
            load_dn(DN_OD + 3)
            ffn(3, None)

        @block.tensor
        def _(pe):
            mm, tr = pe.matmul, pe.transpose

            def prologue():
                pe.wait_ge(consts, 1)
                pe.wait_ge(x_in, 32)
                for i in range(3):
                    rows = P if i < 2 else TS
                    for half in range(2):
                        for k in range(4):
                            ins = tr(bank(2 * i + half)[:, k * P:k * P + rows],
                                     xnat[0:rows, i, (4 * half + k) * P:(4 * half + k + 1) * P], ident[0:rows, 0:rows])
                        ins.then_inc(pro_pe, 1)
                pe.wait_ge(params_in, 16 * 11)
                tr(bank(6)[:, 0:54], rs[0:54, 0:P], ident[0:54, 0:54])
                tr(bank(6)[:, 54:150], rs[0:96, P:2 * P], ident[0:96, 0:96])
                tr(bank(6)[:, 150:222], rs[0:72, 2 * P:3 * P], ident[0:72, 0:72]).then_inc(pro_pe, 1)

            def norm(r):
                if r == 0:
                    pe.wait_ge(pro_evac, 7)
                    for k in range(KT):
                        if k % 2 == 0:
                            pe.wait_ge(sq_done, k // 2 + 1)
                        ins = mm(bank(6, T), ones[:, :], squares[:, k, :], start=(k == 0), stop=(k == KT - 1))
                else:
                    pe.wait_ge(total_ready, r)
                    ins = mm(bank(6, T), ones[:, :], total, start=True, stop=True)
                ins.then_inc(norm_sum, 1)

            def block_product(out, slot, at, hi, lo, first, last):
                w_hi, w_lo = w_parts[:, slot, 0, at:at + P], w_parts[:, slot, 1, at:at + P]
                mm(out, w_hi, hi, start=first, stop=False)
                mm(out, w_hi, lo, start=False, stop=False)
                return mm(out, w_lo, hi, start=False, stop=last)

            def ffn(f):
                def gate_up(slot, c, i):
                    pe.wait_ge(act_done, FT * f + 1 + c + 2 * i)
                    for j, done in ((0, gu_half), (1, gu_done)):
                        pe.wait_ge(lo_done, halves_before(f, c) + 1 + j + 4 * i)
                        for k in range(KT):
                            if type(i) is int and c == 0 and j == 0:
                                pe.wait_ge(h_ready, KT * NORM_FFN[f] + k + 1)
                            ins = block_product(bank(2 * slot + j, T), slot, j * 1024 + k * P, h_hi[:, k, :],
                                                h_lo[:, k, :], k == 0, k == KT - 1)
                        ins.then_inc(done, 1)

                def down(slot, m, i):
                    pe.wait_ge(x_upd, X_FFN[f] + 1 + m + 2 * i)
                    for k in range(FT):
                        if k % (FT // 2) == 0:
                            pe.wait_ge(lo_done, halves_before(f, FT + m) + 1 + k // (FT // 2) + 4 * i)
                        if type(i) is int and m == 0 and k in (0, FT - 1):
                            pe.wait_ge(act_split, FT * (f + 1) + 2 - (k == 0))
                        ins = block_product(bank(4 + slot, T), slot, k * P, act_hi[:, k * T:(k + 1) * T],
                                            act_lo[:, k * T:(k + 1) * T], k == 0, k == FT - 1)
                    ins.then_inc(dn_done, 1)

                gate_up(0, 0, 0)
                norm(NORM_FFN[f])
                gate_up(1, 1, 0)
                with pe.Fori(1, FT // 2) as i:
                    gate_up(0, 0, i)
                    gate_up(1, 1, i)
                down(0, 0, 0)
                down(1, 1, 0)
                with pe.Fori(1, KT // 2) as i:
                    down(0, 0, i)
                    down(1, 1, i)

            def project_out(base_dn, base_x):
                for m in range(KT):
                    n = base_dn + m // 2
                    if m % 2 == 0:
                        pe.wait_ge(dn_loaded[n % 2], 16 * (n // 2 + 1))
                    pe.wait_ge(x_upd, base_x + 1 + m)
                    for k in range(KT):
                        ins = mm(bank(4 + m % 2, T), dn[:, n % 2, k * 256 + (m % 2) * P:k * 256 + (m % 2) * P + P],
                                 oT[:, k, :], start=(k == 0), stop=(k == KT - 1))
                    ins.then_inc((dn_half, dn_done)[m % 2], 1)

            def project_in(n, t, widths, evac):
                pe.wait_ge(gu_loaded[n % 2], 32 * (n // 2 + 1))
                for j in range(2):
                    if t + j >= 4:
                        pe.wait_ge(evac, t + j - 3)
                    for k in range(KT):
                        ins = mm(bank((t + j) % 4, T)[0:widths[j], :],
                                 gu[:, n % 2, k * 256 + j * P:k * 256 + j * P + widths[j]], hT[:, k, :],
                                 start=(k == 0), stop=(k == KT - 1))
                    ins.then_inc((gu_half, gu_done)[j], 1)

            def even():
                pe.wait_ge(x_upd, X_EV + 2)
                pe.wait_ge(caches_in, 16 * 5)
                for p in range(A_PAIRS):
                    for kt in range(4):
                        ins = tr(bank(p)[:, kt * P:(kt + 1) * P], kcn[:, kt, p * P:(p + 1) * P], ident[:, :])
                    ins.then_inc(s["kct_pe"], 1)
                for kt in range(4):
                    ins = tr(bank(7)[0:IDX_D, kt * P:(kt + 1) * P], ipn[:, kt, :], ident[:, :])
                ins.then_inc(s["kct_pe"], 1)
                norm(NORM_EV)
                pe.wait_ge(h_ready, KT * (NORM_EV + 1))
                pe.wait_ge(s["kct_evac"], 5)
                for l, tiles in enumerate(EV_LOADS):
                    project_in(GU_EV + l, 2 * l, [w for _, w in tiles], s["ev_evac"])
                    if l == 2:
                        key_token_rows()
                    if l == 4:
                        raw_scores_x()
                    if l == 5:
                        combine_x()
                    if l == 6:
                        raw_scores_y()
                    if l == 7:
                        combine_y()
                    if l == 8:
                        head_sums(s["qsq"], s["combY_used"], 1, s["qsum"])
                    if l == 9:
                        head_sums(s["ksq"], s["qk_recip"], 1, s["ksum"])
                    if l == 10:
                        gate()
                token_rows()
                gla()
                attention()
                pe.wait_ge(s["ob_ready"], 4)
                pe.wait_ge(s["pv_evac"], 5)
                project_out(DN_EV, X_EV)

            def key_token_rows():
                pe.wait_ge(s["ev_evac"], T_KI + 1)
                for i in range(3):
                    rows = P if i < 2 else TS
                    ins = tr(bank(7)[0:rows, i * 68:(i + 1) * 68], pr[0:68, T_KI, i * P:i * P + rows], ident[0:68, 0:68])
                ins.then_inc(s["kw_pe"], 1)

            def raw_scores_x():
                pe.wait_ge(s["idx_prep"], 1)
                for b, bk in ((3, 4), (2, 5)):
                    for p in range(IDX_PAIRS):
                        ins = mm(bank(bk)[:, p * 256:p * 256 + CH * (b + 1)], qibd[:, b, p, :], kiT[:, 0:CH * (b + 1)],
                                 start=True, stop=True)
                ins.then_inc(s["rawX"], 1)

            def weigh(b, out, rrow, done=None):
                for p in range(IDX_PAIRS):
                    ins = mm(out, dwi[:, 2 * b + p, :], rrow(p), start=(p == 0), stop=(p == 1))
                if done is not None:
                    ins.then_inc(done, 1)

            def combine_x():
                pe.wait_ge(s["rawX_used"], 1)
                pe.wait_ge(s["dwi_ready"], 1)
                weigh(3, bank(7)[CH:P, 0:256], lambda p: rX3[:, p, :])
                weigh(2, bank(7)[0:CH, 0:192], lambda p: rX2[:, p, :], s["combX"])

            def raw_scores_y():
                for p in range(IDX_PAIRS):
                    mm(bank(4)[:, p * 128:(p + 1) * 128], qibd[:, 1, p, :], kiT[:, 0:128], start=True, stop=True)
                    mm(bank(5 + p), qibd[:, 4, p, :], kiT[:, TP:TP + 512], start=True, stop=True)
                    ins = mm(bank(4)[:, 256 + 64 * p:320 + 64 * p], qibd[:, 4, p, :], kiT[:, TP + 512:TP + NK_S],
                             start=True, stop=True)
                ins.then_inc(s["rawY"], 1)

            def combine_y():
                pe.wait_ge(s["rawY_used"], 1)
                pe.wait_ge(s["combX_used"], 1)
                weigh(4, bank(7)[CH:P, :], lambda p: rYS[:, p, 0:512])
                weigh(4, bank(4)[CH:P, 0:64], lambda p: rYS[:, p, 512:NK_S])
                weigh(1, bank(4)[0:CH, 128:256], lambda p: rY1[:, p, :], s["combY"])

            def head_sums(squared, free, n_free, done):
                pe.wait_ge(free, n_free)
                for p in range(4):
                    pe.wait_ge(squared, p + 1)
                    ins = mm(bank(4 + p, T), halves[:, :], sqE[:, p, :], start=True, stop=True)
                ins.then_inc(done, 1)

            def gate():
                pe.wait_ge(s["qk_recip"], 2)
                for j in range(2):
                    ins = mm(bank(4 + j, T), w2[0:B_RANK, j * P:(j + 1) * P], pr[0:B_RANK, T_AB, :], start=True, stop=True)
                ins.then_inc(s["gate_pe"], 1)

            def token_rows():
                pe.wait_ge(s["ev_evac"], N_EV)
                pe.wait_ge(s["k_ready"], 4)
                pe.wait_ge(s["gate_used"], 1)
                for name, first, src, done in (("v", 0, T_V, s["vtr"]), ("k", 4, T_K, s["ktr"])):
                    for i in range(3):
                        rows = P if i < 2 else TS
                        for p in range(4):
                            ins = tr(bank(first + i)[0:rows, p * P:(p + 1) * P], pr[:, src + p, i * P:i * P + rows],
                                     ident[:, :])
                        ins.then_inc(done, 1)

            def gla():
                pe.wait_ge(s["q_ready"], 8)
                pe.wait_ge(s["vtok_evac"], 3)
                for u in range(10):
                    p, c = divmod(u, NCH)
                    ins = tr(PS[:, u * P:(u + 1) * P], vbx[:, p, c, :],
                             ident[:, :])
                ins.then_inc(s["vp_pe"], 1)
                pe.wait_ge(s["bds_ready"], 1)
                pe.wait_ge(s["ktok_evac"], 3)
                for u in range(10):
                    ins = tr(PS[:, 1536 + u * P:1536 + (u + 1) * P], kl_bd[:, u // NCH, u % NCH, :], ident[:, :])
                ins.then_inc(s["kl_pe"], 1)
                for u in range(10):
                    p, c = divmod(u, NCH)
                    ins = mm(PS[:, 3072 + u * CH:3072 + (u + 1) * CH], km_bd[:, p, c, :], qm[:, p, c * CH:(c + 1) * CH],
                             start=True, stop=True)
                ins.then_inc(s["ga_pe"], 1)
                pe.wait_ge(s["vp_evac"], 1)
                pe.wait_ge(s["kl_evac"], 1)
                for u in range(10):
                    ins = mm(PS[:, u * P:(u + 1) * P], kl_bd[:, u // NCH, u % NCH, :], vp[:, u, :], start=True, stop=True)
                ins.then_inc(s["su_pe"], 1)
                pe.wait_ge(s["abd_ready"], 1)
                pe.wait_ge(s["sg_ready"], 1)
                for u in range(10):
                    p, c = divmod(u, NCH)
                    mm(PS[:, 1536 + u * P:1536 + (u + 1) * P], vp[:, u, :], km_bd[:, p, c, :], start=True, stop=False)
                    ins = mm(PS[:, 1536 + u * P:1536 + (u + 1) * P], Sg(c if c < 4 else 5)[:, p, :], qe_bd[:, p, c, :],
                             start=False, stop=True)
                ins.then_inc(s["go_pe"], 1)
                pe.wait_ge(s["gsq"], 1)
                for h in range(4):
                    ins = mm(bank(h, T), ones[:, :], sqE[:, h, :], start=True, stop=True)
                ins.then_inc(s["gsum"], 1)

            def attention():
                QK0 = [0, 2, 0, 2, 0]
                PTB = [[4], [5], [4, 5], [4, 5], [5, 6, 7, 0, 1]]
                PVB = [6, 7, 6, 7, 2]

                def scores(b):
                    if b == 0:
                        pe.wait_ge(s["grecip"], 1)
                        pe.wait_ge(s["go_evac"], 2)
                    if b >= 2 and b < 4:
                        pe.wait_ge(s["l_done"], b - 1)
                    if b == 4:
                        pe.wait_ge(s["l_done"], 4)
                        pe.wait_ge(s["pt_evac"], 4)
                    for p in range(A_PAIRS):
                        if b < 4:
                            nk = CH * (b + 1)
                            ins = mm(PS[:, QK0[b] * 512 + p * 256:QK0[b] * 512 + p * 256 + nk], qbd[:, b, p, :],
                                     pr[:, T_K + p, 0:nk], start=True, stop=True)
                        else:
                            mm(bank(p), qbd[:, b, p, :], kcT[:, p, :], start=True, stop=True)
                            ins = mm(bank(4)[:, p * 64:(p + 1) * 64], qbd[:, b, p, :], pr[:, T_K + p, TP:T],
                                     start=True, stop=True)
                    ins.then_inc(s["qk_pe"], 1)

                def turn(b):
                    pe.wait_ge(s["p_ready"], b + 1)
                    if b in (2, 3):
                        pe.wait_ge(s["pt_evac"], b)
                    if b == 4:
                        pe.wait_ge(s["pv_evac"], 4)
                    nk = CH * (b + 1) if b < 4 else NK_S
                    for kt, bk in enumerate(PTB[b]):
                        w = min(P, nk - kt * P)
                        for p in range(A_PAIRS):
                            ins = tr(bank(bk)[0:w, p * P:(p + 1) * P], logit(b)[:, p, kt * P:kt * P + w], ident[:, :])
                    ins.then_inc(s["pt_pe"], 1)

                def values(b):
                    pe.wait_ge(s["pt_evac"], b + 1)
                    if b in (2, 3):
                        pe.wait_ge(s["pv_evac"], b - 1)
                    nk = CH * (b + 1) if b < 4 else NK_S
                    kts = range((nk + P - 1) // P)
                    for p in range(A_PAIRS):
                        for kt in kts:
                            w = min(P, nk - kt * P)
                            if b < 4:
                                v = vtok[0:w, kt, p * P:(p + 1) * P]
                            else:
                                v = vcache[:, kt, p * P:(p + 1) * P] if kt < 4 else vtok[0:w, 2, p * P:(p + 1) * P]
                            ins = mm(bank(PVB[b])[:, p * P:(p + 1) * P], v, pT[0:w, pt_slot(b) + kt, p * P:(p + 1) * P],
                                     start=(kt == 0), stop=(kt == kts[-1]))
                    ins.then_inc(s["pv_pe"], 1)

                scores(0)
                scores(1)
                turn(0)
                scores(2)
                values(0)
                turn(1)
                scores(3)
                values(1)
                turn(2)
                values(2)
                turn(3)
                values(3)
                scores(4)
                turn(4)
                values(4)

            def odd():
                pe.wait_ge(h_ready, KT * (NORM_OD + 1))
                pe.wait_ge(o["ab_in"], 16)
                for j in range(2):
                    for k in range(KT):
                        ins = mm(bank(4 + j, T)[0:C_H, :], wab[:, k, 8 * j:8 * j + 8], hT[:, k, :],
                                 start=(k == 0), stop=(k == KT - 1))
                ins.then_inc(o["ab_pe"], 1)
                for l in range(16):
                    project_in(GU_OD + l, 2 * l, [P, P], o["evac"])
                    if l == 1:
                        gate_columns()
                    if l == 2:
                        gate_rows(0)
                    if l == 3:
                        gate_rows(1)
                    if l in (5, 6, 8, 9):
                        key_sums((5, 6, 8, 9).index(l))
                    if l == 12:
                        key_products()
                    if l == 14:
                        first_inverse()
                for level in range(5):
                    double_inverse(level)
                state_rows()
                recurrence()
                out_sums()
                pe.wait_ge(o["og"], 1)
                project_out(DN_OD, X_OD)

            def gate_columns():
                pe.wait_ge(o["g_rows"], 1)
                for w in range(2):
                    for c in range(NCH):
                        at = (w * NCH + c) * 8
                        ins = tr(bank(6)[0:CH, at:at + 8], growv(2 + w)[0:C_H, c * CH:(c + 1) * CH], ident[0:C_H, 0:C_H])
                ins.then_inc(o["col_pe"], 1)

            def gate_rows(half):
                if half == 0:
                    pe.wait_ge(o["cols_ready"], 1)
                else:
                    pe.wait_ge(o["row_used"], 1)
                for h in range(4):
                    ins = mm(bank(4 + h, T), ident[0:C_H, 4 * half + h:4 * half + h + 1].to_broadcast([C_H, P]),
                             growv(2)[0:C_H, :], start=True, stop=True)
                ins.then_inc(o["row_pe"], 1)

            def key_sums(g):
                if g == 0:
                    pe.wait_ge(o["row_used"], 2)
                else:
                    pe.wait_ge(o["recip"], g)
                pe.wait_ge(o["sq"], g + 1)
                for h in range(4):
                    ins = mm(bank(4 + h, T), ones[:, :], sq4[:, h * T:(h + 1) * T], start=True, stop=True)
                ins.then_inc(o["sum"], 1)

            def kview(p, c):
                return cv[:, 1, p, c, :]

            def qview(p, c):
                return cv[:, 0, p, c, :]

            def key_products():
                pe.wait_ge(o["kq_ready"], 4)
                for c in range(NCH):
                    if c:
                        pe.wait_ge(o["kk_used"], 2 * c)
                        pe.wait_ge(o["kt_evac"], c)
                    for p in range(C_PAIRS):
                        mm(bank(4)[:, p * P:(p + 1) * P], kview(p, c), kview(p, c), start=True, stop=True)
                        mm(bank(5)[:, p * P:(p + 1) * P], kview(p, c), qview(p, c), start=True, stop=True)
                        ins = tr(bank(6)[:, p * P:(p + 1) * P], kview(p, c), ident[:, :])
                    ins.then_inc(o["kk_pe"], 1)

            def first_inverse():
                for c in range(NCH):
                    pe.wait_ge(o["t1"], c + 1)
                    if c == 0:
                        pe.wait_ge(o["kt_evac"], NCH)
                    else:
                        pe.wait_ge(o["u1_evac"], c)
                    for p in range(C_PAIRS):
                        ins = tr(bank(7)[:, p * P:(p + 1) * P], tT[:, c, p, :], ident[:, :])
                    ins.then_inc(o["u1_pe"], 1)

            def double_inverse(level):
                def y(c):
                    m = level * NCH + c
                    pe.wait_ge(o["bm"], m + 1)
                    if m >= 2:
                        pe.wait_ge(o["y_evac"], m - 1)
                    if level:
                        pe.wait_ge(o["u_upd"], m - NCH + 1)
                    for p in range(C_PAIRS):
                        ins = mm(bank(4 + m % 2)[:, p * P:(p + 1) * P], Dm[:, c, p, :], uT[:, c, p, :], start=True, stop=True)
                    ins.then_inc(o["y_pe"], 1)

                def tu(c):
                    m = level * NCH + c
                    pe.wait_ge(o["y_evac"], m + 1)
                    if level:
                        pe.wait_ge(o["t_upd"], m - NCH + 1)
                    if level < 4:
                        if m:
                            pe.wait_ge(o["t_upd"], m)
                        for p in range(C_PAIRS):
                            ins = mm(bank(6)[:, p * P:(p + 1) * P], yT[:, c, p, :], tT[:, c, p, :], start=True, stop=True)
                        ins.then_inc(o["t_pe"], 1)
                    if m:
                        pe.wait_ge(o["u_upd"], m)
                    for p in range(C_PAIRS):
                        ins = mm(bank(7)[:, p * P:(p + 1) * P], tT[:, c, p, :], yT[:, c, p, :], start=True, stop=True)
                    ins.then_inc(o["u_pe"], 1)

                if level == 0:
                    pe.wait_ge(o["u1_evac"], NCH)
                y(0)
                y(1)
                for c in range(NCH):
                    tu(c)
                    if c + 2 < NCH:
                        y(c + 2)

            def state_rows():
                pe.wait_ge(o["evac"], N_OD)
                pe.wait_ge(o["silu"], 24)
                for c in range(NCH):
                    if c >= 2:
                        pe.wait_ge(o["vt_evac"], c - 1)
                    for p in range(C_PAIRS):
                        ins = tr(bank(c % 2)[:, p * P:(p + 1) * P],
                                 cv[:, 2, p, c, :], ident[:, :])
                    ins.then_inc(o["vt_pe"], 1)
                pe.wait_ge(o["vt_evac"], NCH)
                pe.wait_ge(o["u_upd"], 5 * NCH)
                for t in range(24):
                    ins = tr(PS[0:6, t * P:(t + 1) * P], cst[:, t, :], ident[:, :])
                ins.then_inc(o["cs_pe"], 1)
                pe.wait_ge(o["cs_evac"], 1)
                for h in range(C_H):
                    ins = mm(bank(h, T), ident[0:C_H, h:h + 1].to_broadcast([C_H, P]), growv(2)[0:C_H, :],
                             start=True, stop=True)
                ins.then_inc(o["rg_pe"], 1)

            def recurrence():
                pe.wait_ge(o["qe"], C_PAIRS)
                pe.wait_ge(o["zero_v"], 1)
                pe.wait_ge(o["states"], 1)
                pe.wait_ge(o["ds_in"], 16)
                for n_, c in enumerate((0, 4, 1, 2, 3)):
                    S = Sd[:, 1 if c == 4 else 0, :, :]
                    if n_:
                        pe.wait_ge(o["r_ready"], n_)
                    if n_ > 1:
                        pe.wait_ge(o["s_upd"], n_ if n_ > 2 else 1)
                    for p in range(C_PAIRS):
                        for par in range(2):
                            ins = mm(bank(0)[par * CH:(par + 1) * CH, p * P:(p + 1) * P],
                                     cv[:, 1, p, c, par * CH:(par + 1) * CH], S[:, 2 * p + par, :],
                                     start=True, stop=True)
                    ins.then_inc(o["ks_pe"], 1)
                    pe.wait_ge(o["r_ready"], n_ + 1)
                    if n_:
                        pe.wait_ge(o["vn_evac"], n_)
                    for p in range(C_PAIRS):
                        ins = mm(bank(1)[:, p * P:(p + 1) * P], uT[:, c, p, :], Rr[:, p, :], start=True, stop=True)
                    ins.then_inc(o["vn_pe"], 1)
                    pe.wait_ge(o["vn_evac"], n_ + 1)
                    if n_:
                        pe.wait_ge(o["o_evac"], n_)
                    for p in range(C_PAIRS):
                        for par in range(2):
                            out = bank(2)[:, p * P + par * CH:p * P + (par + 1) * CH]
                            mm(out, S[:, 2 * p + par, :], cv[:, 0, p, c, par * CH:(par + 1) * CH],
                               start=True, stop=False)
                            ins = mm(out, vnew[:, p, par, :], At[:, c, p, par * CH:(par + 1) * CH],
                                     start=False, stop=True)
                    ins.then_inc(o["o_pe"], 1)
                    if n_:
                        pe.wait_ge(o["s_upd"], n_)
                    for p in range(C_PAIRS):
                        ins = mm(bank(3 + p // 2)[:, (p % 2) * 256:(p % 2) * 256 + 256], Kl[:, c, p, :],
                                 vnew[:, p, :, :], start=True, stop=True)
                    ins.then_inc(o["s_pe"], 1)

            def out_sums():
                pe.wait_ge(o["osq"], 1)
                pe.wait_ge(o["s_upd"], NCH)
                pe.wait_ge(o["o_evac"], NCH)
                for h in range(C_H):
                    ins = mm(bank(h, T), ones[:, :], sqO[:, h, :], start=True, stop=True)
                ins.then_inc(o["osum"], 1)

            def epilogue():
                pe.wait_ge(x_upd, X_FFN[3] + 2 + KT)
                for i in range(3):
                    rows = P if i < 2 else TS
                    for half in range(2):
                        for k in range(4):
                            ins = tr(bank(2 * i + half)[0:rows, k * P:(k + 1) * P],
                                     xT[:, 4 * half + k, i * P:i * P + rows], ident[:, :])
                        ins.then_inc(pro_pe, 1)

            prologue()
            ffn(0)
            even()
            ffn(1)
            ffn(2)
            norm(NORM_OD)
            odd()
            ffn(3)
            epilogue()

        @block.scalar
        def _(sc):
            act_ = sc.activation
            steps = [0]

            def link(ins):
                steps[0] += 1
                ins.then_inc(act_step, 1)
                sc.wait_ge(act_step, steps[0])

            def copy(out, in_, scale=1.0):
                return act_(out, in_, ACT.Copy, scale=scale)

            def prologue():
                rows = [(0, 32, 0, I["ffn_norm"].rearrange("a b (k p) -> (a b k) p", p=P)),
                        (32, 48, 0, I["mix_norm"].rearrange("a (k p) -> (a k) p", p=P)),
                        (48, 49, 0, I["ev_gla_norm"]), (49, 50, 0, I["od_norm"]),
                        (50, 52, 0, I["ev_gate_b2"].rearrange("a (k p) -> (a k) p", p=P)),
                        (0, 96, P, I["od_conv_w"][0].rearrange("j (k p) -> (j k) p", p=P)),
                        (0, 72, 2 * P, I["state_conv"][0, 0].rearrange("j (k p) -> (j k) p", p=P))]
                for r0, r1, at, src in rows:
                    sc.dma_start(rs[r0:r1, at:at + P], src).then_inc(params_in, 16)
                for row, name in ((C_QN, "ev_q_norm"), (C_KN, "ev_k_norm")):
                    for par in range(2):
                        sc.dma_start(rs[row:row + 1, par * A_D:(par + 1) * A_D], I[name]).then_inc(params_in, 16)
                sc.dma_start(rbT[0:A_H, :], I["rel_bias"].rearrange("b h -> h b"),
                             allow_slow_non_contiguous=True).then_inc(small_in, 16)
                sc.dma_start(cols[0:C_H, 222:223], I["od_a_log"].rearrange("a h -> h a")).then_inc(small_in, 16)
                sc.dma_start(cols[0:C_H, 223:224], I["od_dt_bias"].rearrange("a h -> h a")).then_inc(small_in, 16)
                for i in range(3):
                    n_ = P if i < 2 else TS
                    for half in range(2):
                        sc.wait_ge(pro_pe, 2 * i + half + 1)
                        copy(xT[:, 4 * half:4 * half + 4, i * P:i * P + n_],
                             bank(2 * i + half).rearrange("p (k c) -> p k c", k=4)[:, :, 0:n_]).then_inc(pro_evac, 1)
                sc.wait_ge(pro_pe, 7)
                copy(cols[:, 0:222], bank(6, 222)).then_inc(pro_evac, 1)

            def root(r):
                sc.wait_ge(norm_recip, r + 1)
                act_(rstd, rstd, ACT.Sqrt).then_inc(norm_rstd, 1)

            def split_gate_up(f, slot, c, i):
                n = GU_FFN[f] + c
                sc.wait_ge(gu_loaded[slot], 32 * (n // 2) + 32 + 32 * i)
                if type(i) is not int or c >= 2:
                    sc.wait_ge(gu_done, n - 1 + 2 * i)
                elif f == 2:
                    sc.wait_ge(dn_done, DN_FFN[1] + KT - 1 + c)
                elif f:
                    if f == 1:
                        sc.wait_ge(s["pv_evac"], NCH)
                        sc.wait_ge(s["ob_ready"], 4)
                        sc.wait_ge(out_sem, 16 * 8)
                    else:
                        sc.wait_ge(o["og"], 1)
                        sc.wait_ge(out_sem, 16 * 12)
                for j in range(2):
                    copy(w_parts[:, slot, 0, j * 1024:(j + 1) * 1024], gu[:, slot, j * 1024:(j + 1) * 1024])\
                        .then_inc(hi_done, 1)

            def split_down(f, slot, m, i):
                n = DN_FFN[f] + m
                sc.wait_ge(dn_loaded[slot], 16 * (n // 2) + 16 + 16 * i)
                if type(i) is not int or m >= 2:
                    sc.wait_ge(dn_done, n - 1 + 2 * i)
                else:
                    sc.wait_ge(gu_done, GU_FFN[f] + FT - 1 + m)
                for j in range(2):
                    w = slice(j * FT * P // 2, (j + 1) * FT * P // 2)
                    copy(w_parts[:, slot, 0, w], dn[:, slot, w]).then_inc(hi_done, 1)

            def ffn(f, gain, x_base):
                def tanh(slot, c, i):
                    sc.wait_ge(scaled, FT * f + 1 + c + 2 * i)
                    act_(tanh_g[:, slot, :], gated[:, slot, :], ACT.Tanh, scale=0.5).then_inc(tanh_done, 1)

                if f == 0:
                    sc.wait_ge(pro_evac, 7)
                    for j in range(4):
                        act_(squares[:, 2 * j:2 * j + 2, :], xT[:, 2 * j:2 * j + 2, :], ACT.Square).then_inc(sq_done, 1)
                sc.wait_ge(x_upd, x_base + 2)
                for k in range(KT):
                    copy(h_hi[:, k, :], xT[:, k, :], cols[:, gain + k:gain + k + 1]).then_inc(h_hi_done, 1)
                split_gate_up(f, 1, 1, 0)
                root(NORM_FFN[f])
                tanh(0, 0, 0)
                with sc.Fori(0, FT // 2 - 1) as i:
                    split_gate_up(f, 0, 2, i)
                    tanh(1, 1, i)
                    split_gate_up(f, 1, 3, i)
                    tanh(0, 2, i)
                split_down(f, 0, 0, 0)
                tanh(1, FT - 1, 0)
                split_down(f, 1, 1, 0)
                with sc.Fori(1, KT // 2) as i:
                    split_down(f, 0, 0, i)
                    split_down(f, 1, 1, i)
                if f == 1:
                    split_gate_up(2, 0, 0, 0)

            def even():
                for p in range(A_PAIRS):
                    sc.wait_ge(s["kct_pe"], p + 1)
                    copy(kcT[:, p, :], bank(p)).then_inc(s["kct_evac"], 1)
                sc.wait_ge(s["kct_pe"], 5)
                copy(kiT[0:IDX_D, TP:TP + PAST], bank(7)[0:IDX_D, :])
                copy(kiT[IDX_D:P, TP:TP + PAST], bank(7)[0:IDX_D, :]).then_inc(s["kct_evac"], 1)
                root(NORM_EV)
                for l, tiles in enumerate(EV_LOADS):
                    for j, done in ((0, gu_half), (1, gu_done)):
                        t, w = 2 * l + j, tiles[j][1]
                        sc.wait_ge(done, GU_EV + l + 1)
                        if T_VB <= t < T_VB + 4:
                            dst = vbx[:, (t - T_VB) // 2, :, (t % 2) * CH:(t % 2 + 1) * CH]
                            copy(dst, bank(t % 4, T).rearrange("p (c t) -> p c t", t=CH)).then_inc(s["ev_evac"], 1)
                        else:
                            copy(pr[0:w, t, :], bank(t % 4, T)[0:w, :]).then_inc(s["ev_evac"], 1)
                    if l == 4:
                        sc.wait_ge(s["rawX"], 1)
                        act_(rX3, bank(4).rearrange("p (a c) -> p a c", a=2), ACT.Relu)
                        act_(rX2, bank(5).rearrange("p (a c) -> p a c", a=2)[:, :, 0:192], ACT.Relu)\
                            .then_inc(s["rawX_used"], 1)
                    if l == 5:
                        for p in range(4):
                            sc.wait_ge(s["ev_evac"], T_Q + p + 1)
                            act_(sqE[:, p, :], pr[:, T_Q + p, :], ACT.Square).then_inc(s["qsq"], 1)
                    if l == 6:
                        sc.wait_ge(s["rawY"], 1)
                        for p in range(IDX_PAIRS):
                            act_(rYS[:, p, 0:512], bank(5 + p), ACT.Relu)
                            act_(rYS[:, p, 512:NK_S], bank(4)[:, 256 + 64 * p:320 + 64 * p], ACT.Relu)
                        act_(rY1, bank(4, 256).rearrange("p (a c) -> p a c", a=2), ACT.Relu).then_inc(s["rawY_used"], 1)
                    if l == 9:
                        sc.wait_ge(s["qsum"], 1)
                        for p in range(4):
                            act_(sqE[:, p, :], pr[:, T_K + p, :], ACT.Square).then_inc(s["ksq"], 1)
                        sc.wait_ge(s["qk_recip"], 1)
                        act_(rs[:, 0:4 * T], rs[:, 0:4 * T], ACT.Sqrt).then_inc(s["qk_rstd"], 1)
                    if l == 11:
                        sc.wait_ge(s["qk_recip"], 2)
                        act_(rs[:, 0:4 * T], rs[:, 0:4 * T], ACT.Sqrt).then_inc(s["qk_rstd"], 1)
                sc.wait_ge(s["g_neg"], 1)
                link(act_(gx2, gx2, ACT.Exp))
                act_(gx2, gx2, ACT.Ln, bias=1.0).then_inc(s["g_ln"], 1)
                for name, dst, first in (("v", vtok, 0), ("k", ktok, 4)):
                    for i in range(3):
                        n_ = P if i < 2 else TS
                        sc.wait_ge(s[name + "tr"], i + 1)
                        copy(dst[0:n_, i, :], bank(first + i)[0:n_, :]).then_inc(s[name + "tok_evac"], 1)
                sc.wait_ge(s["g_args"], 1)
                k_ = 1.0 / B_TAU
                act_(e_b, gB, ACT.Exp, scale=k_)
                act_(es, gB.rearrange("p a (c t) -> p a c t", t=CH)[:, :, :, CH - 1], ACT.Exp, scale=k_)
                act_(e_mid_n, gdm, ACT.Exp, scale=-k_)
                act_(gdm, gdm, ACT.Exp, scale=k_)
                act_(gdl, gdl, ACT.Exp, scale=k_).then_inc(s["g_exps"], 1)
                sc.wait_ge(s["vp_pe"], 1)
                copy(vp, PS[:, 0:1280].rearrange("p (u e) -> p u e", e=P)).then_inc(s["vp_evac"], 1)
                sc.wait_ge(s["kl_pe"], 1)
                copy(kl_bd, PS[:, 1536:2816].rearrange("p (a c e) -> p a c e", a=2, e=P)).then_inc(s["kl_evac"], 1)
                sc.wait_ge(s["go_pe"], 1)
                for p in range(B_PAIRS):
                    copy(oT[:, 4 + 2 * p:6 + 2 * p, :].rearrange("p a (c t) -> p c a t", t=CH),
                         PS[:, 1536 + 640 * p:2176 + 640 * p].rearrange("p (c a t) -> p c a t", a=2, t=CH))\
                        .then_inc(s["go_evac"], 1)
                sc.wait_ge(s["go_evac"], 2)
                act_(sqE, oT[:, 4:8, :], ACT.Square).then_inc(s["gsq"], 1)
                act_(kl_bd.rearrange("p a c e -> p (a c e)"), pr[:, T_RB:T_RB + 4, :].rearrange("p a b -> p (a b)"),
                     ACT.Tanh, scale=0.5).then_inc(s["sil_t"], 1)
                sc.wait_ge(s["grecip"], 1)
                act_(rs[:, 0:4 * T], rs[:, 0:4 * T], ACT.Sqrt).then_inc(s["grstd"], 1)

                def exps(b):
                    sc.wait_ge(s["nmx"], b + 1)
                    for p in range(A_PAIRS):
                        ins = act_(logit(b)[:, p, :], logit(b)[:, p, :], ACT.Exp, bias=mx[:, b, 1, p:p + 1],
                                   accum_out=mx[:, b, 2, p:p + 1])
                    ins.then_inc(s["exps_done"], 1)

                def turned(b):
                    sc.wait_ge(s["pt_pe"], b + 1)
                    if b >= 2:
                        sc.wait_ge(s["pv_pe"], b - 1 if b < 4 else 4)
                    nk = CH * (b + 1) if b < 4 else NK_S
                    for kt, bk in enumerate([[4], [5], [4, 5], [4, 5], [5, 6, 7, 0, 1]][b]):
                        w = min(P, nk - kt * P)
                        ins = copy(pT[0:w, pt_slot(b) + kt, :], bank(bk)[0:w, :])
                    ins.then_inc(s["pt_evac"], 1)

                exps(0)
                exps(1)
                sc.wait_ge(s["ob_ready"], 4)
                turned(0)
                exps(2)
                turned(1)
                exps(3)
                turned(2)
                turned(3)
                exps(4)
                turned(4)

            def odd():
                def tile_out(t):
                    done = (gu_half, gu_done)[t % 2]
                    sc.wait_ge(done, GU_OD + t // 2 + 1)
                    if t < 24:
                        if t >= 4:
                            sc.wait_ge(o["conv"], t - 3)
                        copy(qp[:, t % 4, 3:259], bank(t % 4, TP))
                        copy(qp[:, t % 4, 262:326], bank(t % 4)[:, TP:T]).then_inc(o["evac"], 1)
                    else:
                        copy(zT[:, t - 24, :], bank(t % 4, T)).then_inc(o["evac"], 1)

                def silu_tanh(t):
                    sc.wait_ge(o["conv"], t + 1)
                    if t >= 2:
                        sc.wait_ge(o["silu"], t - 1)
                    act_(th2[:, t % 2, :], cring[:, t % 4, :], ACT.Tanh, scale=0.5).then_inc(o["th"], 1)

                def square(g):
                    sc.wait_ge(o["silu"], 4 * g + 4)
                    if g:
                        sc.wait_ge(o["sum"], g)
                    act_(sq4, group(g), ACT.Square).then_inc(o["sq"], 1)

                def root(g):
                    sc.wait_ge(o["recip"], g + 1)
                    act_(rs[:, 0:4 * T], rs[:, 0:4 * T], ACT.Sqrt).then_inc(o["rstd"], 1)

                sc.wait_ge(small_in, 48)
                act_(cols[0:C_H, 224:225], cols[0:C_H, 222:223], ACT.Exp)
                sc.wait_ge(o["g1"], 1)
                act_(growv(3)[0:C_H, :], growv(3)[0:C_H, :], ACT.Exp)
                link(act_(growv(1)[0:C_H, :], growv(1)[0:C_H, :], ACT.Exp))
                act_(growv(1)[0:C_H, :], growv(1)[0:C_H, :], ACT.Ln, bias=1.0).then_inc(o["g2"], 1)
                for t in range(N_OD):
                    tile_out(t)
                    if t and t <= 24:
                        silu_tanh(t - 1)
                    if t == 3:
                        sc.wait_ge(o["cols_ready"], 1)
                        act_(egc, colG[:, 0, :, :], ACT.Exp).then_inc(o["gexp"], 1)
                    if t == 9:
                        sc.wait_ge(o["row_used"], 2)
                        act_(es8, gl, ACT.Exp)
                        act_(klc, klc, ACT.Exp)
                        act_(Dm, Dm, ACT.Exp, scale=-1.0)
                        act_(At, At, ACT.Exp).then_inc(o["dexp"], 1)
                    if t == 11:
                        square(0)
                    if t == 13:
                        root(0)
                        square(1)
                    if t == 15:
                        root(1)
                    if t == 17:
                        square(2)
                    if t == 19:
                        root(2)
                        square(3)
                    if t == 21:
                        root(3)
                    if t == 25:
                        for c in range(NCH):
                            sc.wait_ge(o["kk_pe"], c + 1)
                            for p in range(C_PAIRS):
                                ins = copy(Kl[:, c, p, :], bank(6)[:, p * P:(p + 1) * P], klc[:, c, p:p + 1])
                            ins.then_inc(o["kt_evac"], 1)
                    if t == 29:
                        for c in range(NCH):
                            sc.wait_ge(o["u1_pe"], c + 1)
                            copy(uT[:, c, :, :], bank(7).rearrange("p (a c) -> p a c", a=4)).then_inc(o["u1_evac"], 1)
                for level in range(5):
                    for c in range(NCH):
                        m = level * NCH + c
                        sc.wait_ge(o["y_pe"], m + 1)
                        if level:
                            sc.wait_ge(o["u_pe"], m - NCH + 1)
                        copy(yT[:, c, :, :], bank(4 + m % 2).rearrange("p (a c) -> p a c", a=4)).then_inc(o["y_evac"], 1)
                sc.wait_ge(o["bm"], 25)
                for c in range(NCH):
                    sc.wait_ge(o["vt_pe"], c + 1)
                    for p in range(C_PAIRS):
                        ins = copy(Vb[:, c, p, :], bank(c % 2)[:, p * P:(p + 1) * P], bhalf[:, c, p:p + 1])
                    ins.then_inc(o["vt_evac"], 1)
                sc.wait_ge(o["cs_pe"], 1)
                copy(csr[0:6, :], PS[0:6, 0:3072]).then_inc(o["cs_evac"], 1)
                sc.wait_ge(o["rg_pe"], 1)
                act_(oT, banks(0, 8, T), ACT.Exp).then_inc(o["eg"], 1)
                for n_, c in enumerate((0, 4, 1, 2, 3)):
                    sc.wait_ge(o["vn_pe"], n_ + 1)
                    if n_:
                        sc.wait_ge(o["s_pe"], n_)
                    for par in range(2):
                        h = slice(par * CH, (par + 1) * CH)
                        ins = copy(vnew[h, :, par, :], bank(1)[h, :].rearrange("p (a e) -> p a e", a=4))
                    ins.then_inc(o["vn_evac"], 1)
                    sc.wait_ge(o["o_pe"], n_ + 1)
                    copy(oT[:, :, c * CH:(c + 1) * CH], bank(2).rearrange("p (h t) -> p h t", t=CH))\
                        .then_inc(o["o_evac"], 1)
                sc.wait_ge(o["o_evac"], NCH)
                act_(sqO, oT, ACT.Square).then_inc(o["osq"], 1)
                act_(zth, zT, ACT.Tanh, scale=0.5).then_inc(o["zt"], 1)
                sc.wait_ge(o["orecip"], 1)
                act_(orr, orr, ACT.Sqrt).then_inc(o["orstd"], 1)

            def epilogue():
                for i in range(3):
                    n_ = P if i < 2 else TS
                    for half in range(2):
                        sc.wait_ge(pro_pe, 7 + 2 * i + half + 1)
                        copy(ytok[0:n_, i, half * 512:(half + 1) * 512], bank(2 * i + half)[0:n_, :])\
                            .then_inc(pro_evac, 1)

            prologue()
            split_gate_up(0, 0, 0, 0)
            ffn(0, C_FFN, 0)
            even()
            split_gate_up(1, 0, 0, 0)
            ffn(1, C_FFN + 8, X_FFN[1])
            ffn(2, C_FFN + 16, X_FFN[2])
            root(NORM_OD)
            odd()
            split_gate_up(3, 0, 0, 0)
            ffn(3, C_FFN + 24, X_FFN[3])
            epilogue()

        @block.vector
        def _(ve):
            tt, ts, stt, cp = ve.tensor_tensor, ve.tensor_scalar, ve.scalar_tensor_tensor, ve.tensor_copy
            steps = [0]

            def link(ins):
                steps[0] += 1
                ins.then_inc(dve_step, 1)
                ve.wait_ge(dve_step, steps[0])

            def mean_square_recip(r):
                ve.wait_ge(norm_sum, r + 1)
                link(ts(rstd, bank(6, T), 1.0 / D, EPS, ALU.mult, ALU.add))
                ve.reciprocal(rstd, rstd).then_inc(norm_recip, 1)
                ve.wait_ge(norm_rstd, r + 1)

            def norm(r, gain):
                mean_square_recip(r)
                for k in range(KT):
                    stt(hT[:, k, :], xT[:, k, :], cols[:, gain + k:gain + k + 1], rstd, ALU.mult, ALU.mult)\
                        .then_inc(h_ready, 1)

            def split(f, raw, slot, c, i):
                for j in range(2):
                    half = raw[:, slot, j * raw.shape[2] // 2:(j + 1) * raw.shape[2] // 2]
                    w = slice(j * raw.shape[2] // 2, (j + 1) * raw.shape[2] // 2)
                    ve.wait_ge(hi_done, halves_before(f, c) + 1 + j + 4 * i)
                    tt(w_parts[:, slot, 1, w], half, w_parts[:, slot, 0, w].bitcast(F32), ALU.subtract).then_inc(lo_done, 1)

            def ffn(f, gain):
                act_hi_32 = act_hi[:, :].bitcast(F32)
                mids = (2 * FT + KT) * f

                def activate(slot, c, i):
                    n = FT * f + c + 2 * i
                    ve.wait_ge(act_split, n + 1)
                    ve.wait_ge(gu_half, GU_FFN[f] + 1 + c + 2 * i)
                    tt(gated[:, slot, :], bank(2 * slot, T), rstd, ALU.mult).then_inc(scaled, 1)
                    ve.wait_ge(tanh_done, n + 1)
                    stt(gated[:, slot, :], tanh_g[:, slot, :], 1.0, gated[:, slot, :], ALU.add, ALU.mult)\
                        .then_inc(act_mid, 1)
                    ve.wait_ge(act_mid, mids + 1 + 2 * c + 4 * i)
                    ve.wait_ge(gu_done, GU_FFN[f] + 1 + c + 2 * i)
                    tt(gated[:, slot, :], gated[:, slot, :], bank(2 * slot + 1, T), ALU.mult).then_inc(act_done, 1)
                    ve.wait_ge(act_done, n + 3)
                    cols_ = slice(c * T, (c + 1) * T) if type(i) is int else bass.ds(2 * T * i + T * c, T)
                    cp(act_hi[:, cols_], gated[:, slot, :]).then_inc(act_mid, 1)
                    ve.wait_ge(act_mid, mids + 2 + 2 * c + 4 * i)
                    tt(act_lo[:, cols_], gated[:, slot, :], act_hi_32[:, cols_], ALU.subtract).then_inc(act_split, 1)

                def residual(slot, m, i):
                    ve.wait_ge(dn_done, DN_FFN[f] + 1 + m + 2 * i)
                    tt(tanh_g[:, slot, :], bank(4 + slot, T), rstd, ALU.mult).then_inc(act_mid, 1)
                    ve.wait_ge(act_mid, mids + 2 * FT + 1 + m + 2 * i)
                    xm = xf[:, m * T:(m + 1) * T] if type(i) is int else xf[:, bass.ds(2 * T * i + T * m, T)]
                    stt(xm, tanh_g[:, slot, :], 0.25, xm, ALU.mult, ALU.add).then_inc(x_upd, 1)

                xf = xT[:, :, :].rearrange("p k t -> p (k t)")
                for k in range(KT):
                    ve.wait_ge(h_hi_done, KT * f + k + 1)
                    stt(h_lo[:, k, :], xT[:, k, :], cols[:, gain + k:gain + k + 1], h_hi[:, k, :].bitcast(F32),
                        ALU.mult, ALU.subtract).then_inc(h_ready, 1)
                split(f, gu, 1, 1, 0)
                mean_square_recip(NORM_FFN[f])
                activate(0, 0, 0)
                with ve.Fori(0, FT // 2 - 1) as i:
                    split(f, gu, 0, 2, i)
                    activate(1, 1, i)
                    split(f, gu, 1, 3, i)
                    activate(0, 2, i)
                split(f, dn, 0, FT, 0)
                activate(1, FT - 1, 0)
                with ve.Fori(0, KT // 2 - 1) as i:
                    split(f, dn, 1, FT + 1, i)
                    residual(0, 0, i)
                    split(f, dn, 0, FT + 2, i)
                    residual(1, 1, i)
                split(f, dn, 1, FT + KT - 1, 0)
                residual(0, KT - 2, 0)
                if f == 1:
                    split(2, gu, 0, 0, 0)
                residual(1, KT - 1, 0)

            def residual(base_dn):
                for m in range(KT):
                    ve.wait_ge((dn_half, dn_done)[m % 2], half_count(base_dn, m))
                    tt(xT[:, m, :], bank(4 + m % 2, T), xT[:, m, :], ALU.add).then_inc(x_upd, 1)

            def half_count(base_dn, m):
                if m % 2:
                    return base_dn + m // 2 + 1
                return (4 if base_dn == DN_OD else 0) + m // 2 + 1

            def even():
                norm(1, C_MIX)
                ve.wait_ge(s["ev_evac"], 3)
                ve.wait_ge(s["zero_qi"], 1)
                for h in (slice(0, IDX_D), slice(IDX_D, P)):
                    cp(kiT[h, 0:TP], pr[0:IDX_D, T_KI, 0:TP])
                    cp(kiT[h, TP + PAST:TP + NK_S], pr[0:IDX_D, T_KI, TP:T])
                for par in range(2):
                    h = slice(par * IDX_D, (par + 1) * IDX_D)
                    for p in range(IDX_PAIRS):
                        ins = cp(qibd[h, :, p, par * CH:(par + 1) * CH],
                                 pr[h, T_QI + p, :].rearrange("p (c t) -> p c t", t=CH))
                ins.then_inc(s["idx_prep"], 1)
                ve.wait_ge(s["kw_pe"], 1)
                cp(kwtok[:, 0:2, :], bank(7, 136).rearrange("p (a c) -> p a c", a=2))
                ins = cp(kwtok[0:TS, 2, :], bank(7)[0:TS, 136:204])
                ins.then_inc(s["kw_evac"], 1)
                ve.wait_ge(s["kw_evac"], 1)
                for par in range(2):
                    h = slice(par * CH, (par + 1) * CH)
                    for bp in range(2):
                        cp(wcol[h, bp:4:2, :], kwtok[bp * CH:(bp + 1) * CH, 0:2, IDX_D + par:IDX_D + IDX_H:2])
                    ins = cp(wcol[h, 4, :], kwtok[0:CH, 2, IDX_D + par:IDX_D + IDX_H:2])
                link(ins)
                tt(dwi, istk.unsqueeze(1).to_broadcast([P, 10, CH]),
                   wcol.rearrange("p c a -> p (c a)").unsqueeze(2).to_broadcast([P, 10, CH]), ALU.mult)\
                    .then_inc(s["dwi_ready"], 1)

                def take8(work, rounds):
                    for _ in range(rounds):
                        link(ve.max(top8, work))
                        link(ve.match_replace(work, top8, work, TAKEN))

                def penalty(pen, work):
                    ts(pen[0:CH, :], work, TAKEN, -BIG, ALU.not_equal, ALU.mult)
                    return ts(pen[CH:P, :], work, TAKEN, -BIG, ALU.not_equal, ALU.mult)

                ve.memset(workX[0:CH, 192:256], PADDED)
                ve.memset(workY[0:CH, 128:NK_S], PADDED)
                ve.wait_ge(s["combX"], 1)
                cp(workX[CH:P, :], bank(7)[CH:P, 0:256])
                cp(workX[0:CH, 0:192], bank(7)[0:CH, 0:192]).then_inc(s["combX_used"], 1)
                ve.wait_ge(s["combX_used"], 1)
                take8(workX, TOP_P // 8)
                penalty(pen3, workX[CH:P, :])
                penalty(pen2, workX[0:CH, 0:192])
                ve.wait_ge(s["combY"], 1)
                cp(workY[CH:P, 0:512], bank(7)[CH:P, :])
                cp(workY[CH:P, 512:NK_S], bank(4)[CH:P, 0:64])
                cp(workY[0:CH, 0:128], bank(4)[0:CH, 128:256]).then_inc(s["combY_used"], 1)
                ve.wait_ge(s["combY_used"], 1)
                take8(workY, TOP_P // 8)
                penalty(pen1, workY[0:CH, 0:128])

                def head_rstd(summed, n_):
                    ve.wait_ge(summed, 1)
                    link(ts(view(rs, 0, 4, T), banks(4, 4, T), 1.0 / A_D, EPS, ALU.mult, ALU.add))
                    ve.reciprocal(rs[:, 0:4 * T], rs[:, 0:4 * T]).then_inc(s["qk_recip"], 1)

                left = TOP_S // 8 - TOP_P // 8
                head_rstd(s["qsum"], 1)
                take8(workY, left // 2)
                ve.wait_ge(s["qk_rstd"], 1)
                ve.wait_ge(s["zero_q"], 1)
                for p in range(A_PAIRS):
                    for par in range(2):
                        h = slice(par * A_D, (par + 1) * A_D)
                        ins = stt(qbd[h, :, p, par * CH:(par + 1) * CH],
                                  pr[h, T_Q + p, :].rearrange("p (c t) -> p c t", t=CH), cols[h, C_QN:C_QN + 1],
                                  rs[h, p * T:(p + 1) * T].rearrange("p (c t) -> p c t", t=CH), ALU.mult, ALU.mult)
                        ins.then_inc(s["q_ready"], 1)
                ve.wait_ge(s["q_ready"], 8)
                head_rstd(s["ksum"], 2)
                take8(workY, left - left // 2)
                link(penalty(penS, workY[CH:P, :]))
                ve.wait_ge(s["qk_rstd"], 2)
                for p in range(A_PAIRS):
                    stt(pr[:, T_K + p, :], pr[:, T_K + p, :], cols[:, C_KN:C_KN + 1], rs[:, p * T:(p + 1) * T],
                        ALU.mult, ALU.mult).then_inc(s["k_ready"], 1)
                ve.wait_ge(s["gate_pe"], 1)
                for j in range(2):
                    ins = ts(gx[:, j, :], bank(4 + j, T), cols[:, C_B2 + j:C_B2 + j + 1], None, ALU.add)
                ins.then_inc(s["gate_used"], 1)
                ve.wait_ge(s["gate_used"], 1)
                stt(gx2, gx, -1.0, gx, ALU.mult, ALU.min).then_inc(s["g_neg"], 1)
                ve.wait_ge(s["g_ln"], 1)
                link(stt(gx, gx, 0.0, gx2, ALU.min, ALU.subtract))
                for p in range(B_PAIRS):
                    for c in range(NCH):
                        w = slice(c * CH, (c + 1) * CH)
                        ins = ve.tensor_tensor_scan(gB[:, p, w], ones[:, 0:CH], gx[:, p, w], 0.0, ALU.mult, ALU.add)
                link(ins)
                g4 = gB.rearrange("p a (c t) -> p (a c) t", t=CH)
                tt(gdm.rearrange("p a (c t) -> p (a c) t", t=CH), g4, g4[:, :, CH // 2:CH // 2 + 1].to_broadcast([P, 10, CH]),
                   ALU.subtract)
                tt(gdl.rearrange("p a (c t) -> p (a c) t", t=CH), g4[:, :, CH - 1:CH].to_broadcast([P, 10, CH]), g4,
                   ALU.subtract).then_inc(s["g_args"], 1)
                ve.wait_ge(s["g_exps"], 1)
                ve.wait_ge(s["zero_bd"], 1)
                for par in range(2):
                    h = slice(par * B_K, (par + 1) * B_K)
                    w = slice(par * CH, (par + 1) * CH)
                    for p in range(B_PAIRS):
                        def ch(x):
                            return x.rearrange("p (c t) -> p c t", t=CH)
                        stt(qe_bd[h, p, :, w], ch(pr[h, T_QB + p, :]), B_K ** -0.5, ch(e_b[h, p, :]), ALU.mult, ALU.mult)
                        tt(km_bd[h, p, :, w], ch(pr[h, T_KB + p, :]), ch(e_mid_n[h, p, :]), ALU.mult)
                        tt(kl_bd[h, p, :, w], ch(pr[h, T_KB + p, :]), ch(gdl[h, p, :]), ALU.mult)
                stt(qm, pr[:, T_QB:T_QB + 2, :], B_K ** -0.5, gdm, ALU.mult, ALU.mult).then_inc(s["bds_ready"], 1)
                ve.wait_ge(s["ga_pe"], 1)
                kmu = km_bd.rearrange("p a c e -> p (a c) e")
                for par in range(2):
                    h = slice(par * B_K, (par + 1) * B_K)
                    ins = tt(kmu[h, :, par * CH:(par + 1) * CH], PS[h, 3072:3712].rearrange("p (u t) -> p u t", t=CH),
                             causal[h, :].unsqueeze(1).to_broadcast([CH, 10, CH]), ALU.mult)
                ins.then_inc(s["abd_ready"], 1)
                ve.wait_ge(s["su_pe"], 1)
                ve.wait_ge(caches_in, 16 * 5)
                link(ve.memset(Sg(0), 0.0))
                for c in (4, 0, 1, 2, 3):
                    src, dst = (5, 6) if c == 4 else (c, c + 1)
                    for p in range(B_PAIRS):
                        u = p * NCH + c
                        ins = stt(Sg(dst)[:, p, :], Sg(src)[:, p, :], es[:, p, c:c + 1], PS[:, u * P:(u + 1) * P],
                                  ALU.mult, ALU.add)
                    if c < 3 or c == 4:
                        link(ins)
                ins.then_inc(s["sg_ready"], 1)
                ve.wait_ge(s["gsum"], 1)
                link(ts(view(rs, 0, 4, T), banks(0, 4, T), 1.0 / B_V, EPS, ALU.mult, ALU.add))
                ve.reciprocal(rs[:, 0:4 * T], rs[:, 0:4 * T]).then_inc(s["grecip"], 1)
                ve.wait_ge(s["grstd"], 1)
                th = kl_bd.rearrange("p a c e -> p (a c e)")
                ve.wait_ge(s["sil_t"], 1)
                stt(th, th, 1.0, pr[:, T_RB:T_RB + 4, :].rearrange("p a b -> p (a b)"), ALU.add, ALU.mult)
                link(stt(oT[:, 4:8, :], oT[:, 4:8, :], cols[:, C_GLA:C_GLA + 1], view(rs, 0, 4, T), ALU.mult, ALU.mult))
                for h in range(4):
                    stt(oT[:, 4 + h, :], oT[:, 4 + h, :], 0.5, th[:, h * T:(h + 1) * T], ALU.mult, ALU.mult)\
                        .then_inc(s["ob_ready"], 1)

                def logits(b):
                    ve.wait_ge(s["qk_pe"], b + 1)
                    if b in (2, 3):
                        ve.wait_ge(s["pt_pe"], b - 1)
                    if b == 4:
                        ve.wait_ge(s["pt_pe"], 4)
                    L = logit(b)
                    k0 = PAST - CH * b
                    if b < 4:
                        nk = CH * (b + 1)
                        src = PS[:, (0, 2, 0, 2)[b] * 512:(0, 2, 0, 2)[b] * 512 + 1024]\
                            .rearrange("p (a c) -> p a c", a=4)[:, :, 0:nk]
                        ins = stt(L, src, A_D ** -0.5, biasT[:, :, k0:NK_S], ALU.mult, ALU.add)
                    else:
                        nk = NK_S
                        stt(L[:, :, 0:512], PS[:, 0:2048].rearrange("p (a c) -> p a c", a=4), A_D ** -0.5,
                            biasT[:, :, 0:512], ALU.mult, ALU.add)
                        ins = stt(L[:, :, 512:NK_S], bank(4, 256).rearrange("p (a c) -> p a c", a=4), A_D ** -0.5,
                                  biasT[:, :, 512:NK_S], ALU.mult, ALU.add)
                    ins.then_inc(s["l_done"], 1)
                    ve.wait_ge(s["l_done"], b + 1)
                    if b:
                        pen = (None, pen1, pen2, pen3, penS)[b]
                        link(tt(L, L, pen.unsqueeze(1).to_broadcast([P, A_PAIRS, nk]), ALU.add))
                    link(ve.tensor_reduce(mx[:, b, 0, :], L, AX, ALU.max))
                    ts(mx[:, b, 1, :], mx[:, b, 0, :], -1.0, None, ALU.mult).then_inc(s["nmx"], 1)

                def probs(b):
                    nk = CH * (b + 1) if b < 4 else NK_S
                    ve.wait_ge(s["exps_done"], b + 1)
                    link(ve.reciprocal(mx[:, b, 0, :], mx[:, b, 2, :]))
                    tt(logit(b), logit(b), mx[:, b, 0, :].unsqueeze(2).to_broadcast([P, A_PAIRS, nk]), ALU.mult)\
                        .then_inc(s["p_ready"], 1)

                def heads_out(b):
                    ve.wait_ge(s["pv_pe"], b + 1)
                    for par in range(2):
                        h = slice(par * A_D, (par + 1) * A_D)
                        ins = cp(oT[h, 0:4, b * CH:(b + 1) * CH],
                                 bank((6, 7, 6, 7, 2)[b])[h, :].rearrange("p (a c) -> p a c", a=4)
                                 [:, :, par * CH:(par + 1) * CH])
                    ins.then_inc(s["pv_evac"], 1)

                ve.wait_ge(s["bias_in"], 32)
                logits(0)
                logits(1)
                probs(0)
                logits(2)
                probs(1)
                heads_out(0)
                logits(3)
                probs(2)
                heads_out(1)
                probs(3)
                heads_out(2)
                heads_out(3)
                logits(4)
                probs(4)
                heads_out(4)
                split(1, gu, 0, 0, 0)
                residual(DN_EV)

            def odd():
                g = [growv(i)[0:C_H, :] for i in range(4)]
                link(ve.memset(qp[:, :, 0:3], 0.0))
                ve.wait_ge(small_in, 48)
                ve.wait_ge(o["ab_pe"], 1)
                ts(g[3], bank(5, T)[0:C_H, :], -80.0, -1.0, ALU.max, ALU.mult)
                link(ts(g[0], bank(4, T)[0:C_H, :], cols[0:C_H, 223:224], None, ALU.add))
                stt(g[1], g[0], -1.0, g[0], ALU.mult, ALU.min).then_inc(o["g1"], 1)
                ve.wait_ge(o["g2"], 1)
                link(ts(g[3], g[3], 1.0, None, ALU.add))
                ve.reciprocal(g[3], g[3])
                link(stt(g[0], g[0], 0.0, g[1], ALU.max, ALU.add))
                link(ts(g[0], g[0], cols[0:C_H, 224:225], -1.0, ALU.mult, ALU.mult))
                for c in range(NCH):
                    w = slice(c * CH, (c + 1) * CH)
                    ins = ve.tensor_tensor_scan(g[2][:, w], ones[0:C_H, 0:CH], g[0][:, w], 0.0, ALU.mult, ALU.add)
                ins.then_inc(o["g_rows"], 1)

                def conv(t):
                    tile_ = OD_TILES[t]
                    buf = qp[:, t % 4, :]
                    ve.wait_ge(o["evac"], t + 1)
                    cp(cst[:, tile_, 0:3], buf[:, 256:259])
                    cp(cst[:, tile_, 3:6], buf[:, 323:326])
                    link(cp(buf[:, 259:262], cols[:, C_ST + tile_:C_ST + 72:24]))
                    c_ = cring[:, t % 4, :]
                    link(ts(c_, buf[:, 0:323], cols[:, C_CONV + tile_:C_CONV + tile_ + 1], None, ALU.mult))
                    for j in range(1, 4):
                        at = C_CONV + 24 * j + tile_
                        ins = stt(c_, buf[:, j:j + 323], cols[:, at:at + 1], c_, ALU.mult, ALU.add)
                        if j < 3:
                            link(ins)
                    ins.then_inc(o["conv"], 1)

                def silu(t):
                    ve.wait_ge(o["th"], t + 1)
                    part, h = OD_TILES[t] // 8, OD_TILES[t] % 8
                    dst = cv[:, part, h // 2, :, (h % 2) * CH:(h % 2 + 1) * CH]
                    for c0, c1, at in ((0, 4, 0), (4, 5, TP + 3)):
                        ins = stt(dst[:, c0:c1, :], th2[:, t % 2, at:at + CH * (c1 - c0)].rearrange("p (c t) -> p c t", t=CH),
                                  1.0, cring[:, t % 4, at:at + CH * (c1 - c0)].rearrange("p (c t) -> p c t", t=CH),
                                  ALU.add, ALU.mult)
                    ins.then_inc(o["silu"], 1)

                def columns():
                    ve.wait_ge(o["col_pe"], 1)
                    for par in range(2):
                        ins = cp(colG[par * CH:(par + 1) * CH, :, :, :].rearrange("p w c a -> p (w c) a"),
                                 bank(6, 80)[0:CH, :].rearrange("p (u h) -> p u h", h=8)[:, :, par:8:2])
                    ins.then_inc(o["cols_ready"], 1)
                    ve.wait_ge(o["cols_ready"], 1)
                    ts(bhalf, colG[:, 1, :, :], 0.5, None, ALU.mult)

                def differences(half):
                    ve.wait_ge(o["row_pe"], half + 1)
                    if half == 0:
                        ve.wait_ge(o["masks"], 1)
                    cp(gl[:, 4 * half:4 * half + 4, :],
                       banks(4, 4, T).rearrange("p h (c t) -> p h c t", t=CH)[:, :, :, CH - 1])
                    for pp in range(2):
                        p = 2 * half + pp
                        for c in range(NCH):
                            row = banks(4 + 2 * pp, 2, T)[:, :, c * CH:(c + 1) * CH]
                            for dst, mask in ((At, maskI), (Dm, maskS)):
                                ins = stt(dst[:, c, p, :].rearrange("p (a t) -> p a t", a=2), row, colG[:, 0, c, p:p + 1],
                                          mask.rearrange("p (a t) -> p a t", a=2), ALU.subtract, ALU.add)
                    if half == 1:
                        link(ins)
                        for par in range(2):
                            h = slice(par * CH, (par + 1) * CH)
                            ins = tt(klc[h, :, :], gl[h, par:8:2, :].rearrange("p a c -> p c a"), colG[h, 0, :, :],
                                     ALU.subtract)
                    ins.then_inc(o["row_used"], 1)

                def head_rstd(g_):
                    ve.wait_ge(o["sum"], g_ + 1)
                    link(ts(view(rs, 0, 4, T), banks(4, 4, T), 0.25, EPS, ALU.mult, ALU.add))
                    ve.reciprocal(rs[:, 0:4 * T], rs[:, 0:4 * T]).then_inc(o["recip"], 1)

                def unit_heads(g_):
                    ve.wait_ge(o["rstd"], g_ + 1)
                    scale = 0.5 if g_ < 2 else 0.5 * C_D ** -0.5
                    c_ = group(g_)
                    stt(c_, c_, scale, rs[:, 0:4 * T], ALU.mult, ALU.mult).then_inc(o["kq_ready"], 1)
                    ve.wait_ge(o["kq_ready"], g_ + 1)

                for t in range(24):
                    conv(t)
                    if t:
                        silu(t - 1)
                    if t == 2:
                        columns()
                    if t == 4:
                        differences(0)
                    if t == 6:
                        differences(1)
                    if t == 12:
                        head_rstd(0)
                    if t == 14:
                        unit_heads(0)
                        head_rstd(1)
                    if t == 16:
                        unit_heads(1)
                    if t == 18:
                        head_rstd(2)
                    if t == 20:
                        unit_heads(2)
                        head_rstd(3)
                    if t == 22:
                        unit_heads(3)
                silu(23)
                ve.wait_ge(o["gexp"], 1)
                stt(ncol, egc, -1.0, colG[:, 1, :, :], ALU.mult, ALU.mult)
                ve.wait_ge(o["dexp"], 1)
                for c in range(NCH):
                    ve.wait_ge(o["kk_pe"], c + 1)
                    for p in range(C_PAIRS):
                        ins = stt(Lm[:, c, p, :], bank(4)[:, p * P:(p + 1) * P], colG[:, 1, c, p:p + 1], Dm[:, c, p, :],
                                  ALU.mult, ALU.mult)
                    ins.then_inc(o["kk_used"], 1)
                    tt(At[:, c, :, :], bank(5).rearrange("p (a c) -> p a c", a=4), At[:, c, :, :], ALU.mult)\
                        .then_inc(o["kk_used"], 1)
                for c in range(NCH):
                    ve.wait_ge(o["kk_used"], 2 * NCH)
                    link(tt(tT[:, c, :, :], Lm[:, c, :, :], lev[:, 0:1, :].to_broadcast([P, C_PAIRS, P]), ALU.mult))
                    tt(tT[:, c, :, :], ident[:, :].unsqueeze(1).to_broadcast([P, C_PAIRS, P]), tT[:, c, :, :],
                       ALU.subtract).then_inc(o["t1"], 1)
                for level in range(5):
                    for c in range(NCH):
                        m = level * NCH + c
                        ve.wait_ge(o["u_pe"], m + 1)
                        if level == 0:
                            ve.wait_ge(o["t1"], NCH)
                            ve.wait_ge(o["u1_evac"], NCH)
                        if level < 4:
                            ve.wait_ge(o["t_pe"], m + 1)
                            tt(tT[:, c, :, :], tT[:, c, :, :], bank(6).rearrange("p (a c) -> p a c", a=4), ALU.subtract)\
                                .then_inc(o["t_upd"], 1)
                        tt(uT[:, c, :, :], uT[:, c, :, :], bank(7).rearrange("p (a c) -> p a c", a=4), ALU.subtract)\
                            .then_inc(o["u_upd"], 1)
                ve.wait_ge(o["eg"], 1)
                for p in range(C_PAIRS):
                    c_ = cv[:, 0, p, :, :].rearrange("p c (a t) -> p c a t", a=2)
                    tt(c_, c_, oT[:, 2 * p:2 * p + 2, :].rearrange("p a (c t) -> p c a t", t=CH), ALU.mult)\
                        .then_inc(o["qe"], 1)
                ve.wait_ge(o["states"], 1)
                for n_, c in enumerate((0, 4, 1, 2, 3)):
                    ve.wait_ge(o["ks_pe"], n_ + 1)
                    ve.wait_ge(o["vt_evac"], NCH)
                    if n_:
                        ve.wait_ge(o["vn_pe"], n_)
                    for p in range(C_PAIRS):
                        ins = stt(Rr[:, p, :], bank(0)[:, p * P:(p + 1) * P], ncol[:, c, p:p + 1], Vb[:, c, p, :],
                                  ALU.mult, ALU.add)
                    ins.then_inc(o["r_ready"], 1)
                    ve.wait_ge(o["s_pe"], n_ + 1)
                    S = Sd[:, 1 if c == 4 else 0, :, :]
                    if n_ > 1:
                        ve.wait_ge(o["s_upd"], n_)
                    for h in range(C_H):
                        ins = stt(S[:, h, :], S[:, h, :], es8[:, h, c:c + 1],
                                  bank(3 + h // 4)[:, (h % 4) * P:(h % 4 + 1) * P], ALU.mult, ALU.add)
                    ins.then_inc(o["s_upd"], 1)
                ve.wait_ge(o["osum"], 1)
                link(ts(orr, banks(0, 8, T), 1.0 / C_D, EPS, ALU.mult, ALU.add))
                ve.reciprocal(orr, orr).then_inc(o["orecip"], 1)
                ve.wait_ge(o["zt"], 1)
                stt(zth, zth, 1.0, zT, ALU.add, ALU.mult)
                ve.wait_ge(o["orstd"], 1)
                link(stt(oT, oT, cols[:, C_OD:C_OD + 1], orr, ALU.mult, ALU.mult))
                stt(oT, oT, 0.5, zth, ALU.mult, ALU.mult).then_inc(o["og"], 1)
                split(3, gu, 0, 0, 0)
                residual(DN_OD)

            ve.sem_inc(x_upd, 2)
            ve.sem_inc(act_done, 2)
            ve.sem_inc(act_split, 2)
            split(0, gu, 0, 0, 0)
            ffn(0, C_FFN)
            even()
            ffn(1, C_FFN + 8)
            ffn(2, C_FFN + 16)
            norm(NORM_OD, C_MIX + 8)
            odd()
            ffn(3, C_FFN + 24)

        @block.gpsimd
        def _(po):
            steps = [0]

            def link(ins):
                steps[0] += 1
                ins.then_inc(pool_step, 1)
                po.wait_ge(pool_step, steps[0])

            def store(dst, src):
                po.dma_start(dst, src).then_inc(out_sem, 16)

            sel = po.affine_select
            po.memset(ones[:, :], 1.0)
            link(po.memset(ident[:, :], 0.0))
            sel(out=ident[:, :], in_=ident[:, :], compare_op=ALU.not_equal, fill=1.0, base=0, pattern=[[-1, P]],
                channel_multiplier=1).then_inc(consts, 1)
            po.memset(halves, 0.0)
            po.memset(istk, 0.0)
            link(po.memset(causal, 1.0))
            po.memset(halves[0:64, 0:64], 1.0)
            po.memset(halves[64:P, 64:P], 1.0)
            for par in range(2):
                h = slice(par * CH, (par + 1) * CH)
                sel(out=causal[h, :], in_=causal[h, :], compare_op=ALU.is_ge, fill=0.0, base=0, pattern=[[1, CH]],
                    channel_multiplier=-1)
                ins = sel(out=istk[h, :], in_=istk[h, :], compare_op=ALU.not_equal, fill=1.0, base=0,
                          pattern=[[-1, CH]], channel_multiplier=1)
            link(ins)
            po.wait_ge(small_in, 48)
            for b, lo, hi in bucket_runs():
                ins = po.tensor_copy(biasrow[0:A_H, lo + REL0:hi + REL0 + 1],
                                     rbT[0:A_H, b:b + 1].to_broadcast([A_H, hi - lo + 1]))
            link(ins)
            po.dma_start(scratch, biasrow[0:A_H, :].unsqueeze(1).to_broadcast([A_H, CH, REL_N])).then_inc(s["bias_out"], 16)
            po.wait_ge(s["bias_out"], 16)
            for par in range(2):
                src = bass.AP(scratch.tensor, par * CH * REL_N + CH - 1,
                              [[REL_N - 1, CH], [2 * CH * REL_N, A_PAIRS], [1, NK_S]])
                po.dma_start(biasT[par * CH:(par + 1) * CH, :, :], src).then_inc(s["bias_in"], 16)

            def squares_of(r, x_base):
                for k in range(KT):
                    po.wait_ge(x_upd, x_base - KT + k + 3)
                    if k:
                        link(po.tensor_tensor(square, xT[:, k, :], xT[:, k, :], ALU.mult))
                        ins = po.tensor_tensor(total, total, square, ALU.add)
                    else:
                        ins = po.tensor_tensor(total, xT[:, k, :], xT[:, k, :], ALU.mult)
                    if k < KT - 1:
                        link(ins)
                ins.then_inc(total_ready, 1)

            squares_of(NORM_EV, X_EV)
            po.wait_ge(x_upd, X_EV + 2)
            po.wait_ge(h_ready, KT * (NORM_EV + 1))
            po.memset(view(RA, 2560, 1280), 0.0).then_inc(s["zero_qi"], 1)
            po.memset(view(RA, 0, 2560), 0.0).then_inc(s["zero_q"], 1)
            po.wait_ge(s["kct_pe"], 4)
            po.memset(view(RB, bd_at, 3840), 0.0).then_inc(s["zero_bd"], 1)
            po.wait_ge(s["kw_evac"], 1)
            store(O["p_idx_k"][0, 0].rearrange("(i p) d -> p i d", p=P), kwtok[:, 0:2, 0:IDX_D])
            store(O["s_idx_k"][0, 0], kwtok[0:TS, 2, 0:IDX_D])
            for name, tok in (("v", vtok), ("k", ktok)):
                po.wait_ge(s[name + "tok_evac"], 3)
                store(O[f"p_attn_{name}"][0, 0].rearrange("(i p) h d -> p i (h d)", p=P), tok[:, 0:2, :])
                store(O[f"s_attn_{name}"][0, 0].rearrange("p h d -> p (h d)"), tok[0:TS, 2, :])
            po.wait_ge(s["sg_ready"], 1)
            for name, i in (("p_gla", 4), ("s_gla", 6)):
                store(O[name][0, 0].rearrange("(a b) d e -> a (b d) e", b=2).rearrange("a q e -> q a e"), Sg(i))
            squares_of(NORM_FFN[1], X_FFN[1])
            po.wait_ge(x_upd, X_FFN[1] + 2)
            po.wait_ge(out_sem, 16 * 8)
            po.memset(lev, 0.0)
            po.memset(maskI, -BIG)
            po.memset(maskS, BIG)
            po.memset(Sd[:, 0, :, :], 0.0)
            link(po.memset(klc, 0.0))
            for par in range(2):
                h = slice(par * CH, (par + 1) * CH)
                po.memset(maskI[h, par * CH:(par + 1) * CH], 0.0)
                link(po.memset(maskS[h, par * CH:(par + 1) * CH], 0.0))
                link(sel(out=maskI[h, par * CH:(par + 1) * CH], in_=maskI[h, par * CH:(par + 1) * CH], compare_op=ALU.is_ge,
                    fill=-BIG, base=0, pattern=[[1, CH]], channel_multiplier=-1))
                link(sel(out=maskS[h, par * CH:(par + 1) * CH], in_=maskS[h, par * CH:(par + 1) * CH], compare_op=ALU.is_gt,
                    fill=BIG, base=0, pattern=[[-1, CH]], channel_multiplier=1))
            for i in range(6):
                m = 1 << i
                part = lev[:, i, :].rearrange("p (n r) -> p n r", r=2 * m)[:, :, 0:m]
                link(po.memset(part, 1.0))
                link(sel(out=part, in_=part, compare_op=ALU.is_ge, fill=0.0, base=-m, pattern=[[-2 * m, P // (2 * m)], [0, m]],
                         channel_multiplier=1))
                ins = sel(out=part, in_=part, compare_op=ALU.is_ge, fill=0.0, base=2 * m - 1,
                          pattern=[[2 * m, P // (2 * m)], [0, m]], channel_multiplier=-1)
                if i < 5:
                    link(ins)
            ins.then_inc(o["masks"], 1)
            squares_of(NORM_FFN[2], X_FFN[2])
            squares_of(NORM_OD, X_OD)
            po.memset(vnew.rearrange("p a b e -> p (a b e)"), 0.0).then_inc(o["zero_v"], 1)
            po.sem_inc(o["states"], 1)
            for level in range(5):
                for c in range(NCH):
                    m = level * NCH + c
                    if level == 0:
                        po.wait_ge(o["kk_used"], 2 * NCH)
                    else:
                        po.wait_ge(o["y_pe"], m - NCH + 1)
                    po.tensor_tensor(Dm[:, c, :, :], Lm[:, c, :, :],
                                     lev[:, level + 1:level + 2, :].to_broadcast([P, C_PAIRS, P]), ALU.mult)\
                        .then_inc(o["bm"], 1)
            po.wait_ge(o["cs_evac"], 1)
            store(O["p_conv"][0, 0], csr[0:3, :])
            store(O["s_conv"][0, 0], csr[3:6, :])
            po.wait_ge(o["s_upd"], NCH)
            store(O["p_delta"][0, 0].rearrange("h d e -> d h e"), Sd[:, 0, :, :])
            store(O["s_delta"][0, 0].rearrange("h d e -> d h e"), Sd[:, 1, :, :])
            squares_of(NORM_FFN[3], X_FFN[3])
            po.wait_ge(pro_evac, 13)
            store(O["y_prompt"][0].rearrange("(i p) d -> p i d", p=P), ytok[:, 0:2, :])
            store(O["y_sample"][0], ytok[0:TS, 2, :])
            po.wait_ge(out_sem, 16 * 14)


INPUTS = ["x_prompt", "x_sample", "cache_attn_k", "cache_attn_v", "cache_idx_k", "state_gla", "state_delta",
          "state_conv", "ffn_norm", "ffn_w_gate", "ffn_w_up", "ffn_w_down", "mix_norm", "ev_w_in", "ev_q_norm",
          "ev_k_norm", "rel_bias", "ev_gate_w2", "ev_gate_b2", "ev_gla_norm", "ev_w_out", "od_w_in", "od_conv_w",
          "od_a_log", "od_dt_bias", "od_norm", "od_w_out"]
OUTPUTS = [("y_prompt", (1, TP, D)), ("y_sample", (1, TS, D)),
           ("p_attn_k", (1, 1, TP, 8, 64)), ("p_attn_v", (1, 1, TP, 8, 64)), ("p_idx_k", (1, 1, TP, 64)),
           ("p_gla", (1, 1, 4, 64, 128)), ("p_delta", (1, 1, 8, 128, 128)), ("p_conv", (1, 1, 3, 3072)),
           ("s_attn_k", (1, 1, TS, 8, 64)), ("s_attn_v", (1, 1, TS, 8, 64)), ("s_idx_k", (1, 1, TS, 64)),
           ("s_gla", (1, 1, 4, 64, 128)), ("s_delta", (1, 1, 8, 128, 128)), ("s_conv", (1, 1, 3, 3072))]


def kernel(**inputs):
    import numpy as np
    import concourse.bacc as bacc
    from concourse.bass_utils import run_bass_kernel_spmd

    nc = bacc.Bacc("TRN2", target_bir_lowering=False, num_devices=1)
    arrays = {f"in_{name}": np.ascontiguousarray(inputs[name]) for name in INPUTS}
    ins = {name: nc.dram_tensor(f"in_{name}", arrays[f"in_{name}"].shape, F32, kind="ExternalInput").ap()
           for name in INPUTS}
    outs = {name: nc.dram_tensor(f"out_{name}", shape, F32, kind="ExternalOutput").ap() for name, shape in OUTPUTS}
    build(nc, ins, outs)
    r = run_bass_kernel_spmd(nc, [arrays], core_ids=[0])
    return tuple(r.results[0][f"out_{name}"] for name, _ in OUTPUTS)
```

```python
from contextlib import ExitStack

import concourse.bass as bass
from concourse import mybir

ALU = mybir.AluOpType
ACT = mybir.ActivationFunctionType
F32 = mybir.dt.float32
F32R = mybir.dt.float32r
AX = mybir.AxisListType.X

P = 128
D = 1024
KT = D // P
TP, TS = 256, 64
T = TP + TS
ARENA_N = 52968
RB_N = 29300
CH = 64
NCH = T // CH
PAST = 512
FF = 2816
FT = FF // P
EPS = 1e-6
SPLIT_N = (KT + FT) * T + 2 * 2 * FT * P
BIG = 1e30
TAKEN = -3.0e38
PADDED = -2.0e38
A_H, A_D, A_PAIRS = 8, 64, 4
IDX_H, IDX_D, IDX_PAIRS = 4, 64, 2
TOP_P = min(256, TP // 4)
NK_S = PAST + TS
TOP_S = min(256, NK_S // 4)
B_PAIRS, B_K, B_V, B_RANK, B_TAU = 2, 64, 128, 16, 16.0
C_H, C_D, C_PAIRS = 8, 128, 4
N_BUCKETS, MAX_DIST = 32, 128
REL0 = NK_S - 1
REL_N = 640

EV = {}
_at = 0
for _name, _size in (("q", 512), ("k", 512), ("v", 512), ("qi", 256), ("ki", 64), ("wi", 4),
                     ("qb", 256), ("kb", 256), ("vb", 512), ("rb", 512), ("ab", 16)):
    EV[_name] = _at
    _at += _size
EV_LOADS = [[(EV["qi"], 128), (EV["qi"] + 128, 128)], [(EV["ki"], 68), (EV["ab"], 16)]]
for _name, _tiles in (("q", 4), ("k", 4), ("qb", 2), ("kb", 2), ("vb", 4), ("v", 4), ("rb", 4)):
    for _t in range(0, _tiles, 2):
        EV_LOADS.append([(EV[_name] + 128 * _t, 128), (EV[_name] + 128 * _t + 128, 128)])
T_QI, T_KI, T_AB, T_Q, T_K, T_QB, T_KB, T_VB, T_V, T_RB = 0, 2, 3, 4, 8, 12, 14, 16, 20, 24
N_EV = 2 * len(EV_LOADS)

OD_TILES = [t for a in (24, 8, 10, 26, 12, 14, 28, 0, 2, 4, 6, 16, 18, 20, 22, 30) for t in (a, a + 1)]
N_OD = len(OD_TILES)
CONV_AT = [t for t, tile_ in enumerate(OD_TILES) if tile_ < 24]

GU_FFN = [0, 22 + 14, 22 + 14 + 22, 22 + 14 + 22 + 22 + 16]
GU_EV = 22
GU_OD = 80
DN_FFN = [0, 12, 20, 32]
DN_EV, DN_OD = 8, 28
SUMS_AFTER, RSTD_AFTER = (4, 7, 11, 13), (7, 9, 13, 14)
CHUNK_ORDER = (0, 4, 1, 2, 3)
N_GU = 118
N_DN = 40


def bucket_runs():
    def bucket(rel):
        n, half = abs(rel), N_BUCKETS // 2
        exact = half // 2
        if n >= exact:
            j = max(j for j in range(half - exact + 1) if n ** exact >= exact ** exact * (MAX_DIST // exact) ** j)
            n = min(half - 1, exact + j)
        return n + (half if rel > 0 else 0)
    runs = []
    for rel in range(-REL0, REL_N - REL0):
        b = bucket(rel)
        if runs and runs[-1][0] == b:
            runs[-1][2] = rel
        else:
            runs.append([b, rel, rel])
    return runs


def build(nc, I, O):
    with ExitStack() as ctx:
        def sb(name, shape):
            return ctx.enter_context(nc.sbuf_tensor(name, shape, F32))

        def sem(name):
            return ctx.enter_context(nc.semaphore(name))

        PS = ctx.enter_context(nc.psum_tensor("PS", [P, 8 * 512], F32))
        arena = sb("arena", [P, ARENA_N])
        arena_at = nc.sbuf_base - 4 * ARENA_N
        placed = [0]

        def place(name, *dims):
            at = placed[0]
            n_ = 1
            for d in dims:
                n_ *= d
            placed[0] = at + (n_ + 7) // 8 * 8
            assert placed[0] <= ARENA_N
            return nc.alloc_sbuf_tensor_at(name, [P, *dims], F32, offset=arena_at + 4 * at), at

        def rounded(name, at, *dims):
            return nc.alloc_sbuf_tensor_at(name, [P, *dims], F32R, offset=arena_at + 4 * at)

        xT, _ = place("xT", KT, T)
        hT, hT_at = place("hT", KT, T)
        gu, _ = place("gu", 2, 2048)
        dn, dn_at = place("dn", 2, FT * 128)
        RA, RA_at = place("RA", 7040)
        RB, RB_at = place("RB", RB_N)
        ident, _ = place("ident", P)
        ones, _ = place("ones", P)
        cols, _ = place("cols", 226)
        rs, _ = place("rs", 1280)
        oT = hT[:, :, :]
        h_hi = rounded("h_hi", hT_at, KT, T)
        act_hi = rounded("act_hi", RA_at, FT * T)
        h_lo = rounded("h_lo", RB_at, KT, T)
        act_lo = rounded("act_lo", RB_at + KT * T, FT * T)
        w_mix = rounded("w_mix", dn_at, 2, 2, KT * P)
        w_parts = rounded("w_parts", RB_at + (KT + FT) * T, 2, 2, FT * P)

        def bank(b, n=512, at=0):
            return PS[:, b * 512 + at:b * 512 + at + n]

        def banks(b, m, n):
            return PS[:, b * 512:(b + m) * 512].rearrange("p (a c) -> p a c", a=m)[:, :, 0:n]

        def view(t, at, *dims):
            n = 1
            for d in dims:
                n *= d
            flat = t[:, at:at + n]
            if len(dims) == 1:
                return flat
            names = "abcd"[:len(dims)]
            return flat.rearrange(f"p ({' '.join(names)}) -> p {' '.join(names)}",
                                  **{n_: d for n_, d in zip(names, dims)})

        act = view(RA, 0, FT, T)
        squares = view(RA, 0, KT, T)
        xnat = view(RA, 0, 3, D)
        qbd = view(RA, 0, NCH, A_PAIRS, P)
        qibd = view(RA, 2560, NCH, IDX_PAIRS, P)
        pT = view(RA, 3840, 5, 512)
        workX = view(RA, 3840, 256)
        workY = view(RA, 3840 + 256, 576)
        sqE = view(RA, 3840 + 1280, 4, T)
        h32_even = view(RA, 3840, KT, T)
        gx = view(RA, 3840, 2, T)
        gx2 = view(RA, 3840 + 640, 2, T)
        e_mid_n = view(RA, 3840 + 1280, 2, T)
        e_b = view(RA, 3840 + 1920, 2, T)
        dwi = view(RA, 6400, 10, CH)
        n = SPLIT_N
        rstd = view(RB, n, T); n += T
        total = view(RB, n, T); n += T
        square = view(RB, n, T); n += T
        high_at = n
        vcache = view(RB, n, 4, 512); n += 2048
        kcn = view(RB, n, 4, 512); n += 2048
        ipn = view(RB, n, 4, 64); n += 256
        biasT = view(RB, n, A_PAIRS, NK_S)
        biasrow = view(RB, n, REL_N); n += A_PAIRS * NK_S
        Sg5 = view(RB, n, B_PAIRS, P); n += B_PAIRS * P
        rbT = view(RB, n, 32); n += 32
        w2 = view(RB, n, 256); n += 256
        halves = view(RB, n, P); n += P
        causal = view(RB, n, CH); n += CH
        istk = view(RB, n, CH); n += CH
        assert n <= RB_N, n
        n = 0
        pr = view(RB, n, N_EV, T); n += N_EV * T
        kcT = view(RB, n, A_PAIRS, 512); n += 2048
        kiT = view(RB, n, TP + NK_S); n += TP + NK_S
        l_at = n
        n += A_PAIRS * NK_S
        bd_at = n
        qe_bd = view(RB, n, B_PAIRS, NCH, P); n += 1280
        km_bd = view(RB, n, B_PAIRS, NCH, P); n += 1280
        kl_bd = view(RB, n, B_PAIRS, NCH, P); n += 1280
        Sgs = view(RB, n, 6, B_PAIRS, P); n += 6 * B_PAIRS * P
        kwtok = view(RB, n, 3, 68); n += 204
        wcol = view(RB, n, NCH, IDX_PAIRS); n += 10
        mx = view(RB, n, NCH, 3, 4); n += 60
        es = view(RB, n, B_PAIRS, NCH); n += 10
        top8 = view(RB, n, 8); n += 8
        qm = view(RB, n, B_PAIRS, T); n += 640
        pen3 = view(RB, n, 256); n += 256
        pen1 = view(RB, n, 128); n += 128
        gcol = view(RB, n, 10); n += 10
        assert n <= SPLIT_N, n
        h_lo_even = rounded("h_lo_even", RB_at + bd_at, KT, T)
        vtok = view(RB, high_at + 2048, 3, 512)
        penS = view(RB, high_at + 2048 + 1536, NK_S)
        pen2 = view(RB, high_at + 2048 + 1536 + NK_S, 192)
        ktok = view(RB, 0, 3, 512)
        rX3 = view(RB, l_at, 2, 256)
        rX2 = view(RB, l_at + 512, 2, 192)
        rYS = view(RB, l_at + 896, 2, NK_S)
        rY1 = view(RB, l_at + 2048, 2, 128)
        gB = view(RB, l_at, B_PAIRS, T)
        gdm = view(RB, l_at + 640, B_PAIRS, T)
        gdl = view(RB, l_at + 1280, B_PAIRS, T)
        vp = pr[:, T_V:T_V + 4, :].rearrange("p a b -> p (a b)").rearrange("p (u e) -> p u e", e=P)
        n = high_at
        Sd = view(RB, n, 2, C_H, P); n += 2048
        cst = view(RB, n, 24, 6); n += 144
        csr = view(RB, n, 24 * P)
        Dm = view(RB, n, NCH, C_PAIRS, P); n += 2560
        lev = view(RB, n, 6, P); n += 768
        maskI = view(RB, n, P); n += P
        maskS = view(RB, n, P); n += P
        rows8 = view(RB, n, 4, T); n += 4 * T
        gl = view(RB, n, C_H, NCH); n += C_H * NCH
        es8 = view(RB, n, C_H, NCH); n += C_H * NCH
        colG = view(RB, n, 2, NCH, C_PAIRS); n += 40
        egc = view(RB, n, NCH, C_PAIRS); n += 20
        ncol = view(RB, n, NCH, C_PAIRS); n += 20
        bhalf = view(RB, n, NCH, C_PAIRS); n += 20
        klc = view(RB, n, NCH, C_PAIRS); n += 20
        hcol = view(RB, n, 4, 10); n += 40
        ocol = view(RB, n, NCH, 4); n += 20
        assert n <= RB_N, n
        n = 0
        cv = view(RB, n, 3, C_PAIRS, NCH, P); n += 24 * T
        qp = view(RB, n, 4, 326); n += 4 * 326
        zT = view(RB, n, 8, T); n += 8 * T
        expG = view(RB, n, 8, T)
        uT = view(RB, n, NCH, C_PAIRS, P); n += 2560
        At = view(RB, n, NCH, C_PAIRS, P); n += 2560
        Kl = view(RB, n, NCH, C_PAIRS, P); n += 2560
        lm_at = n
        Lm = view(RB, n, NCH, C_PAIRS, P); n += 2560
        Vb = Lm
        assert n <= high_at, n
        tT = view(RA, 0, NCH, C_PAIRS, P)
        yT = view(RA, 2560, NCH, C_PAIRS, P)
        vnew = view(RA, 5120, C_PAIRS, 2, P)
        Rr = view(RA, 6144, C_PAIRS, P)
        S_odd = view(RA, 0, C_H, P)
        S_sample = view(RA, 1024, C_H, P)
        sqO = view(RA, 2048, 512)
        zth = view(RA, 2560, 8, T)
        cring = view(RA, 0, 4, 323)
        sq4 = view(RA, 1292, 4 * T)
        th2 = view(RA, 2572, 2, 323)
        wab = view(RA, 3224, KT, 40)
        h32_odd = view(RA, 0, KT, T)
        h_lo_odd = rounded("h_lo_odd", RA_at + 4480, KT, T)
        vbx = pr[:, T_VB:T_VB + 4, :].rearrange("p a b -> p (a b)").rearrange("p (a c e) -> p a c e", a=2, e=P)
        ytok = view(RA, 0, 3, D)
        tanh_g = view(rs, 0, 2, T)
        gated = view(rs, 640, 2, T)

        def group(g):
            return cv[:, 1 - g // 2, 2 * (g % 2):2 * (g % 2) + 2, :, :].rearrange("p a c e -> p (a c e)")

        def Sg(i):
            return Sg5 if i == 5 else Sgs[:, i if i < 5 else 5, :, :]

        def product_bank(c):
            return 0 if c % 2 else 4

        def state_before(c):
            return (Sd[:, 0, :, :], S_odd, Sd[:, 0, :, :], S_odd, Sd[:, 1, :, :])[c]

        def state_after(c):
            return (S_odd, Sd[:, 0, :, :], S_odd, Sd[:, 0, :, :], S_sample)[c]

        def growv(i):
            return rows8[:, i, :]

        def logit(b):
            return view(RB, l_at + (0, 256, 1280, 0, 0)[b], A_PAIRS, CH * (b + 1) if b < 4 else NK_S)

        def raw_logit(b):
            step = (64, 128, 256, 256)[b]
            return PS[:, (0, 512, 1024, 0)[b]:(0, 512, 1024, 0)[b] + 4 * step]\
                .rearrange("p (a c) -> p a c", a=A_PAIRS)[:, :, 0:CH * (b + 1)]

        def pt_slot(b):
            return (0, 2, 0, 2, 0)[b]

        C_FFN, C_MIX, C_GLA, C_OD, C_B2, C_QN, C_KN = 0, 32, 48, 49, 50, 52, 53
        C_CONV, C_ST = 54, 150
        eps_col = cols[:, 225:226]

        gu_loaded = [sem("gu_loaded0"), sem("gu_loaded1")]
        dn_loaded = [sem("dn_loaded0"), sem("dn_loaded1")]
        gu_half, gu_done = sem("gu_half"), sem("gu_done")
        dn_half, dn_done = sem("dn_half"), sem("dn_done")
        x_upd = sem("x_upd")
        scaled, tanh_done, act_mid, act_done, act_split = (sem(s) for s in (
            "scaled", "tanh_done", "act_mid", "act_done", "act_split"))
        hi_done, lo_done, h_hi_done, h_made = sem("hi_done"), sem("lo_done"), sem("h_hi_done"), sem("h_made")
        mix_hi, mix_lo, mix_half = sem("mix_hi"), sem("mix_lo"), sem("mix_half")
        sq_done, total_ready, norm_sum, norm_rstd, h_ready = (sem(s) for s in (
            "sq_done", "total_ready", "norm_sum", "norm_rstd", "h_ready"))
        consts = sem("consts")
        params_in, x_in, caches_in, small_in, out_sem = (sem(s) for s in (
            "params_in", "x_in", "caches_in", "small_in", "out_sem"))
        pool_step, dve_step, act_step = sem("pool_step"), sem("dve_step"), sem("act_step")
        pro_pe, pro_evac = sem("pro_pe"), sem("pro_evac")

        scratch = nc.dram_tensor("bias_rows", (A_H, CH, REL_N), F32, kind="Internal").ap()

        def gu_source(n):
            slot = gu[:, n % 2, :]
            for f in range(4):
                if GU_FFN[f] <= n < GU_FFN[f] + FT:
                    g = n - GU_FFN[f]
                    return [(slot[:, j * 1024:(j + 1) * 1024].rearrange("p (k c) -> p k c", k=KT),
                             ffn_w(I[name], f)[:, :, g * P:(g + 1) * P])
                            for j, name in enumerate(("ffn_w_gate", "ffn_w_up"))]
            if GU_EV <= n < GU_EV + len(EV_LOADS):
                tiles = EV_LOADS[n - GU_EV]
                w = I["ev_w_in"][0].rearrange("(k p) c -> p k c", p=P)
                if tiles[1][0] == tiles[0][0] + P:
                    dst = slot.rearrange("p (k c) -> p k c", k=KT)
                    src = w[:, :, tiles[0][0]:tiles[0][0] + 256]
                    return [(dst[:, 4 * j:4 * j + 4, :], src[:, 4 * j:4 * j + 4, :]) for j in range(2)]
                return [(slot.rearrange("p (k c) -> p k c", k=KT)[:, :, 128 * j:128 * j + w_],
                         w[:, :, c0:c0 + w_]) for j, (c0, w_) in enumerate(tiles)]
            t = OD_TILES[2 * (n - GU_OD)]
            dst = slot.rearrange("p (k c) -> p k c", k=KT)
            src = I["od_w_in"][0].rearrange("(k p) c -> p k c", p=P)[:, :, t * P:t * P + 256]
            return [(dst[:, 4 * j:4 * j + 4, :], src[:, 4 * j:4 * j + 4, :]) for j in range(2)]

        def ffn_w(w, f):
            return w[f // 2, f % 2].rearrange("(k p) c -> p k c", p=P)

        def dn_source(n):
            for f in range(4):
                if DN_FFN[f] <= n < DN_FFN[f] + KT:
                    m = n - DN_FFN[f]
                    return (dn[:, n % 2, :].rearrange("p (k c) -> p k c", k=FT),
                            ffn_w(I["ffn_w_down"], f)[:, :, m * P:(m + 1) * P])
            w, m = (I["ev_w_out"], n - DN_EV) if n < DN_EV + 4 else (I["od_w_out"], n - DN_OD)
            return (dn[:, n % 2, 0:2048].rearrange("p (k c) -> p k c", k=KT),
                    w[0].rearrange("(k p) c -> p k c", p=P)[:, :, m * 256:(m + 1) * 256])

        def halves_before(f, c):
            return 2 * ((FT + KT) * f + c)

        def gu_free(n):
            for f in range(4):
                if GU_FFN[f] <= n < GU_FFN[f] + FT:
                    return lo_done, halves_before(f, n - GU_FFN[f] + 1)
            return mix_lo, mix_halves(n) + 4

        def mix_halves(n):
            return 4 * (n - GU_EV) if n < GU_OD else 2 * N_EV + 4 * (n - GU_OD)

        def dn_free(n):
            for f in range(4):
                if DN_FFN[f] <= n < DN_FFN[f] + KT:
                    return lo_done, halves_before(f, FT + n - DN_FFN[f] + 1)
            return dn_done, n + 1

        X_FFN = [0, 16, 24, 40]
        X_EV, X_OD = 8, 32
        NORM_FFN = [0, 2, 3, 5]
        NORM_EV, NORM_OD = 1, 4

        names = ("ev_evac kct_pe kct_evac kw_pe kw_evac idx_prep raw raw_used comb comb_used qk_read gspread "
                 "gnormed dwi_ready qsq ksq qsum ksum qk_rstd q_ready k_ready gate_pe gate_used g_neg g_ln g_args "
                 "g_exps bds_ready zero ktr ktok_evac vtr vtok_evac ga_pe abd_ready vp_pe vp_evac kl_pe kl_evac "
                 "su_pe sg_ready go_pe go_evac gsq gsum grecip grstd sil_t ob_ready qk_pe l_done nmx exps_done "
                 "p_ready pt_pe pt_evac pv_pe pv_evac bias_out bias_in")
        s = {k: sem("ev_" + k) for k in names.split()}
        names = ("evac ab_in ab_pe conv th silu zero_v masks g1 g2 g_rows col_pe cols_ready row_pe row_used dexp "
                 "sq sum recip rstd kq_ready kk_pe kk_used kt_evac vt_pe vt_evac t1 u1_pe u1_evac bm y_pe y_evac "
                 "t_pe u_pe t_upd u_upd cs_pe cs_evac eg qe ks_pe r_ready vn_pe vn_evac o_pe s_pe s_upd osq osum "
                 "orecip orstd osp zt og states ds_in gexp spread")
        o = {k: sem("od_" + k) for k in names.split()}

        block = ctx.enter_context(nc.Block())

        @block.sync
        def _(sp):
            def load_gu(n):
                if n >= 2:
                    sp.wait_ge(*gu_free(n - 2))
                for dst, src in gu_source(n):
                    sp.dma_start(dst, src).then_inc(gu_loaded[n % 2], 16)

            def load_dn(n):
                if n >= 2:
                    sp.wait_ge(*dn_free(n - 2))
                dst, src = dn_source(n)
                sp.dma_start(dst, src).then_inc(dn_loaded[n % 2], 16)

            def ffn(f, following):
                wg, wu = ffn_w(I["ffn_w_gate"], f), ffn_w(I["ffn_w_up"], f)
                with sp.Fori(1, FT // 2) as i:
                    for slot in range(2):
                        sp.wait_ge(lo_done, halves_before(f, slot - 1) + 4 * i)
                        for j, w in enumerate((wg, wu)):
                            dst = gu[:, slot, j * 1024:(j + 1) * 1024].rearrange("p (k c) -> p k c", k=KT)
                            sp.dma_start(dst, w[:, :, bass.ds(256 * i + P * slot, P)]).then_inc(gu_loaded[slot], 16)
                load_dn(DN_FFN[f])
                load_dn(DN_FFN[f] + 1)
                if following is not None:
                    load_gu(following)
                    load_gu(following + 1)
                wd = ffn_w(I["ffn_w_down"], f)
                with sp.Fori(1, KT // 2) as i:
                    for slot in range(2):
                        sp.wait_ge(lo_done, halves_before(f, FT + slot - 1) + 4 * i)
                        sp.dma_start(dn[:, slot, :].rearrange("p (k c) -> p k c", k=FT),
                                     wd[:, :, bass.ds(256 * i + P * slot, P)]).then_inc(dn_loaded[slot], 16)

            sp.dma_start(xnat[:, 0:2, :], I["x_prompt"][0].rearrange("(i p) d -> p i d", p=P)).then_inc(x_in, 16)
            sp.dma_start(xnat[0:TS, 2, :], I["x_sample"][0]).then_inc(x_in, 16)
            load_gu(0)
            sp.wait_ge(params_in, 16 * 11)
            load_gu(1)
            sp.dma_start(kcn, I["cache_attn_k"][0, 0].rearrange("(t p) h d -> p t (h d)", p=P)).then_inc(caches_in, 16)
            sp.dma_start(vcache, I["cache_attn_v"][0, 0].rearrange("(t p) h d -> p t (h d)", p=P)).then_inc(caches_in, 16)
            sp.dma_start(ipn, I["cache_idx_k"][0, 0].rearrange("(t p) d -> p t d", p=P)).then_inc(caches_in, 16)
            sp.dma_start(Sg5,
                         I["state_gla"][0, 0].rearrange("(a b) d e -> a (b d) e", b=2).rearrange("a q e -> q a e")).then_inc(caches_in, 16)
            sp.dma_start(w2[0:B_RANK, :], I["ev_gate_w2"][0]).then_inc(caches_in, 16)
            ffn(0, GU_EV)
            for l in range(2, len(EV_LOADS)):
                load_gu(GU_EV + l)
            load_gu(GU_FFN[1])
            load_gu(GU_FFN[1] + 1)
            sp.wait_ge(gu_done, GU_EV + len(EV_LOADS))
            load_dn(DN_EV)
            load_dn(DN_EV + 1)
            load_dn(DN_EV + 2)
            load_dn(DN_EV + 3)
            ffn(1, GU_FFN[2])
            sp.wait_ge(x_upd, X_FFN[1] + 2)
            sp.wait_ge(out_sem, 16 * 8)
            sp.dma_start(Sd[:, 1, :, :], I["state_delta"][0, 0].rearrange("h d e -> d h e")).then_inc(o["ds_in"], 16)
            ffn(2, GU_OD)
            sp.wait_ge(x_upd, X_OD + 2)
            for at, c0, width in ((0, 4 * D, 16), (16, 4 * D, 16), (32, 4 * D + C_H, C_H)):
                sp.dma_start(wab[:, :, at:at + width],
                             I["od_w_in"][0].rearrange("(k p) c -> p k c", p=P)[:, :, c0:c0 + width]).then_inc(o["ab_in"], 16)
            for l in range(2, 16):
                load_gu(GU_OD + l)
            load_gu(GU_FFN[3])
            load_gu(GU_FFN[3] + 1)
            sp.wait_ge(gu_done, GU_OD + 16)
            load_dn(DN_OD)
            load_dn(DN_OD + 1)
            load_dn(DN_OD + 2)
            load_dn(DN_OD + 3)
            ffn(3, None)

        @block.tensor
        def _(pe):
            mm, tr = pe.matmul, pe.transpose

            def prologue():
                pe.wait_ge(consts, 1)
                pe.wait_ge(x_in, 32)
                for i in range(3):
                    rows = P if i < 2 else TS
                    for half in range(2):
                        for k in range(4):
                            ins = tr(bank(2 * i + half)[:, k * P:k * P + rows],
                                     xnat[0:rows, i, (4 * half + k) * P:(4 * half + k + 1) * P], ident[0:rows, 0:rows])
                        ins.then_inc(pro_pe, 1)
                pe.wait_ge(params_in, 16 * 11)
                tr(bank(6)[:, 0:54], rs[0:54, 0:P], ident[0:54, 0:54])
                tr(bank(6)[:, 54:150], rs[0:96, P:2 * P], ident[0:96, 0:96])
                tr(bank(6)[:, 150:222], rs[0:72, 2 * P:3 * P], ident[0:72, 0:72]).then_inc(pro_pe, 1)

            def norm(r):
                if r == 0:
                    pe.wait_ge(pro_evac, 7)
                    for k in range(KT):
                        if k % 2 == 0:
                            pe.wait_ge(sq_done, k // 2 + 1)
                        ins = mm(bank(6, T), ones[:, :], squares[:, k, :], start=(k == 0), stop=(k == KT - 1))
                else:
                    pe.wait_ge(total_ready, r)
                    ins = mm(bank(6, T), ones[:, :], total, start=True, stop=True)
                ins.then_inc(norm_sum, 1)

            def block_product(out, slot, at, hi, lo, first, last):
                w_hi, w_lo = w_parts[:, slot, 0, at:at + P], w_parts[:, slot, 1, at:at + P]
                mm(out, w_hi, hi, start=first, stop=False)
                mm(out, w_hi, lo, start=False, stop=False)
                return mm(out, w_lo, hi, start=False, stop=last)

            def ffn(f):
                def gate_up(slot, c, i):
                    pe.wait_ge(act_done, FT * f + 1 + c + 2 * i)
                    for j, done in ((0, gu_half), (1, gu_done)):
                        pe.wait_ge(lo_done, halves_before(f, c) + 1 + j + 4 * i)
                        for k in range(KT):
                            if type(i) is int and c == 0 and j == 0:
                                pe.wait_ge(h_ready, KT * NORM_FFN[f] + k + 1)
                            ins = block_product(bank(2 * slot + j, T), slot, j * 1024 + k * P, h_hi[:, k, :],
                                                h_lo[:, k, :], k == 0, k == KT - 1)
                        ins.then_inc(done, 1)

                def down(slot, m, i):
                    pe.wait_ge(x_upd, X_FFN[f] + 1 + m + 2 * i)
                    for k in range(FT):
                        if k % (FT // 2) == 0:
                            pe.wait_ge(lo_done, halves_before(f, FT + m) + 1 + k // (FT // 2) + 4 * i)
                        if type(i) is int and m == 0 and k in (0, FT - 1):
                            pe.wait_ge(act_split, FT * (f + 1) + 2 - (k == 0))
                        ins = block_product(bank(4 + slot, T), slot, k * P, act_hi[:, k * T:(k + 1) * T],
                                            act_lo[:, k * T:(k + 1) * T], k == 0, k == FT - 1)
                    ins.then_inc(dn_done, 1)

                gate_up(0, 0, 0)
                norm(NORM_FFN[f])
                gate_up(1, 1, 0)
                with pe.Fori(1, FT // 2) as i:
                    gate_up(0, 0, i)
                    gate_up(1, 1, i)
                down(0, 0, 0)
                down(1, 1, 0)
                with pe.Fori(1, KT // 2) as i:
                    down(0, 0, i)
                    down(1, 1, i)

            def project_out(base_dn, base_x):
                for m in range(KT):
                    n = base_dn + m // 2
                    if m % 2 == 0:
                        pe.wait_ge(dn_loaded[n % 2], 16 * (n // 2 + 1))
                    pe.wait_ge(x_upd, base_x + 1 + m)
                    for k in range(KT):
                        ins = mm(bank(4 + m % 2, T), dn[:, n % 2, k * 256 + (m % 2) * P:k * 256 + (m % 2) * P + P],
                                 oT[:, k, :], start=(k == 0), stop=(k == KT - 1))
                    ins.then_inc((dn_half, dn_done)[m % 2], 1)

            def project_in(n, t, h_lo_, evac):
                for j in range(2):
                    if t + j >= 4:
                        pe.wait_ge(evac, t + j - 3)
                    for k in range(KT):
                        if k % 4 == 0:
                            pe.wait_ge(mix_lo, mix_halves(n) + 2 * j + k // 4 + 1)
                        if t + j == 0:
                            pe.wait_ge(h_ready, KT * (NORM_EV if n < GU_OD else NORM_OD) + k + 1)
                        w_hi, w_lo = (w_mix[:, j, part, k * P:(k + 1) * P] for part in range(2))
                        out = bank((t + j) % 4, T)
                        mm(out, w_hi, h_hi[:, k, :], start=(k == 0), stop=False)
                        mm(out, w_hi, h_lo_[:, k, :], start=False, stop=False)
                        ins = mm(out, w_lo, h_hi[:, k, :], start=False, stop=(k == KT - 1))
                        if k == 3:
                            ins.then_inc(mix_half, 1)
                    ins.then_inc((gu_half, gu_done)[j], 1)

            def even():
                pe.wait_ge(x_upd, X_EV + 2)
                pe.wait_ge(caches_in, 16 * 5)
                for p in range(A_PAIRS):
                    for kt in range(4):
                        ins = tr(bank(p)[:, kt * P:(kt + 1) * P], kcn[:, kt, p * P:(p + 1) * P], ident[:, :])
                    ins.then_inc(s["kct_pe"], 1)
                for kt in range(4):
                    ins = tr(bank(7)[0:IDX_D, kt * P:(kt + 1) * P], ipn[:, kt, :], ident[:, :])
                ins.then_inc(s["kct_pe"], 1)
                norm(NORM_EV)
                pe.wait_ge(s["kct_evac"], 5)
                for l in range(len(EV_LOADS)):
                    project_in(GU_EV + l, 2 * l, h_lo_even, s["ev_evac"])
                    if l == 2:
                        key_token_rows()
                    if l == 4:
                        raw_scores_x()
                    if l == 5:
                        combine_x()
                    if l == 6:
                        raw_scores_y()
                    if l == 7:
                        combine_y()
                    if l == 8:
                        head_sums(s["qsq"], s["comb_used"], 2, s["qsum"])
                    if l == 10:
                        head_sums(s["ksq"], s["qk_read"], 1, s["ksum"])
                    if l == 12:
                        gate()
                token_rows()
                gla()
                attention()
                pe.wait_ge(s["ob_ready"], 4)
                pe.wait_ge(s["pv_evac"], 5)
                project_out(DN_EV, X_EV)

            def key_token_rows():
                pe.wait_ge(s["ev_evac"], T_KI + 1)
                for i in range(3):
                    rows = P if i < 2 else TS
                    ins = tr(bank(7)[0:rows, i * 68:(i + 1) * 68], pr[0:68, T_KI, i * P:i * P + rows], ident[0:68, 0:68])
                ins.then_inc(s["kw_pe"], 1)

            def raw_scores_x():
                pe.wait_ge(s["idx_prep"], 1)
                for b, bk in ((3, 4), (2, 5)):
                    for p in range(IDX_PAIRS):
                        ins = mm(bank(bk)[:, p * 256:p * 256 + CH * (b + 1)], qibd[:, b, p, :], kiT[:, 0:CH * (b + 1)],
                                 start=True, stop=True)
                ins.then_inc(s["raw"], 1)

            def weigh(b, out, rrow, done=None):
                for p in range(IDX_PAIRS):
                    ins = mm(out, dwi[:, 2 * b + p, :], rrow(p), start=(p == 0), stop=(p == 1))
                if done is not None:
                    ins.then_inc(done, 1)

            def combine_x():
                pe.wait_ge(s["raw_used"], 1)
                pe.wait_ge(s["dwi_ready"], 1)
                weigh(3, bank(7)[CH:P, 0:256], lambda p: rX3[:, p, :])
                weigh(2, bank(7)[0:CH, 0:192], lambda p: rX2[:, p, :], s["comb"])

            def raw_scores_y():
                for p in range(IDX_PAIRS):
                    mm(bank(4)[:, p * 128:(p + 1) * 128], qibd[:, 1, p, :], kiT[:, 0:128], start=True, stop=True)
                    mm(bank(5 + p), qibd[:, 4, p, :], kiT[:, TP:TP + 512], start=True, stop=True)
                    ins = mm(bank(4)[:, 256 + 64 * p:320 + 64 * p], qibd[:, 4, p, :], kiT[:, TP + 512:TP + NK_S],
                             start=True, stop=True)
                ins.then_inc(s["raw"], 1)

            def combine_y():
                pe.wait_ge(s["raw_used"], 2)
                pe.wait_ge(s["comb_used"], 1)
                weigh(4, bank(7)[CH:P, :], lambda p: rYS[:, p, 0:512])
                weigh(4, bank(4)[CH:P, 0:64], lambda p: rYS[:, p, 512:NK_S])
                weigh(1, bank(4)[0:CH, 128:256], lambda p: rY1[:, p, :], s["comb"])

            def head_sums(squared, free, n_free, done):
                pe.wait_ge(free, n_free)
                for p in range(4):
                    pe.wait_ge(squared, p + 1)
                    ins = mm(bank(4 + p, T), halves[:, :], sqE[:, p, :], start=True, stop=True)
                ins.then_inc(done, 1)

            def gate():
                pe.wait_ge(s["qk_read"], 2)
                for j in range(2):
                    ins = mm(bank(4 + j, T), w2[0:B_RANK, j * P:(j + 1) * P], pr[0:B_RANK, T_AB, :], start=True, stop=True)
                ins.then_inc(s["gate_pe"], 1)

            def token_rows():
                pe.wait_ge(s["ev_evac"], N_EV)
                pe.wait_ge(s["k_ready"], 4)
                pe.wait_ge(s["gate_used"], 1)
                for name, first, src, done in (("v", 0, T_V, s["vtr"]), ("k", 4, T_K, s["ktr"])):
                    for i in range(3):
                        rows = P if i < 2 else TS
                        for p in range(4):
                            ins = tr(bank(first + i)[0:rows, p * P:(p + 1) * P], pr[:, src + p, i * P:i * P + rows],
                                     ident[:, :])
                        ins.then_inc(done, 1)

            def gla():
                pe.wait_ge(s["q_ready"], 8)
                pe.wait_ge(s["vtok_evac"], 3)
                for u in range(10):
                    p, c = divmod(u, NCH)
                    ins = tr(PS[:, u * P:(u + 1) * P], vbx[:, p, c, :],
                             ident[:, :])
                ins.then_inc(s["vp_pe"], 1)
                pe.wait_ge(s["bds_ready"], 1)
                pe.wait_ge(s["ktok_evac"], 3)
                for u in range(10):
                    ins = tr(PS[:, 1536 + u * P:1536 + (u + 1) * P], kl_bd[:, u // NCH, u % NCH, :], ident[:, :])
                ins.then_inc(s["kl_pe"], 1)
                pe.wait_ge(s["bds_ready"], 2)
                for u in range(10):
                    p, c = divmod(u, NCH)
                    ins = mm(PS[:, 3072 + u * CH:3072 + (u + 1) * CH], km_bd[:, p, c, :], qm[:, p, c * CH:(c + 1) * CH],
                             start=True, stop=True)
                ins.then_inc(s["ga_pe"], 1)
                pe.wait_ge(s["vp_evac"], 1)
                pe.wait_ge(s["kl_evac"], 1)
                for u in range(10):
                    ins = mm(PS[:, u * P:(u + 1) * P], kl_bd[:, u // NCH, u % NCH, :], vp[:, u, :], start=True, stop=True)
                ins.then_inc(s["su_pe"], 1)
                pe.wait_ge(s["abd_ready"], 1)
                pe.wait_ge(s["sg_ready"], 1)
                pe.wait_ge(s["bds_ready"], 3)
                for u in range(10):
                    p, c = divmod(u, NCH)
                    mm(PS[:, 1536 + u * P:1536 + (u + 1) * P], vp[:, u, :], km_bd[:, p, c, :], start=True, stop=False)
                    ins = mm(PS[:, 1536 + u * P:1536 + (u + 1) * P], Sg(c if c < 4 else 5)[:, p, :], qe_bd[:, p, c, :],
                             start=False, stop=True)
                ins.then_inc(s["go_pe"], 1)
                pe.wait_ge(s["gsq"], 1)
                for u in range(10):
                    ins = mm(bank(7)[:, u:u + 1], view(RA, 3840 + 1280 + u * P, P), ones[:, 0:1], start=True, stop=True)
                ins.then_inc(s["gsum"], 1)

            def gla_rstd():
                pe.wait_ge(s["grstd"], 1)
                pe.wait_ge(s["go_evac"], 2)
                for u in range(10):
                    ins = mm(PS[:, 2048 + u * P:2048 + (u + 1) * P], gcol[:, u:u + 1].to_broadcast([P, P]), ident[:, :],
                             start=True, stop=True)
                ins.then_inc(s["gspread"], 1)

            def attention():
                PTB = [[4], [5], [4, 5], [4, 5]]
                PVB = [6, 7, 6, 7]

                def scores(b):
                    if b == 3:
                        pe.wait_ge(s["l_done"], 2)
                    for p in range(A_PAIRS):
                        ins = mm(raw_logit(b)[:, p, :], qbd[:, b, p, :], pr[:, T_K + p, 0:CH * (b + 1)],
                                 start=True, stop=True)
                    ins.then_inc(s["qk_pe"], 1)

                def turn(b):
                    if b == 0:
                        pe.wait_ge(s["gnormed"], 1)
                    pe.wait_ge(s["p_ready"], b + 1)
                    if b in (2, 3):
                        pe.wait_ge(s["pt_evac"], b)
                    nk = CH * (b + 1)
                    for kt, bk in enumerate(PTB[b]):
                        w = min(P, nk - kt * P)
                        for p in range(A_PAIRS):
                            ins = tr(bank(bk)[0:w, p * P:(p + 1) * P], logit(b)[:, p, kt * P:kt * P + w], ident[:, :])
                    ins.then_inc(s["pt_pe"], 1)

                def values(b):
                    pe.wait_ge(s["pt_evac"], b + 1)
                    if b in (2, 3):
                        pe.wait_ge(s["pv_evac"], b - 1)
                    nk = CH * (b + 1)
                    kts = range((nk + P - 1) // P)
                    for p in range(A_PAIRS):
                        for kt in kts:
                            w = min(P, nk - kt * P)
                            ins = mm(bank(PVB[b])[:, p * P:(p + 1) * P], vtok[0:w, kt, p * P:(p + 1) * P],
                                     pT[0:w, pt_slot(b) + kt, p * P:(p + 1) * P], start=(kt == 0), stop=(kt == kts[-1]))
                    ins.then_inc(s["pv_pe"], 1)

                def scores_sample(part):
                    if part == 0:
                        pe.wait_ge(s["l_done"], 4)
                        for p in range(A_PAIRS):
                            mm(bank(p), qbd[:, 4, p, :], kcT[:, p, :], start=True, stop=True)
                    else:
                        pe.wait_ge(s["pt_evac"], 4)
                        for p in range(A_PAIRS):
                            ins = mm(bank(4)[:, p * 64:(p + 1) * 64], qbd[:, 4, p, :], pr[:, T_K + p, TP:T],
                                     start=True, stop=True)
                        ins.then_inc(s["qk_pe"], 1)

                def turn_sample(p):
                    pe.wait_ge(s["p_ready"], 5 + p)
                    if p == 0:
                        pe.wait_ge(s["pv_evac"], 4)
                    elif p >= 2:
                        pe.wait_ge(s["pt_evac"], 3 + p)
                    for kt in range(5):
                        w = P if kt < 4 else TS
                        out = bank(p)[:, kt * P:(kt + 1) * P] if kt < 4 else bank(5 + p % 2)[0:TS, 0:P]
                        ins = tr(out, logit(4)[:, p, kt * P:kt * P + w], ident[:, :])
                    ins.then_inc(s["pt_pe"], 1)

                def values_sample(p):
                    pe.wait_ge(s["pt_evac"], 5 + p)
                    for kt in range(5):
                        v = vcache[:, kt, p * P:(p + 1) * P] if kt < 4 else vtok[0:TS, 2, p * P:(p + 1) * P]
                        ins = mm(bank(7)[:, p * P:(p + 1) * P], v, pT[0:P if kt < 4 else TS, kt, p * P:(p + 1) * P],
                                 start=(kt == 0), stop=(kt == 4))
                    if p == A_PAIRS - 1:
                        ins.then_inc(s["pv_pe"], 1)

                scores(0)
                scores(1)
                scores(2)
                gla_rstd()
                scores(3)
                turn(0)
                turn(1)
                values(0)
                values(1)
                turn(2)
                values(2)
                turn(3)
                scores_sample(0)
                values(3)
                scores_sample(1)
                turn_sample(0)
                turn_sample(1)
                values_sample(0)
                turn_sample(2)
                values_sample(1)
                turn_sample(3)
                values_sample(2)
                values_sample(3)

            def odd():
                for l in range(16):
                    project_in(GU_OD + l, 2 * l, h_lo_odd, o["evac"])
                    if l == 0:
                        gates()
                    if l == 2:
                        gate_columns()
                    if l == 3:
                        gate_rows(0)
                    if l == 5:
                        gate_rows(1)
                    if l in SUMS_AFTER:
                        key_sums(SUMS_AFTER.index(l))
                    if l in RSTD_AFTER:
                        key_rstd(RSTD_AFTER.index(l))
                    if l == 15:
                        key_products((0,))
                key_products(range(1, NCH))
                first_inverse()
                value_rows(range(4))
                for level in range(5):
                    double_inverse(level)
                value_rows((4,))
                recurrence()
                pe.wait_ge(o["og"], NCH)
                project_out(DN_OD, X_OD)

            def gates():
                pe.wait_ge(o["ab_in"], 48)
                for k in range(KT):
                    for part, h in ((0, h_hi), (1, h_lo_odd)):
                        ins = mm(bank(4, T)[0:40, :], wab[:, k, :], h[:, k, :].bitcast(F32),
                                 start=(k + part == 0), stop=(k == KT - 1 and part == 1))
                ins.then_inc(o["ab_pe"], 1)

            def gate_columns():
                pe.wait_ge(o["g_rows"], 1)
                for w in range(2):
                    for c in range(NCH):
                        at = (w * NCH + c) * 8
                        ins = tr(bank(6)[0:CH, at:at + 8], growv(2 + w)[0:C_H, c * CH:(c + 1) * CH], ident[0:C_H, 0:C_H])
                ins.then_inc(o["col_pe"], 1)

            def gate_rows(half):
                if half == 0:
                    pe.wait_ge(o["cols_ready"], 1)
                else:
                    pe.wait_ge(o["row_used"], 1)
                    pe.wait_ge(o["eg"], 1)
                    pe.wait_ge(o["recip"], 1)
                for h in range(4):
                    ins = mm(bank(4 + h, T), ident[0:C_H, 4 * half + h:4 * half + h + 1].to_broadcast([C_H, P]),
                             growv(2)[0:C_H, :], start=True, stop=True)
                ins.then_inc(o["row_pe"], 1)

            def key_sums(g):
                pe.wait_ge(o["row_used"], min(g, 1) + 1)
                pe.wait_ge(o["eg"], min(g, 1) + 1)
                if g:
                    pe.wait_ge(o["recip"], g)
                pe.wait_ge(o["sq"], g + 1)
                for u in range(10):
                    ins = mm(bank(7)[:, 10 * g + u:10 * g + u + 1], sq4[:, u * P:(u + 1) * P], ones[:, 0:1],
                             start=True, stop=True)
                ins.then_inc(o["sum"], 1)

            def key_rstd(g):
                pe.wait_ge(o["rstd"], g + 1)
                if g == 0:
                    pe.wait_ge(o["row_used"], 2)
                    pe.wait_ge(o["eg"], 2)
                else:
                    pe.wait_ge(o["kq_ready"], g)
                for u in range(10):
                    ins = mm(PS[:, 2048 + u * P:2048 + (u + 1) * P], hcol[:, g, u:u + 1].to_broadcast([P, P]),
                             ident[:, :], start=True, stop=True)
                ins.then_inc(o["spread"], 1)

            def kview(p, c):
                return cv[:, 1, p, c, :]

            def qview(p, c):
                return cv[:, 0, p, c, :]

            def key_products(chunks):
                pe.wait_ge(o["kq_ready"], 4)
                for c in chunks:
                    b = product_bank(c)
                    if c == 1:
                        pe.wait_ge(o["evac"], N_OD)
                    if c >= 2:
                        pe.wait_ge(o["kk_used"], 2 * (c - 1))
                        pe.wait_ge(o["kt_evac"], c - 1)
                    for p in range(C_PAIRS):
                        mm(bank(b)[:, p * P:(p + 1) * P], kview(p, c), kview(p, c), start=True, stop=True)
                        mm(bank(b + 1)[:, p * P:(p + 1) * P], kview(p, c), qview(p, c), start=True, stop=True)
                        ins = tr(bank(b + 2)[:, p * P:(p + 1) * P], kview(p, c), ident[:, :])
                    ins.then_inc(o["kk_pe"], 1)

            def first_inverse():
                for c in range(NCH):
                    pe.wait_ge(o["t1"], c + 1)
                    if c == 0:
                        pe.wait_ge(o["kt_evac"], NCH)
                    else:
                        pe.wait_ge(o["u1_evac"], c)
                    for p in range(C_PAIRS):
                        ins = tr(bank(7)[:, p * P:(p + 1) * P], tT[:, c, p, :], ident[:, :])
                    ins.then_inc(o["u1_pe"], 1)

            def double_inverse(level):
                def y(c):
                    m = level * NCH + c
                    pe.wait_ge(o["bm"], m + 1)
                    if m >= 2:
                        pe.wait_ge(o["y_evac"], m - 1)
                    if level:
                        pe.wait_ge(o["u_upd"], m - NCH + 1)
                    for p in range(C_PAIRS):
                        ins = mm(bank(4 + m % 2)[:, p * P:(p + 1) * P], Dm[:, c, p, :], uT[:, c, p, :], start=True, stop=True)
                    ins.then_inc(o["y_pe"], 1)

                def tu(c):
                    m = level * NCH + c
                    pe.wait_ge(o["y_evac"], m + 1)
                    if level:
                        pe.wait_ge(o["t_upd"], m - NCH + 1)
                    if level < 4:
                        if m:
                            pe.wait_ge(o["t_upd"], m)
                        for p in range(C_PAIRS):
                            ins = mm(bank(6)[:, p * P:(p + 1) * P], yT[:, c, p, :], tT[:, c, p, :], start=True, stop=True)
                        ins.then_inc(o["t_pe"], 1)
                    if m:
                        pe.wait_ge(o["u_upd"], m)
                    for p in range(C_PAIRS):
                        ins = mm(bank(7)[:, p * P:(p + 1) * P], tT[:, c, p, :], yT[:, c, p, :], start=True, stop=True)
                    ins.then_inc(o["u_pe"], 1)

                if level == 0:
                    pe.wait_ge(o["u1_evac"], NCH)
                y(0)
                y(1)
                for c in range(NCH):
                    tu(c)
                    if c + 2 < NCH:
                        y(c + 2)

            def value_rows(chunks):
                for c in chunks:
                    if c == 0:
                        pe.wait_ge(o["evac"], N_OD)
                        pe.wait_ge(o["silu"], 24)
                    if c == 4:
                        pe.wait_ge(o["vt_evac"], 1)
                    for p in range(C_PAIRS):
                        ins = tr(bank(c % 4)[:, p * P:(p + 1) * P], cv[:, 2, p, c, :], ident[:, :])
                    ins.then_inc(o["vt_pe"], 1)

            def out_sums(n_):
                pe.wait_ge(o["osq"], n_ + 1)
                for p in range(C_PAIRS):
                    ins = mm(bank(7)[:, 4 * n_ + p:4 * n_ + p + 1], sqO[:, p * P:(p + 1) * P], ones[:, 0:1],
                             start=True, stop=True)
                ins.then_inc(o["osum"], 1)

            def out_rstd(n_):
                pe.wait_ge(o["orstd"], n_ + 1)
                if n_:
                    pe.wait_ge(o["og"], n_)
                for p in range(C_PAIRS):
                    ins = mm(bank(5)[:, p * P:(p + 1) * P], ocol[:, n_, p:p + 1].to_broadcast([P, P]), ident[:, :],
                             start=True, stop=True)
                ins.then_inc(o["osp"], 1)

            def recurrence():
                pe.wait_ge(o["u_upd"], 5 * NCH)
                pe.wait_ge(o["vt_evac"], NCH)
                pe.wait_ge(o["qe"], C_PAIRS)
                pe.wait_ge(o["zero_v"], 1)
                pe.wait_ge(o["states"], 1)
                pe.wait_ge(o["ds_in"], 16)
                for n_, c in enumerate(CHUNK_ORDER):
                    S = state_before(c)
                    if n_:
                        pe.wait_ge(o["r_ready"], n_)
                    if n_ > 1:
                        pe.wait_ge(o["s_upd"], n_ if n_ > 2 else 1)
                    for p in range(C_PAIRS):
                        for par in range(2):
                            ins = mm(bank(0)[par * CH:(par + 1) * CH, p * P:(p + 1) * P],
                                     cv[:, 1, p, c, par * CH:(par + 1) * CH], S[:, 2 * p + par, :],
                                     start=True, stop=True)
                    ins.then_inc(o["ks_pe"], 1)
                    if n_:
                        out_sums(n_ - 1)
                    pe.wait_ge(o["r_ready"], n_ + 1)
                    for p in range(C_PAIRS):
                        ins = mm(bank(1)[:, p * P:(p + 1) * P], uT[:, c, p, :], Rr[:, p, :], start=True, stop=True)
                    ins.then_inc(o["vn_pe"], 1)
                    pe.wait_ge(o["vn_evac"], n_ + 1)
                    if n_:
                        pe.wait_ge(o["s_upd"], n_)
                    for p in range(C_PAIRS):
                        ins = mm(bank(3 + p // 2)[:, (p % 2) * 256:(p % 2) * 256 + 256], Kl[:, c, p, :],
                                 vnew[:, p, :, :], start=True, stop=True)
                    ins.then_inc(o["s_pe"], 1)
                    if n_:
                        out_rstd(n_ - 1)
                    if n_:
                        pe.wait_ge(o["osq"], n_)
                    for p in range(C_PAIRS):
                        for par in range(2):
                            out = bank(2)[:, p * P + par * CH:p * P + (par + 1) * CH]
                            mm(out, S[:, 2 * p + par, :], cv[:, 0, p, c, par * CH:(par + 1) * CH],
                               start=True, stop=False)
                            ins = mm(out, vnew[:, p, par, :], At[:, c, p, par * CH:(par + 1) * CH],
                                     start=False, stop=True)
                    ins.then_inc(o["o_pe"], 1)
                out_sums(NCH - 1)
                for t in range(24):
                    if t == 0:
                        pe.wait_ge(o["s_upd"], NCH)
                    b, at = (t // 4, t % 4) if t < 16 else (6 + (t - 16) // 4, t % 4)
                    if t == 20:
                        pe.wait_ge(o["orecip"], NCH)
                    ins = tr(bank(b)[0:6, at * P:(at + 1) * P], cst[:, t, :], ident[:, :])
                ins.then_inc(o["cs_pe"], 1)
                out_rstd(NCH - 1)

            def epilogue():
                pe.wait_ge(x_upd, X_FFN[3] + 2 + KT)
                for i in range(3):
                    rows = P if i < 2 else TS
                    for half in range(2):
                        for k in range(4):
                            ins = tr(bank(2 * i + half)[0:rows, k * P:(k + 1) * P],
                                     xT[:, 4 * half + k, i * P:i * P + rows], ident[:, :])
                        ins.then_inc(pro_pe, 1)

            prologue()
            ffn(0)
            even()
            ffn(1)
            ffn(2)
            norm(NORM_OD)
            odd()
            ffn(3)
            epilogue()

        @block.scalar
        def _(sc):
            act_ = sc.activation
            steps = [0]

            def link(ins):
                steps[0] += 1
                ins.then_inc(act_step, 1)
                sc.wait_ge(act_step, steps[0])

            def copy(out, in_, scale=1.0):
                return act_(out, in_, ACT.Copy, scale=scale)

            def prologue():
                rows = [(0, 32, 0, I["ffn_norm"].rearrange("a b (k p) -> (a b k) p", p=P)),
                        (32, 48, 0, I["mix_norm"].rearrange("a (k p) -> (a k) p", p=P)),
                        (48, 49, 0, I["ev_gla_norm"]), (49, 50, 0, I["od_norm"]),
                        (50, 52, 0, I["ev_gate_b2"].rearrange("a (k p) -> (a k) p", p=P)),
                        (0, 96, P, I["od_conv_w"][0].rearrange("j (k p) -> (j k) p", p=P)),
                        (0, 72, 2 * P, I["state_conv"][0, 0].rearrange("j (k p) -> (j k) p", p=P))]
                for r0, r1, at, src in rows:
                    sc.dma_start(rs[r0:r1, at:at + P], src).then_inc(params_in, 16)
                for row, name in ((C_QN, "ev_q_norm"), (C_KN, "ev_k_norm")):
                    for par in range(2):
                        sc.dma_start(rs[row:row + 1, par * A_D:(par + 1) * A_D], I[name]).then_inc(params_in, 16)
                sc.dma_start(rbT[0:A_H, :], I["rel_bias"].rearrange("b h -> h b"),
                             allow_slow_non_contiguous=True).then_inc(small_in, 16)
                sc.dma_start(cols[0:C_H, 222:223], I["od_a_log"].rearrange("a h -> h a")).then_inc(small_in, 16)
                sc.dma_start(cols[0:C_H, 223:224], I["od_dt_bias"].rearrange("a h -> h a")).then_inc(small_in, 16)
                for i in range(3):
                    n_ = P if i < 2 else TS
                    for half in range(2):
                        sc.wait_ge(pro_pe, 2 * i + half + 1)
                        copy(xT[:, 4 * half:4 * half + 4, i * P:i * P + n_],
                             bank(2 * i + half).rearrange("p (k c) -> p k c", k=4)[:, :, 0:n_]).then_inc(pro_evac, 1)
                sc.wait_ge(pro_pe, 7)
                copy(cols[:, 0:222], bank(6, 222)).then_inc(pro_evac, 1)

            def rsqrt(out, in_, scale, read=None):
                ins = act_(out, in_, ACT.Ln, scale=scale, bias=eps_col)
                if read is None:
                    link(ins)
                else:
                    sem_, count = read
                    ins.then_inc(sem_, 1)
                    sc.wait_ge(sem_, count)
                return act_(out, out, ACT.Exp, scale=-0.5)

            def root(r):
                sc.wait_ge(norm_sum, r + 1)
                rsqrt(rstd, bank(6, T), 1.0 / D).then_inc(norm_rstd, 1)

            def split_gate_up(f, slot, c, i):
                n = GU_FFN[f] + c
                sc.wait_ge(gu_loaded[slot], 32 * (n // 2) + 32 + 32 * i)
                if type(i) is not int or c >= 2:
                    sc.wait_ge(gu_done, n - 1 + 2 * i)
                elif f == 2:
                    sc.wait_ge(dn_done, DN_FFN[1] + KT - 1 + c)
                elif f:
                    if f == 1:
                        sc.wait_ge(s["pv_evac"], NCH)
                        sc.wait_ge(s["ob_ready"], 4)
                        sc.wait_ge(out_sem, 16 * 8)
                    else:
                        sc.wait_ge(o["og"], NCH)
                        sc.wait_ge(out_sem, 16 * 12)
                for j in range(2):
                    copy(w_parts[:, slot, 0, j * 1024:(j + 1) * 1024], gu[:, slot, j * 1024:(j + 1) * 1024])\
                        .then_inc(hi_done, 1)

            def split_down(f, slot, m, i):
                n = DN_FFN[f] + m
                sc.wait_ge(dn_loaded[slot], 16 * (n // 2) + 16 + 16 * i)
                if type(i) is not int or m >= 2:
                    sc.wait_ge(dn_done, n - 1 + 2 * i)
                else:
                    sc.wait_ge(gu_done, GU_FFN[f] + FT - 1 + m)
                for j in range(2):
                    w = slice(j * FT * P // 2, (j + 1) * FT * P // 2)
                    copy(w_parts[:, slot, 0, w], dn[:, slot, w]).then_inc(hi_done, 1)

            def split_mix(n, t):
                j = t % 2
                sc.wait_ge(gu_loaded[n % 2], 32 * (n // 2 + 1))
                if t < 2:
                    sc.wait_ge(lo_done, halves_before(1 if n < GU_OD else 3, 0))
                raw = gu[:, n % 2, :].rearrange("p (k c) -> p k c", k=KT)[:, :, j * P:(j + 1) * P]
                for half in range(2):
                    if t >= 2 and half == 0:
                        sc.wait_ge(mix_half, t - 1 + (0 if n < GU_OD else N_EV))
                    elif t >= 2:
                        sc.wait_ge((gu_half, gu_done)[j], n)
                    copy(w_mix[:, j, 0, half * 512:(half + 1) * 512].rearrange("p (k c) -> p k c", k=4),
                         raw[:, 4 * half:4 * half + 4, :]).then_inc(mix_hi, 1)

            def h_high(r, h32):
                for k in range(KT):
                    sc.wait_ge(h_made, KT * (r // 3) + k + 1)
                    copy(h_hi[:, k, :], h32[:, k, :]).then_inc(h_hi_done, 1)

            def ffn(f, gain, x_base):
                def tanh(slot, c, i):
                    sc.wait_ge(scaled, FT * f + 1 + c + 2 * i)
                    act_(tanh_g[:, slot, :], gated[:, slot, :], ACT.Tanh, scale=0.5).then_inc(tanh_done, 1)

                if f == 0:
                    sc.wait_ge(pro_evac, 7)
                sc.wait_ge(x_upd, x_base + 2)
                for k in range(KT):
                    copy(h_hi[:, k, :], xT[:, k, :], cols[:, gain + k:gain + k + 1]).then_inc(h_hi_done, 1)
                if f == 0:
                    for j in range(4):
                        act_(squares[:, 2 * j:2 * j + 2, :], xT[:, 2 * j:2 * j + 2, :], ACT.Square).then_inc(sq_done, 1)
                split_gate_up(f, 1, 1, 0)
                root(NORM_FFN[f])
                tanh(0, 0, 0)
                with sc.Fori(0, FT // 2 - 1) as i:
                    split_gate_up(f, 0, 2, i)
                    tanh(1, 1, i)
                    split_gate_up(f, 1, 3, i)
                    tanh(0, 2, i)
                split_down(f, 0, 0, 0)
                tanh(1, FT - 1, 0)
                split_down(f, 1, 1, 0)
                with sc.Fori(1, KT // 2) as i:
                    split_down(f, 0, 0, i)
                    split_down(f, 1, 1, i)
                if f == 1:
                    split_gate_up(2, 0, 0, 0)

            def even():
                split_mix(GU_EV, 0)
                split_mix(GU_EV, 1)
                for p in range(A_PAIRS):
                    sc.wait_ge(s["kct_pe"], p + 1)
                    copy(kcT[:, p, :], bank(p)).then_inc(s["kct_evac"], 1)
                sc.wait_ge(s["kct_pe"], 5)
                copy(kiT[0:IDX_D, TP:TP + PAST], bank(7)[0:IDX_D, :])
                copy(kiT[IDX_D:P, TP:TP + PAST], bank(7)[0:IDX_D, :]).then_inc(s["kct_evac"], 1)
                root(NORM_EV)
                h_high(NORM_EV, h32_even)
                for l, tiles in enumerate(EV_LOADS):
                    for j, done in ((0, gu_half), (1, gu_done)):
                        t, w = 2 * l + j, tiles[j][1]
                        if t + 2 < N_EV:
                            split_mix(GU_EV + l + 1, t + 2)
                        sc.wait_ge(done, GU_EV + l + 1)
                        if T_VB <= t < T_VB + 4:
                            dst = vbx[:, (t - T_VB) // 2, :, (t % 2) * CH:(t % 2 + 1) * CH]
                            copy(dst, bank(t % 4, T).rearrange("p (c t) -> p c t", t=CH)).then_inc(s["ev_evac"], 1)
                        else:
                            copy(pr[0:w, t, :], bank(t % 4, T)[0:w, :]).then_inc(s["ev_evac"], 1)
                    if l == 4:
                        sc.wait_ge(s["raw"], 1)
                        act_(rX3, bank(4).rearrange("p (a c) -> p a c", a=2), ACT.Relu)
                        act_(rX2, bank(5).rearrange("p (a c) -> p a c", a=2)[:, :, 0:192], ACT.Relu)\
                            .then_inc(s["raw_used"], 1)
                    if l == 5:
                        for p in range(4):
                            sc.wait_ge(s["ev_evac"], T_Q + p + 1)
                            act_(sqE[:, p, :], pr[:, T_Q + p, :], ACT.Square).then_inc(s["qsq"], 1)
                    if l == 6:
                        sc.wait_ge(s["raw"], 2)
                        for p in range(IDX_PAIRS):
                            act_(rYS[:, p, 0:512], bank(5 + p), ACT.Relu)
                            act_(rYS[:, p, 512:NK_S], bank(4)[:, 256 + 64 * p:320 + 64 * p], ACT.Relu)
                        act_(rY1, bank(4, 256).rearrange("p (a c) -> p a c", a=2), ACT.Relu).then_inc(s["raw_used"], 1)
                    if l == 9:
                        sc.wait_ge(s["qsum"], 1)
                        for p in range(4):
                            act_(sqE[:, p, :], pr[:, T_K + p, :], ACT.Square).then_inc(s["ksq"], 1)
                        rsqrt(view(rs, 0, 4, T), banks(4, 4, T), 1.0 / A_D, (s["qk_read"], 1)).then_inc(s["qk_rstd"], 1)
                    if l == 11:
                        sc.wait_ge(s["ksum"], 1)
                        sc.wait_ge(s["q_ready"], 8)
                        rsqrt(view(rs, 0, 4, T), banks(4, 4, T), 1.0 / A_D, (s["qk_read"], 2)).then_inc(s["qk_rstd"], 1)
                    if l == 13:
                        sc.wait_ge(s["g_neg"], 1)
                        link(act_(gx2, gx2, ACT.Exp))
                        act_(gx2, gx2, ACT.Ln, bias=1.0).then_inc(s["g_ln"], 1)
                sc.wait_ge(s["g_args"], 1)
                k_ = 1.0 / B_TAU
                for out, in_, k_ in ((gdl, gdl, k_), (e_mid_n, gdm, -k_), (gdm, gdm, k_), (e_b, gB, k_),
                                     (es, gB.rearrange("p a (c t) -> p a c t", t=CH)[:, :, :, CH - 1], k_)):
                    act_(out, in_, ACT.Exp, scale=k_).then_inc(s["g_exps"], 1)
                for name, dst, first in (("v", vtok, 0), ("k", ktok, 4)):
                    for i in range(3):
                        n_ = P if i < 2 else TS
                        sc.wait_ge(s[name + "tr"], i + 1)
                        copy(dst[0:n_, i, :], bank(first + i)[0:n_, :]).then_inc(s[name + "tok_evac"], 1)
                sc.wait_ge(s["vp_pe"], 1)
                copy(vp, PS[:, 0:1280].rearrange("p (u e) -> p u e", e=P)).then_inc(s["vp_evac"], 1)
                sc.wait_ge(s["kl_pe"], 1)
                copy(kl_bd, PS[:, 1536:2816].rearrange("p (a c e) -> p a c e", a=2, e=P)).then_inc(s["kl_evac"], 1)
                sc.wait_ge(s["go_pe"], 1)
                for p in range(B_PAIRS):
                    copy(oT[:, 4 + 2 * p:6 + 2 * p, :].rearrange("p a (c t) -> p c a t", t=CH),
                         PS[:, 1536 + 640 * p:2176 + 640 * p].rearrange("p (c a t) -> p c a t", a=2, t=CH))\
                        .then_inc(s["go_evac"], 1)
                sc.wait_ge(s["go_evac"], 2)
                act_(sqE, oT[:, 4:8, :], ACT.Square).then_inc(s["gsq"], 1)
                act_(kl_bd.rearrange("p a c e -> p (a c e)"), pr[:, T_RB:T_RB + 4, :].rearrange("p a b -> p (a b)"),
                     ACT.Tanh, scale=0.5).then_inc(s["sil_t"], 1)
                sc.wait_ge(s["grecip"], 1)
                act_(gcol, gcol, ACT.Sqrt).then_inc(s["grstd"], 1)

                def exps(b):
                    sc.wait_ge(s["nmx"], b + 1)
                    for p in range(A_PAIRS):
                        ins = act_(logit(b)[:, p, :], logit(b)[:, p, :], ACT.Exp, bias=mx[:, b, 1, p:p + 1],
                                   accum_out=mx[:, b, 2, p:p + 1])
                    ins.then_inc(s["exps_done"], 1)

                def turned(b):
                    sc.wait_ge(s["pt_pe"], b + 1)
                    if b >= 2:
                        sc.wait_ge(s["pv_pe"], b - 1)
                    nk = CH * (b + 1)
                    for kt, bk in enumerate([[4], [5], [4, 5], [4, 5]][b]):
                        w = min(P, nk - kt * P)
                        ins = copy(pT[0:w, pt_slot(b) + kt, :], bank(bk)[0:w, :])
                    ins.then_inc(s["pt_evac"], 1)

                def exps_sample(p):
                    sc.wait_ge(s["nmx"], 5 + p)
                    act_(logit(4)[:, p, :], logit(4)[:, p, :], ACT.Exp, bias=mx[:, 4, 1, p:p + 1],
                         accum_out=mx[:, 4, 2, p:p + 1]).then_inc(s["exps_done"], 1)

                def turned_sample(p):
                    sc.wait_ge(s["pt_pe"], 5 + p)
                    sc.wait_ge(s["pv_pe"], 4)
                    copy(pT[:, 0:4, p * P:(p + 1) * P], bank(p).rearrange("p (k q) -> p k q", k=4))
                    copy(pT[0:TS, 4, p * P:(p + 1) * P], bank(5 + p % 2)[0:TS, 0:P]).then_inc(s["pt_evac"], 1)

                exps(0)
                exps(1)
                exps(2)
                sc.wait_ge(s["ob_ready"], 4)
                turned(0)
                turned(1)
                turned(2)
                exps(3)
                turned(3)
                exps_sample(0)
                exps_sample(1)
                turned_sample(0)
                exps_sample(2)
                turned_sample(1)
                exps_sample(3)
                turned_sample(2)
                turned_sample(3)

            def odd():
                def tile_out(t):
                    if t + 2 < N_OD:
                        split_mix(GU_OD + t // 2 + 1, t + 2)
                    done = (gu_half, gu_done)[t % 2]
                    sc.wait_ge(done, GU_OD + t // 2 + 1)
                    if OD_TILES[t] < 24:
                        i = CONV_AT.index(t)
                        if i >= 4:
                            sc.wait_ge(o["conv"], i - 3)
                        copy(qp[:, i % 4, 3:259], bank(t % 4, TP))
                        copy(qp[:, i % 4, 262:326], bank(t % 4)[:, TP:T]).then_inc(o["evac"], 1)
                    else:
                        copy(zT[:, OD_TILES[t] - 24, :], bank(t % 4, T)).then_inc(o["evac"], 1)

                def silu_tanh(t):
                    sc.wait_ge(o["conv"], t + 1)
                    if t >= 2:
                        sc.wait_ge(o["silu"], t - 1)
                    act_(th2[:, t % 2, :], cring[:, t % 4, :], ACT.Tanh, scale=0.5).then_inc(o["th"], 1)

                def square(g):
                    sc.wait_ge(o["silu"], 4 * g + 4)
                    if g:
                        sc.wait_ge(o["sum"], g)
                    act_(sq4, group(g), ACT.Square).then_inc(o["sq"], 1)

                def root(g):
                    sc.wait_ge(o["recip"], g + 1)
                    act_(hcol[:, g, :], hcol[:, g, :], ACT.Sqrt).then_inc(o["rstd"], 1)

                def gates():
                    sc.wait_ge(small_in, 48)
                    act_(cols[0:C_H, 224:225], cols[0:C_H, 222:223], ACT.Exp)
                    sc.wait_ge(o["g1"], 1)
                    act_(growv(3)[0:C_H, :], growv(3)[0:C_H, :], ACT.Exp)
                    link(act_(growv(1)[0:C_H, :], growv(1)[0:C_H, :], ACT.Exp))
                    act_(growv(1)[0:C_H, :], growv(1)[0:C_H, :], ACT.Ln, bias=1.0).then_inc(o["g2"], 1)

                tanhs = 0
                for t in range(N_OD):
                    if t in (8, 12):
                        half = t // 4 - 2
                        sc.wait_ge(o["row_pe"], half + 1)
                        act_(expG[:, 4 * half:4 * half + 4, :], banks(4, 4, T), ACT.Exp).then_inc(o["eg"], 1)
                    tile_out(t)
                    if t == 1:
                        gates()
                    seen = sum(c <= t for c in CONV_AT)
                    if tanhs < seen - (2 if OD_TILES[t] < 24 else 0):
                        silu_tanh(tanhs)
                        tanhs += 1
                    if t == 7:
                        sc.wait_ge(o["cols_ready"], 1)
                        act_(egc, colG[:, 0, :, :], ACT.Exp).then_inc(o["gexp"], 1)
                    if t == 15:
                        sc.wait_ge(o["row_used"], 2)
                        act_(es8, gl, ACT.Exp)
                        act_(klc, klc, ACT.Exp)
                        act_(Dm, Dm, ACT.Exp, scale=-1.0)
                        act_(At, At, ACT.Exp).then_inc(o["dexp"], 1)
                    if t in (11, 17, 24, 29):
                        root((11, 17, 24, 29).index(t))
                    if t in (9, 14, 21, 24):
                        square((9, 14, 21, 24).index(t))
                assert tanhs == 24
                for c in range(NCH):
                    sc.wait_ge(o["kk_pe"], c + 1)
                    for p in range(C_PAIRS):
                        ins = copy(Kl[:, c, p, :], bank(product_bank(c) + 2)[:, p * P:(p + 1) * P], klc[:, c, p:p + 1])
                    ins.then_inc(o["kt_evac"], 1)
                sc.wait_ge(o["qe"], C_PAIRS)
                for c in range(NCH):
                    sc.wait_ge(o["u1_pe"], c + 1)
                    copy(uT[:, c, :, :], bank(7).rearrange("p (a c) -> p a c", a=4)).then_inc(o["u1_evac"], 1)
                for level in range(5):
                    for c in range(NCH):
                        m = level * NCH + c
                        sc.wait_ge(o["y_pe"], m + 1)
                        if level:
                            sc.wait_ge(o["u_pe"], m - NCH + 1)
                        copy(yT[:, c, :, :], bank(4 + m % 2).rearrange("p (a c) -> p a c", a=4)).then_inc(o["y_evac"], 1)
                sc.wait_ge(o["bm"], 25)
                for c in range(NCH):
                    sc.wait_ge(o["vt_pe"], c + 1)
                    for p in range(C_PAIRS):
                        ins = copy(Vb[:, c, p, :], bank(c % 4)[:, p * P:(p + 1) * P], bhalf[:, c, p:p + 1])
                    ins.then_inc(o["vt_evac"], 1)
                sc.wait_ge(o["u_pe"], 5 * NCH)
                act_(zth, zT, ACT.Tanh, scale=0.5).then_inc(o["zt"], 1)

                def root_out(n_):
                    sc.wait_ge(o["orecip"], n_ + 1)
                    act_(ocol[:, n_, :], ocol[:, n_, :], ACT.Sqrt).then_inc(o["orstd"], 1)

                for n_, c in enumerate(CHUNK_ORDER):
                    sc.wait_ge(o["vn_pe"], n_ + 1)
                    if n_:
                        sc.wait_ge(o["o_pe"], n_)
                    for par in range(2):
                        h = slice(par * CH, (par + 1) * CH)
                        ins = copy(vnew[h, :, par, :], bank(1)[h, :].rearrange("p (a e) -> p a e", a=4))
                    ins.then_inc(o["vn_evac"], 1)
                    if n_:
                        root_out(n_ - 1)
                        sc.wait_ge(o["osum"], n_)
                    sc.wait_ge(o["o_pe"], n_ + 1)
                    copy(oT[:, :, c * CH:(c + 1) * CH], bank(2).rearrange("p (h t) -> p h t", t=CH))
                    act_(sqO, bank(2), ACT.Square).then_inc(o["osq"], 1)
                root_out(NCH - 1)
                sc.wait_ge(o["cs_pe"], 1)
                copy(csr[0:6, 0:2048], PS[0:6, 0:2048])
                copy(csr[0:6, 2048:3072], PS[0:6, 3072:4096]).then_inc(o["cs_evac"], 1)

            def epilogue():
                for i in range(3):
                    n_ = P if i < 2 else TS
                    for half in range(2):
                        sc.wait_ge(pro_pe, 7 + 2 * i + half + 1)
                        copy(ytok[0:n_, i, half * 512:(half + 1) * 512], bank(2 * i + half)[0:n_, :])\
                            .then_inc(pro_evac, 1)

            prologue()
            split_gate_up(0, 0, 0, 0)
            ffn(0, C_FFN, 0)
            even()
            split_gate_up(1, 0, 0, 0)
            ffn(1, C_FFN + 8, X_FFN[1])
            ffn(2, C_FFN + 16, X_FFN[2])
            split_mix(GU_OD, 0)
            split_mix(GU_OD, 1)
            root(NORM_OD)
            h_high(NORM_OD, h32_odd)
            odd()
            split_gate_up(3, 0, 0, 0)
            ffn(3, C_FFN + 24, X_FFN[3])
            epilogue()

        @block.vector
        def _(ve):
            tt, ts, stt, cp = ve.tensor_tensor, ve.tensor_scalar, ve.scalar_tensor_tensor, ve.tensor_copy
            steps = [0]

            def link(ins):
                steps[0] += 1
                ins.then_inc(dve_step, 1)
                ve.wait_ge(dve_step, steps[0])

            def wait_rstd(r):
                ve.wait_ge(norm_rstd, r + 1)

            def norm(r, gain, h32, h_lo_):
                wait_rstd(r)
                for k in range(KT + 1):
                    if k < KT:
                        stt(h32[:, k, :], xT[:, k, :], cols[:, gain + k:gain + k + 1], rstd, ALU.mult, ALU.mult)\
                            .then_inc(h_made, 1)
                    if k:
                        ve.wait_ge(h_hi_done, KT * r + k)
                        tt(h_lo_[:, k - 1, :], h32[:, k - 1, :], h_hi[:, k - 1, :].bitcast(F32), ALU.subtract)\
                            .then_inc(h_ready, 1)

            def split(f, raw, slot, c, i):
                for j in range(2):
                    half = raw[:, slot, j * raw.shape[2] // 2:(j + 1) * raw.shape[2] // 2]
                    w = slice(j * raw.shape[2] // 2, (j + 1) * raw.shape[2] // 2)
                    ve.wait_ge(hi_done, halves_before(f, c) + 1 + j + 4 * i)
                    tt(w_parts[:, slot, 1, w], half, w_parts[:, slot, 0, w].bitcast(F32), ALU.subtract).then_inc(lo_done, 1)

            def ffn(f, gain):
                act_hi_32 = act_hi[:, :].bitcast(F32)
                mids = (2 * FT + KT) * f

                def activate(slot, c, i):
                    n = FT * f + c + 2 * i
                    ve.wait_ge(act_split, n + 1)
                    ve.wait_ge(gu_half, GU_FFN[f] + 1 + c + 2 * i)
                    tt(gated[:, slot, :], bank(2 * slot, T), rstd, ALU.mult).then_inc(scaled, 1)
                    ve.wait_ge(tanh_done, n + 1)
                    stt(gated[:, slot, :], tanh_g[:, slot, :], 1.0, gated[:, slot, :], ALU.add, ALU.mult)\
                        .then_inc(act_mid, 1)
                    ve.wait_ge(act_mid, mids + 1 + 2 * c + 4 * i)
                    ve.wait_ge(gu_done, GU_FFN[f] + 1 + c + 2 * i)
                    tt(gated[:, slot, :], gated[:, slot, :], bank(2 * slot + 1, T), ALU.mult).then_inc(act_done, 1)
                    ve.wait_ge(act_done, n + 3)
                    cols_ = slice(c * T, (c + 1) * T) if type(i) is int else bass.ds(2 * T * i + T * c, T)
                    cp(act_hi[:, cols_], gated[:, slot, :]).then_inc(act_mid, 1)
                    ve.wait_ge(act_mid, mids + 2 + 2 * c + 4 * i)
                    tt(act_lo[:, cols_], gated[:, slot, :], act_hi_32[:, cols_], ALU.subtract).then_inc(act_split, 1)

                def residual(slot, m, i):
                    ve.wait_ge(dn_done, DN_FFN[f] + 1 + m + 2 * i)
                    tt(tanh_g[:, slot, :], bank(4 + slot, T), rstd, ALU.mult).then_inc(act_mid, 1)
                    ve.wait_ge(act_mid, mids + 2 * FT + 1 + m + 2 * i)
                    xm = xf[:, m * T:(m + 1) * T] if type(i) is int else xf[:, bass.ds(2 * T * i + T * m, T)]
                    stt(xm, tanh_g[:, slot, :], 0.25, xm, ALU.mult, ALU.add).then_inc(x_upd, 1)

                xf = xT[:, :, :].rearrange("p k t -> p (k t)")
                for k in range(KT):
                    ve.wait_ge(h_hi_done, KT * NORM_FFN[f] + k + 1)
                    stt(h_lo[:, k, :], xT[:, k, :], cols[:, gain + k:gain + k + 1], h_hi[:, k, :].bitcast(F32),
                        ALU.mult, ALU.subtract).then_inc(h_ready, 1)
                split(f, gu, 1, 1, 0)
                wait_rstd(NORM_FFN[f])
                activate(0, 0, 0)
                with ve.Fori(0, FT // 2 - 1) as i:
                    split(f, gu, 0, 2, i)
                    activate(1, 1, i)
                    split(f, gu, 1, 3, i)
                    activate(0, 2, i)
                split(f, dn, 0, FT, 0)
                activate(1, FT - 1, 0)
                with ve.Fori(0, KT // 2 - 1) as i:
                    split(f, dn, 1, FT + 1, i)
                    residual(0, 0, i)
                    split(f, dn, 0, FT + 2, i)
                    residual(1, 1, i)
                split(f, dn, 1, FT + KT - 1, 0)
                residual(0, KT - 2, 0)
                if f == 1:
                    split(2, gu, 0, 0, 0)
                residual(1, KT - 1, 0)

            def residual(base_dn):
                for m in range(KT):
                    ve.wait_ge((dn_half, dn_done)[m % 2], half_count(base_dn, m))
                    tt(xT[:, m, :], bank(4 + m % 2, T), xT[:, m, :], ALU.add).then_inc(x_upd, 1)

            def half_count(base_dn, m):
                if m % 2:
                    return base_dn + m // 2 + 1
                return (4 if base_dn == DN_OD else 0) + m // 2 + 1

            def even():
                norm(NORM_EV, C_MIX, h32_even, h_lo_even)
                ve.wait_ge(s["ev_evac"], 3)
                ve.wait_ge(s["zero"], 1)
                for h in (slice(0, IDX_D), slice(IDX_D, P)):
                    cp(kiT[h, 0:TP], pr[0:IDX_D, T_KI, 0:TP])
                    cp(kiT[h, TP + PAST:TP + NK_S], pr[0:IDX_D, T_KI, TP:T])
                for par in range(2):
                    h = slice(par * IDX_D, (par + 1) * IDX_D)
                    for p in range(IDX_PAIRS):
                        ins = cp(qibd[h, :, p, par * CH:(par + 1) * CH],
                                 pr[h, T_QI + p, :].rearrange("p (c t) -> p c t", t=CH))
                ins.then_inc(s["idx_prep"], 1)
                ve.wait_ge(s["kw_pe"], 1)
                cp(kwtok[:, 0:2, :], bank(7, 136).rearrange("p (a c) -> p a c", a=2))
                ins = cp(kwtok[0:TS, 2, :], bank(7)[0:TS, 136:204])
                ins.then_inc(s["kw_evac"], 1)
                ve.wait_ge(s["kw_evac"], 1)
                for par in range(2):
                    h = slice(par * CH, (par + 1) * CH)
                    for bp in range(2):
                        cp(wcol[h, bp:4:2, :], kwtok[bp * CH:(bp + 1) * CH, 0:2, IDX_D + par:IDX_D + IDX_H:2])
                    ins = cp(wcol[h, 4, :], kwtok[0:CH, 2, IDX_D + par:IDX_D + IDX_H:2])
                link(ins)
                tt(dwi, istk.unsqueeze(1).to_broadcast([P, 10, CH]),
                   wcol.rearrange("p c a -> p (c a)").unsqueeze(2).to_broadcast([P, 10, CH]), ALU.mult)\
                    .then_inc(s["dwi_ready"], 1)

                def take8(work, rounds):
                    for _ in range(rounds):
                        link(ve.max(top8, work))
                        link(ve.match_replace(work, top8, work, TAKEN))

                def penalty(pen, work):
                    ts(pen[0:CH, :], work, TAKEN, -BIG, ALU.not_equal, ALU.mult)
                    return ts(pen[CH:P, :], work, TAKEN, -BIG, ALU.not_equal, ALU.mult)

                ve.memset(workX[0:CH, 192:256], PADDED)
                ve.memset(workY[0:CH, 128:NK_S], PADDED)
                ve.wait_ge(s["comb"], 1)
                cp(workX[CH:P, :], bank(7)[CH:P, 0:256])
                cp(workX[0:CH, 0:192], bank(7)[0:CH, 0:192]).then_inc(s["comb_used"], 1)
                ve.wait_ge(s["comb_used"], 1)
                take8(workX, TOP_P // 8)
                penalty(pen3, workX[CH:P, :])
                penalty(pen2, workX[0:CH, 0:192])
                ve.wait_ge(s["comb"], 2)
                cp(workY[CH:P, 0:512], bank(7)[CH:P, :])
                cp(workY[CH:P, 512:NK_S], bank(4)[CH:P, 0:64])
                cp(workY[0:CH, 0:128], bank(4)[0:CH, 128:256]).then_inc(s["comb_used"], 1)
                ve.wait_ge(s["comb_used"], 2)
                take8(workY, TOP_P // 8)
                penalty(pen1, workY[0:CH, 0:128])

                left = TOP_S // 8 - TOP_P // 8
                take8(workY, left // 2)
                ve.wait_ge(s["qk_rstd"], 1)
                ve.wait_ge(s["zero"], 2)
                for p in range(A_PAIRS):
                    for par in range(2):
                        h = slice(par * A_D, (par + 1) * A_D)
                        ins = stt(qbd[h, :, p, par * CH:(par + 1) * CH],
                                  pr[h, T_Q + p, :].rearrange("p (c t) -> p c t", t=CH), cols[h, C_QN:C_QN + 1],
                                  rs[h, p * T:(p + 1) * T].rearrange("p (c t) -> p c t", t=CH), ALU.mult, ALU.mult)
                        ins.then_inc(s["q_ready"], 1)
                take8(workY, left - left // 2)
                link(penalty(penS, workY[CH:P, :]))
                ve.wait_ge(s["qk_rstd"], 2)
                for p in range(A_PAIRS):
                    stt(pr[:, T_K + p, :], pr[:, T_K + p, :], cols[:, C_KN:C_KN + 1], rs[:, p * T:(p + 1) * T],
                        ALU.mult, ALU.mult).then_inc(s["k_ready"], 1)
                ve.wait_ge(s["gate_pe"], 1)
                for j in range(2):
                    ins = ts(gx[:, j, :], bank(4 + j, T), cols[:, C_B2 + j:C_B2 + j + 1], None, ALU.add)
                ins.then_inc(s["gate_used"], 1)
                ve.wait_ge(s["gate_used"], 1)
                stt(gx2, gx, -1.0, gx, ALU.mult, ALU.min).then_inc(s["g_neg"], 1)
                ve.wait_ge(s["g_ln"], 1)
                link(stt(gx, gx, 0.0, gx2, ALU.min, ALU.subtract))
                for p in range(B_PAIRS):
                    for c in range(NCH):
                        w = slice(c * CH, (c + 1) * CH)
                        ins = ve.tensor_tensor_scan(gB[:, p, w], ones[:, 0:CH], gx[:, p, w], 0.0, ALU.mult, ALU.add)
                link(ins)
                g4 = gB.rearrange("p a (c t) -> p (a c) t", t=CH)
                tt(gdm.rearrange("p a (c t) -> p (a c) t", t=CH), g4, g4[:, :, CH // 2:CH // 2 + 1].to_broadcast([P, 10, CH]),
                   ALU.subtract)
                tt(gdl.rearrange("p a (c t) -> p (a c) t", t=CH), g4[:, :, CH - 1:CH].to_broadcast([P, 10, CH]), g4,
                   ALU.subtract).then_inc(s["g_args"], 1)
                ve.wait_ge(s["zero"], 3)

                def bds(dst, src, factor, exps, scale=1.0):
                    ve.wait_ge(s["g_exps"], exps)
                    for par in range(2):
                        h = slice(par * B_K, (par + 1) * B_K)
                        for p in range(B_PAIRS):
                            ins = stt(dst[h, p, :, par * CH:(par + 1) * CH],
                                      pr[h, src + p, :].rearrange("p (c t) -> p c t", t=CH), scale,
                                      factor[h, p, :].rearrange("p (c t) -> p c t", t=CH), ALU.mult, ALU.mult)
                    return ins

                bds(kl_bd, T_KB, gdl, 1).then_inc(s["bds_ready"], 1)
                bds(km_bd, T_KB, e_mid_n, 2)
                ve.wait_ge(s["g_exps"], 3)
                stt(qm, pr[:, T_QB:T_QB + 2, :], B_K ** -0.5, gdm, ALU.mult, ALU.mult).then_inc(s["bds_ready"], 1)
                bds(qe_bd, T_QB, e_b, 4, B_K ** -0.5).then_inc(s["bds_ready"], 1)
                ve.wait_ge(s["ga_pe"], 1)
                kmu = km_bd.rearrange("p a c e -> p (a c) e")
                for par in range(2):
                    h = slice(par * B_K, (par + 1) * B_K)
                    ins = tt(kmu[h, :, par * CH:(par + 1) * CH], PS[h, 3072:3712].rearrange("p (u t) -> p u t", t=CH),
                             causal[h, :].unsqueeze(1).to_broadcast([CH, 10, CH]), ALU.mult)
                ins.then_inc(s["abd_ready"], 1)
                ve.wait_ge(s["su_pe"], 1)
                ve.wait_ge(caches_in, 16 * 5)
                ve.wait_ge(s["g_exps"], 5)
                link(ve.memset(Sg(0), 0.0))
                for c in (4, 0, 1, 2, 3):
                    src, dst = (5, 6) if c == 4 else (c, c + 1)
                    for p in range(B_PAIRS):
                        u = p * NCH + c
                        ins = stt(Sg(dst)[:, p, :], Sg(src)[:, p, :], es[:, p, c:c + 1], PS[:, u * P:(u + 1) * P],
                                  ALU.mult, ALU.add)
                    if c < 3 or c == 4:
                        link(ins)
                ins.then_inc(s["sg_ready"], 1)
                ve.wait_ge(s["gsum"], 1)
                link(ts(gcol, bank(7, 10), 1.0 / B_V, EPS, ALU.mult, ALU.add))
                ve.reciprocal(gcol, gcol).then_inc(s["grecip"], 1)
                th = kl_bd.rearrange("p a c e -> p (a c e)")
                ve.wait_ge(s["sil_t"], 1)
                stt(th, th, 1.0, pr[:, T_RB:T_RB + 4, :].rearrange("p a b -> p (a b)"), ALU.add, ALU.mult)

                def gla_out():
                    ve.wait_ge(s["gspread"], 1)
                    stt(oT[:, 4:8, :], oT[:, 4:8, :], cols[:, C_GLA:C_GLA + 1], view(PS, 2048, 4, T), ALU.mult, ALU.mult)\
                        .then_inc(s["gnormed"], 1)
                    ve.wait_ge(s["gnormed"], 1)
                    for h in range(4):
                        stt(oT[:, 4 + h, :], oT[:, 4 + h, :], 0.5, th[:, h * T:(h + 1) * T], ALU.mult, ALU.mult)\
                            .then_inc(s["ob_ready"], 1)

                def logits(b):
                    ve.wait_ge(s["qk_pe"], b + 1)
                    if b == 3:
                        ve.wait_ge(s["pt_pe"], 2)
                    L = logit(b)
                    nk = CH * (b + 1)
                    ins = stt(L, raw_logit(b), A_D ** -0.5, biasT[:, :, PAST - CH * b:NK_S], ALU.mult, ALU.add)
                    ins.then_inc(s["l_done"], 1)
                    ve.wait_ge(s["l_done"], b + 1)
                    if b:
                        pen = (None, pen1, pen2, pen3)[b]
                        link(tt(L, L, pen.unsqueeze(1).to_broadcast([P, A_PAIRS, nk]), ALU.add))
                    link(ve.tensor_reduce(mx[:, b, 0, :], L, AX, ALU.max))
                    ts(mx[:, b, 1, :], mx[:, b, 0, :], -1.0, None, ALU.mult).then_inc(s["nmx"], 1)

                def logits_sample(p):
                    if p == 0:
                        ve.wait_ge(s["qk_pe"], 5)
                        ve.wait_ge(s["pt_pe"], 4)
                    L = logit(4)[:, p, :]
                    stt(L[:, 0:512], bank(p), A_D ** -0.5, biasT[:, p, 0:512], ALU.mult, ALU.add)
                    stt(L[:, 512:NK_S], bank(4)[:, p * TS:(p + 1) * TS], A_D ** -0.5, biasT[:, p, 512:NK_S], ALU.mult,
                        ALU.add).then_inc(s["l_done"], 1)
                    ve.wait_ge(s["l_done"], 5 + p)
                    link(tt(L, L, penS, ALU.add))
                    link(ve.tensor_reduce(mx[:, 4, 0, p:p + 1], L, AX, ALU.max))
                    ts(mx[:, 4, 1, p:p + 1], mx[:, 4, 0, p:p + 1], -1.0, None, ALU.mult).then_inc(s["nmx"], 1)

                def probs_sample(p):
                    ve.wait_ge(s["exps_done"], 5 + p)
                    link(ve.reciprocal(mx[:, 4, 0, p:p + 1], mx[:, 4, 2, p:p + 1]))
                    ts(logit(4)[:, p, :], logit(4)[:, p, :], mx[:, 4, 0, p:p + 1], None, ALU.mult)\
                        .then_inc(s["p_ready"], 1)

                def probs(b):
                    nk = CH * (b + 1)
                    ve.wait_ge(s["exps_done"], b + 1)
                    link(ve.reciprocal(mx[:, b, 0, :], mx[:, b, 2, :]))
                    tt(logit(b), logit(b), mx[:, b, 0, :].unsqueeze(2).to_broadcast([P, A_PAIRS, nk]), ALU.mult)\
                        .then_inc(s["p_ready"], 1)

                def heads_out(b):
                    ve.wait_ge(s["pv_pe"], b + 1)
                    for par in range(2):
                        h = slice(par * A_D, (par + 1) * A_D)
                        ins = cp(oT[h, 0:4, b * CH:(b + 1) * CH],
                                 bank((6, 7, 6, 7, 7)[b])[h, :].rearrange("p (a c) -> p a c", a=4)
                                 [:, :, par * CH:(par + 1) * CH])
                    ins.then_inc(s["pv_evac"], 1)

                ve.wait_ge(s["bias_in"], 32)
                logits(0)
                logits(1)
                logits(2)
                gla_out()
                probs(0)
                probs(1)
                probs(2)
                logits(3)
                heads_out(0)
                heads_out(1)
                probs(3)
                heads_out(2)
                heads_out(3)
                logits_sample(0)
                logits_sample(1)
                probs_sample(0)
                logits_sample(2)
                probs_sample(1)
                logits_sample(3)
                probs_sample(2)
                probs_sample(3)
                heads_out(4)
                split(1, gu, 0, 0, 0)
                residual(DN_EV)

            def odd():
                g = [growv(i)[0:C_H, :] for i in range(4)]
                link(ve.memset(qp[:, :, 0:3], 0.0))
                ve.wait_ge(small_in, 48)
                ve.wait_ge(o["ab_pe"], 1)
                ts(g[3], bank(4, T)[32:32 + C_H, :], -80.0, -1.0, ALU.max, ALU.mult)
                link(ts(g[0], bank(4, T)[0:C_H, :], cols[0:C_H, 223:224], None, ALU.add))
                stt(g[1], g[0], -1.0, g[0], ALU.mult, ALU.min).then_inc(o["g1"], 1)
                ve.wait_ge(o["g2"], 1)
                link(ts(g[3], g[3], 1.0, None, ALU.add))
                ve.reciprocal(g[3], g[3])
                link(stt(g[0], g[0], 0.0, g[1], ALU.max, ALU.add))
                link(ts(g[0], g[0], cols[0:C_H, 224:225], -1.0, ALU.mult, ALU.mult))
                for c in range(NCH):
                    w = slice(c * CH, (c + 1) * CH)
                    ins = ve.tensor_tensor_scan(g[2][:, w], ones[0:C_H, 0:CH], g[0][:, w], 0.0, ALU.mult, ALU.add)
                ins.then_inc(o["g_rows"], 1)

                def conv(t):
                    tile_ = OD_TILES[CONV_AT[t]]
                    buf = qp[:, t % 4, :]
                    ve.wait_ge(o["evac"], CONV_AT[t] + 1)
                    cp(cst[:, tile_, 0:3], buf[:, 256:259])
                    cp(cst[:, tile_, 3:6], buf[:, 323:326])
                    link(cp(buf[:, 259:262], cols[:, C_ST + tile_:C_ST + 72:24]))
                    c_ = cring[:, t % 4, :]
                    link(ts(c_, buf[:, 0:323], cols[:, C_CONV + tile_:C_CONV + tile_ + 1], None, ALU.mult))
                    for j in range(1, 4):
                        at = C_CONV + 24 * j + tile_
                        ins = stt(c_, buf[:, j:j + 323], cols[:, at:at + 1], c_, ALU.mult, ALU.add)
                        if j < 3:
                            link(ins)
                    ins.then_inc(o["conv"], 1)

                def silu(t):
                    ve.wait_ge(o["th"], t + 1)
                    part, h = OD_TILES[CONV_AT[t]] // 8, OD_TILES[CONV_AT[t]] % 8
                    dst = cv[:, part, h // 2, :, (h % 2) * CH:(h % 2 + 1) * CH]
                    for c0, c1, at in ((0, 4, 0), (4, 5, TP + 3)):
                        ins = stt(dst[:, c0:c1, :], th2[:, t % 2, at:at + CH * (c1 - c0)].rearrange("p (c t) -> p c t", t=CH),
                                  1.0, cring[:, t % 4, at:at + CH * (c1 - c0)].rearrange("p (c t) -> p c t", t=CH),
                                  ALU.add, ALU.mult)
                    ins.then_inc(o["silu"], 1)

                def columns():
                    ve.wait_ge(o["col_pe"], 1)
                    for par in range(2):
                        ins = cp(colG[par * CH:(par + 1) * CH, :, :, :].rearrange("p w c a -> p (w c) a"),
                                 bank(6, 80)[0:CH, :].rearrange("p (u h) -> p u h", h=8)[:, :, par:8:2])
                    ins.then_inc(o["cols_ready"], 1)
                    ve.wait_ge(o["cols_ready"], 1)
                    ts(bhalf, colG[:, 1, :, :], 0.5, None, ALU.mult)

                def differences(half):
                    ve.wait_ge(o["eg"], half + 1)
                    if half == 0:
                        ve.wait_ge(o["masks"], 1)
                    cp(gl[:, 4 * half:4 * half + 4, :],
                       banks(4, 4, T).rearrange("p h (c t) -> p h c t", t=CH)[:, :, :, CH - 1])
                    for pp in range(2):
                        p = 2 * half + pp
                        for c in range(NCH):
                            row = banks(4 + 2 * pp, 2, T)[:, :, c * CH:(c + 1) * CH]
                            for dst, mask in ((At, maskI), (Dm, maskS)):
                                ins = stt(dst[:, c, p, :].rearrange("p (a t) -> p a t", a=2), row, colG[:, 0, c, p:p + 1],
                                          mask.rearrange("p (a t) -> p a t", a=2), ALU.subtract, ALU.add)
                    if half == 1:
                        link(ins)
                        for par in range(2):
                            h = slice(par * CH, (par + 1) * CH)
                            ins = tt(klc[h, :, :], gl[h, par:8:2, :].rearrange("p a c -> p c a"), colG[h, 0, :, :],
                                     ALU.subtract)
                    ins.then_inc(o["row_used"], 1)

                def head_rstd(g_):
                    ve.wait_ge(o["sum"], g_ + 1)
                    link(ts(hcol[:, g_, :], bank(7)[:, 10 * g_:10 * g_ + 10], 0.25, EPS, ALU.mult, ALU.add))
                    ve.reciprocal(hcol[:, g_, :], hcol[:, g_, :]).then_inc(o["recip"], 1)

                def unit_heads(g_):
                    ve.wait_ge(o["spread"], g_ + 1)
                    scale = 0.5 if g_ < 2 else 0.5 * C_D ** -0.5
                    c_ = group(g_)
                    stt(c_, c_, scale, PS[:, 2048:2048 + 4 * T], ALU.mult, ALU.mult).then_inc(o["kq_ready"], 1)
                    ve.wait_ge(o["kq_ready"], g_ + 1)

                silus = 0
                for t in range(24):
                    conv(t)
                    ready = t + 1 if t in (3, 7, 23) else t - 1
                    while silus < ready:
                        silu(silus)
                        silus += 1
                    if t == 3:
                        columns()
                    if t in (3, 7):
                        differences((3, 7).index(t))
                    if t in (5, 10, 17, 21):
                        head_rstd((5, 10, 17, 21).index(t))
                    if t in (11, 14, 21, 22):
                        unit_heads((11, 14, 21, 22).index(t))
                ve.wait_ge(o["gexp"], 1)
                stt(ncol, egc, -1.0, colG[:, 1, :, :], ALU.mult, ALU.mult)
                ve.wait_ge(o["dexp"], 1)
                for c in range(NCH):
                    ve.wait_ge(o["kk_pe"], c + 1)
                    for p in range(C_PAIRS):
                        ins = stt(Lm[:, c, p, :], bank(product_bank(c))[:, p * P:(p + 1) * P], colG[:, 1, c, p:p + 1], Dm[:, c, p, :],
                                  ALU.mult, ALU.mult)
                    ins.then_inc(o["kk_used"], 1)
                    tt(At[:, c, :, :], bank(product_bank(c) + 1).rearrange("p (a c) -> p a c", a=4), At[:, c, :, :], ALU.mult)\
                        .then_inc(o["kk_used"], 1)
                ve.wait_ge(o["eg"], 2)
                for p in range(C_PAIRS):
                    c_ = cv[:, 0, p, :, :].rearrange("p c (a t) -> p c a t", a=2)
                    tt(c_, c_, expG[:, 2 * p:2 * p + 2, :].rearrange("p a (c t) -> p c a t", t=CH), ALU.mult)\
                        .then_inc(o["qe"], 1)
                for c in range(NCH):
                    ve.wait_ge(o["kk_used"], 2 * NCH)
                    link(tt(tT[:, c, :, :], Lm[:, c, :, :], lev[:, 0:1, :].to_broadcast([P, C_PAIRS, P]), ALU.mult))
                    tt(tT[:, c, :, :], ident[:, :].unsqueeze(1).to_broadcast([P, C_PAIRS, P]), tT[:, c, :, :],
                       ALU.subtract).then_inc(o["t1"], 1)
                for level in range(5):
                    for c in range(NCH):
                        m = level * NCH + c
                        ve.wait_ge(o["u_pe"], m + 1)
                        if level == 0:
                            ve.wait_ge(o["t1"], NCH)
                            ve.wait_ge(o["u1_evac"], NCH)
                        if level < 4:
                            ve.wait_ge(o["t_pe"], m + 1)
                            tt(tT[:, c, :, :], tT[:, c, :, :], bank(6).rearrange("p (a c) -> p a c", a=4), ALU.subtract)\
                                .then_inc(o["t_upd"], 1)
                        tt(uT[:, c, :, :], uT[:, c, :, :], bank(7).rearrange("p (a c) -> p a c", a=4), ALU.subtract)\
                            .then_inc(o["u_upd"], 1)
                def out_norm(n_):
                    ve.wait_ge(o["osum"], n_ + 1)
                    link(ts(ocol[:, n_, :], bank(7)[:, 4 * n_:4 * n_ + 4], 1.0 / C_D, EPS, ALU.mult, ALU.add))
                    ve.reciprocal(ocol[:, n_, :], ocol[:, n_, :]).then_inc(o["orecip"], 1)

                def out_gate(n_):
                    w = slice(CHUNK_ORDER[n_] * CH, (CHUNK_ORDER[n_] + 1) * CH)
                    ve.wait_ge(o["osp"], n_ + 1)
                    link(stt(oT[:, :, w], oT[:, :, w], cols[:, C_OD:C_OD + 1],
                             bank(5).rearrange("p (h t) -> p h t", t=CH), ALU.mult, ALU.mult))
                    stt(oT[:, :, w], oT[:, :, w], 0.5, zth[:, :, w], ALU.mult, ALU.mult).then_inc(o["og"], 1)

                ve.wait_ge(o["states"], 1)
                for n_, c in enumerate(CHUNK_ORDER):
                    ve.wait_ge(o["ks_pe"], n_ + 1)
                    ve.wait_ge(o["vt_evac"], NCH)
                    if n_:
                        ve.wait_ge(o["vn_pe"], n_)
                    for p in range(C_PAIRS):
                        ins = stt(Rr[:, p, :], bank(0)[:, p * P:(p + 1) * P], ncol[:, c, p:p + 1], Vb[:, c, p, :],
                                  ALU.mult, ALU.add)
                    ins.then_inc(o["r_ready"], 1)
                    if n_:
                        out_norm(n_ - 1)
                    ve.wait_ge(o["s_pe"], n_ + 1)
                    if n_ > 1:
                        ve.wait_ge(o["s_upd"], n_)
                    for h in range(C_H):
                        ins = stt(state_after(c)[:, h, :], state_before(c)[:, h, :], es8[:, h, c:c + 1],
                                  bank(3 + h // 4)[:, (h % 4) * P:(h % 4 + 1) * P], ALU.mult, ALU.add)
                    ins.then_inc(o["s_upd"], 1)
                    if n_ == 0:
                        ve.wait_ge(o["zt"], 1)
                        link(stt(zth, zth, 1.0, zT, ALU.add, ALU.mult))
                    else:
                        out_gate(n_ - 1)
                out_norm(NCH - 1)
                out_gate(NCH - 1)
                split(3, gu, 0, 0, 0)
                residual(DN_OD)

            ve.sem_inc(x_upd, 2)
            ve.sem_inc(act_done, 2)
            ve.sem_inc(act_split, 2)
            split(0, gu, 0, 0, 0)
            ffn(0, C_FFN)
            even()
            ffn(1, C_FFN + 8)
            ffn(2, C_FFN + 16)
            norm(NORM_OD, C_MIX + 8, h32_odd, h_lo_odd)
            odd()
            ffn(3, C_FFN + 24)

        @block.gpsimd
        def _(po):
            steps = [0]

            def link(ins):
                steps[0] += 1
                ins.then_inc(pool_step, 1)
                po.wait_ge(pool_step, steps[0])

            def store(dst, src):
                po.dma_start(dst, src).then_inc(out_sem, 16)

            sel = po.affine_select
            po.memset(ones[:, :], 1.0)
            po.memset(eps_col, EPS)
            link(po.memset(ident[:, :], 0.0))
            sel(out=ident[:, :], in_=ident[:, :], compare_op=ALU.not_equal, fill=1.0, base=0, pattern=[[-1, P]],
                channel_multiplier=1).then_inc(consts, 1)
            po.memset(halves, 0.0)
            po.memset(istk, 0.0)
            link(po.memset(causal, 1.0))
            po.memset(halves[0:64, 0:64], 1.0)
            po.memset(halves[64:P, 64:P], 1.0)
            for par in range(2):
                h = slice(par * CH, (par + 1) * CH)
                sel(out=causal[h, :], in_=causal[h, :], compare_op=ALU.is_ge, fill=0.0, base=0, pattern=[[1, CH]],
                    channel_multiplier=-1)
                ins = sel(out=istk[h, :], in_=istk[h, :], compare_op=ALU.not_equal, fill=1.0, base=0,
                          pattern=[[-1, CH]], channel_multiplier=1)
            link(ins)
            po.wait_ge(small_in, 48)
            for b, lo, hi in bucket_runs():
                ins = po.tensor_copy(biasrow[0:A_H, lo + REL0:hi + REL0 + 1],
                                     rbT[0:A_H, b:b + 1].to_broadcast([A_H, hi - lo + 1]))
            link(ins)
            po.dma_start(scratch, biasrow[0:A_H, :].unsqueeze(1).to_broadcast([A_H, CH, REL_N])).then_inc(s["bias_out"], 16)
            po.wait_ge(s["bias_out"], 16)
            for par in range(2):
                src = bass.AP(scratch.tensor, par * CH * REL_N + CH - 1,
                              [[REL_N - 1, CH], [2 * CH * REL_N, A_PAIRS], [1, NK_S]])
                po.dma_start(biasT[par * CH:(par + 1) * CH, :, :], src).then_inc(s["bias_in"], 16)

            def squares_of(r, x_base):
                for k in range(KT):
                    po.wait_ge(x_upd, x_base - KT + k + 3)
                    if k:
                        link(po.tensor_tensor(square, xT[:, k, :], xT[:, k, :], ALU.mult))
                        ins = po.tensor_tensor(total, total, square, ALU.add)
                    else:
                        ins = po.tensor_tensor(total, xT[:, k, :], xT[:, k, :], ALU.mult)
                    if k < KT - 1:
                        link(ins)
                ins.then_inc(total_ready, 1)

            def split_mix(n, t):
                j = t % 2
                raw = gu[:, n % 2, :].rearrange("p (k c) -> p k c", k=KT)[:, :, j * P:(j + 1) * P]
                for half in range(2):
                    w = slice(half * 512, (half + 1) * 512)
                    po.wait_ge(mix_hi, mix_halves(n) + 2 * j + half + 1)
                    po.tensor_tensor(w_mix[:, j, 1, w].rearrange("p (k c) -> p k c", k=4),
                                     raw[:, 4 * half:4 * half + 4, :],
                                     w_mix[:, j, 0, w].bitcast(F32).rearrange("p (k c) -> p k c", k=4),
                                     ALU.subtract).then_inc(mix_lo, 1)

            squares_of(NORM_EV, X_EV)
            for t in range(N_EV):
                split_mix(GU_EV + t // 2, t)
                if t == 1:
                    po.memset(view(RA, 2560, 1280), 0.0).then_inc(s["zero"], 1)
                    po.memset(view(RA, 0, 2560), 0.0).then_inc(s["zero"], 1)
                if t == 12:
                    po.wait_ge(s["kw_evac"], 1)
                    store(O["p_idx_k"][0, 0].rearrange("(i p) d -> p i d", p=P), kwtok[:, 0:2, 0:IDX_D])
                    store(O["s_idx_k"][0, 0], kwtok[0:TS, 2, 0:IDX_D])
            po.wait_ge(gu_done, GU_EV + len(EV_LOADS))
            po.memset(view(RB, bd_at, 3840), 0.0).then_inc(s["zero"], 1)
            for name, tok in (("v", vtok), ("k", ktok)):
                po.wait_ge(s[name + "tok_evac"], 3)
                store(O[f"p_attn_{name}"][0, 0].rearrange("(i p) h d -> p i (h d)", p=P), tok[:, 0:2, :])
                store(O[f"s_attn_{name}"][0, 0].rearrange("p h d -> p (h d)"), tok[0:TS, 2, :])
            po.wait_ge(s["sg_ready"], 1)
            for name, i in (("p_gla", 4), ("s_gla", 6)):
                store(O[name][0, 0].rearrange("(a b) d e -> a (b d) e", b=2).rearrange("a q e -> q a e"), Sg(i))
            squares_of(NORM_FFN[1], X_FFN[1])
            po.wait_ge(x_upd, X_FFN[1] + 2)
            po.wait_ge(out_sem, 16 * 8)
            po.memset(lev, 0.0)
            po.memset(maskI, -BIG)
            po.memset(maskS, BIG)
            po.memset(Sd[:, 0, :, :], 0.0)
            link(po.memset(klc, 0.0))
            for par in range(2):
                h = slice(par * CH, (par + 1) * CH)
                po.memset(maskI[h, par * CH:(par + 1) * CH], 0.0)
                link(po.memset(maskS[h, par * CH:(par + 1) * CH], 0.0))
                link(sel(out=maskI[h, par * CH:(par + 1) * CH], in_=maskI[h, par * CH:(par + 1) * CH], compare_op=ALU.is_ge,
                    fill=-BIG, base=0, pattern=[[1, CH]], channel_multiplier=-1))
                link(sel(out=maskS[h, par * CH:(par + 1) * CH], in_=maskS[h, par * CH:(par + 1) * CH], compare_op=ALU.is_gt,
                    fill=BIG, base=0, pattern=[[-1, CH]], channel_multiplier=1))
            for i in range(6):
                m = 1 << i
                part = lev[:, i, :].rearrange("p (n r) -> p n r", r=2 * m)[:, :, 0:m]
                link(po.memset(part, 1.0))
                link(sel(out=part, in_=part, compare_op=ALU.is_ge, fill=0.0, base=-m, pattern=[[-2 * m, P // (2 * m)], [0, m]],
                         channel_multiplier=1))
                ins = sel(out=part, in_=part, compare_op=ALU.is_ge, fill=0.0, base=2 * m - 1,
                          pattern=[[2 * m, P // (2 * m)], [0, m]], channel_multiplier=-1)
                if i < 5:
                    link(ins)
            ins.then_inc(o["masks"], 1)
            squares_of(NORM_FFN[2], X_FFN[2])
            squares_of(NORM_OD, X_OD)
            for t in range(N_OD):
                split_mix(GU_OD + t // 2, t)
            po.wait_ge(gu_done, GU_OD + 16)
            po.memset(vnew.rearrange("p a b e -> p (a b e)"), 0.0).then_inc(o["zero_v"], 1)
            po.sem_inc(o["states"], 1)
            for level in range(5):
                for c in range(NCH):
                    m = level * NCH + c
                    if level == 0:
                        po.wait_ge(o["kk_used"], 2 * NCH)
                    else:
                        po.wait_ge(o["y_pe"], m - NCH + 1)
                    po.tensor_tensor(Dm[:, c, :, :], Lm[:, c, :, :],
                                     lev[:, level + 1:level + 2, :].to_broadcast([P, C_PAIRS, P]), ALU.mult)\
                        .then_inc(o["bm"], 1)
            po.wait_ge(o["s_upd"], NCH)
            store(O["p_delta"][0, 0].rearrange("h d e -> d h e"), Sd[:, 0, :, :])
            store(O["s_delta"][0, 0].rearrange("h d e -> d h e"), S_sample)
            po.wait_ge(o["cs_evac"], 1)
            store(O["p_conv"][0, 0], csr[0:3, :])
            store(O["s_conv"][0, 0], csr[3:6, :])
            squares_of(NORM_FFN[3], X_FFN[3])
            po.wait_ge(pro_evac, 13)
            store(O["y_prompt"][0].rearrange("(i p) d -> p i d", p=P), ytok[:, 0:2, :])
            store(O["y_sample"][0], ytok[0:TS, 2, :])
            po.wait_ge(out_sem, 16 * 14)


INPUTS = ["x_prompt", "x_sample", "cache_attn_k", "cache_attn_v", "cache_idx_k", "state_gla", "state_delta",
          "state_conv", "ffn_norm", "ffn_w_gate", "ffn_w_up", "ffn_w_down", "mix_norm", "ev_w_in", "ev_q_norm",
          "ev_k_norm", "rel_bias", "ev_gate_w2", "ev_gate_b2", "ev_gla_norm", "ev_w_out", "od_w_in", "od_conv_w",
          "od_a_log", "od_dt_bias", "od_norm", "od_w_out"]
OUTPUTS = [("y_prompt", (1, TP, D)), ("y_sample", (1, TS, D)),
           ("p_attn_k", (1, 1, TP, 8, 64)), ("p_attn_v", (1, 1, TP, 8, 64)), ("p_idx_k", (1, 1, TP, 64)),
           ("p_gla", (1, 1, 4, 64, 128)), ("p_delta", (1, 1, 8, 128, 128)), ("p_conv", (1, 1, 3, 3072)),
           ("s_attn_k", (1, 1, TS, 8, 64)), ("s_attn_v", (1, 1, TS, 8, 64)), ("s_idx_k", (1, 1, TS, 64)),
           ("s_gla", (1, 1, 4, 64, 128)), ("s_delta", (1, 1, 8, 128, 128)), ("s_conv", (1, 1, 3, 3072))]


def kernel(**inputs):
    import numpy as np
    import concourse.bacc as bacc
    from concourse.bass_utils import run_bass_kernel_spmd

    nc = bacc.Bacc("TRN2", target_bir_lowering=False, num_devices=1)
    arrays = {f"in_{name}": np.ascontiguousarray(inputs[name]) for name in INPUTS}
    ins = {name: nc.dram_tensor(f"in_{name}", arrays[f"in_{name}"].shape, F32, kind="ExternalInput").ap()
           for name in INPUTS}
    outs = {name: nc.dram_tensor(f"out_{name}", shape, F32, kind="ExternalOutput").ap() for name, shape in OUTPUTS}
    build(nc, ins, outs)
    r = run_bass_kernel_spmd(nc, [arrays], core_ids=[0])
    return tuple(r.results[0][f"out_{name}"] for name, _ in OUTPUTS)
```
